# Optimizing a Trainium2 kernel written in Bass

```python
import jax
import jax.numpy as jnp
from jax import lax
import numpy as np
import math
import jax, jax.numpy as jnp

D_MODEL = 1024
BATCH = 1
SEQ = 512
DEPTH = 1

HEAD_DIM = 64
NA_HEADS = 8
NA_WIDTH = NA_HEADS * HEAD_DIM
NA_ROWS = 8
NA_COLS = 16
GRID_W = 64
DIL_PAIRS = ((128, 1), (512, 4), (2048, 16))
NB_GROUPS = len(DIL_PAIRS)
NB_HEADS_PER_GROUP = 4
NB_HEADS = NB_GROUPS * NB_HEADS_PER_GROUP
NB_WIDTH = NB_HEADS * HEAD_DIM
ALIBI_MAX_EXP = 8.0
LOCAL_QBLOCK = 64
D_FF = 2816
N_IN = 3 * NA_WIDTH + 3 * NB_WIDTH + 2 * D_MODEL
NORM_EPS = 1e-6
ATTN_SCALE = HEAD_DIM ** -0.5


def _rmsnorm(x, g):
    xf = x.astype(jnp.float32)
    y = xf * lax.rsqrt(jnp.mean(xf * xf, axis=-1, keepdims=True) + NORM_EPS)
    return (y * g.astype(jnp.float32)).astype(x.dtype)

def _swiglu(x, w_gate, w_up, w_down):
    return (jax.nn.silu(x @ w_gate) * (x @ w_up)) @ w_down

def _neighbourhood_attention(q, k, v, rpb):
    B, T, H, Dh = q.shape
    rows = T // GRID_W
    kh = min(NA_ROWS, rows)
    r = jnp.arange(rows)
    row0 = jnp.clip(r - kh // 2, 0, rows - kh)
    key_rows = row0[:, None] + jnp.arange(kh)[None, :]
    c = jnp.arange(GRID_W)
    col0 = jnp.clip(c - NA_COLS // 2, 0, GRID_W - NA_COLS)
    col_ok = (c[None, :] >= col0[:, None]) & (c[None, :] < col0[:, None] + NA_COLS)
    col_rel = jnp.clip(c[None, :] - c[:, None], -(NA_COLS - 1), NA_COLS - 1)
    row_rel = key_rows - r[:, None]
    bias = rpb[:, (row_rel + NA_ROWS - 1)[:, None, :, None],
               (col_rel + NA_COLS - 1)[None, :, None, :]]
    qg = q.reshape(B, rows, GRID_W, H, Dh)
    kg = k.reshape(B, rows, GRID_W, H, Dh)[:, key_rows]
    vg = v.reshape(B, rows, GRID_W, H, Dh)[:, key_rows]
    s = jnp.einsum('brqhd,brkwhd->bhrqkw', qg, kg).astype(jnp.float32) * ATTN_SCALE
    s = s + bias[None].astype(jnp.float32)
    s = jnp.where(col_ok[:, None, :], s, -jnp.inf)
    p = jax.nn.softmax(s.reshape(B, H, rows, GRID_W, kh * GRID_W), axis=-1)
    p = p.reshape(s.shape).astype(v.dtype)
    o = jnp.einsum('bhrqkw,brkwhd->brqhd', p, vg)
    return o.reshape(B, T, H * Dh)

def _banded_attention(q, k, v, half, dilation, slopes):
    N, H, L, Dh = q.shape
    nb = -(-L // LOCAL_QBLOCK)
    lp = nb * LOCAL_QBLOCK
    pad = lp - L
    qp = jnp.pad(q, ((0, 0), (0, 0), (0, pad), (0, 0))).reshape(N, H, nb, LOCAL_QBLOCK, Dh)
    kp = jnp.pad(k, ((0, 0), (0, 0), (half, half + pad), (0, 0)))
    vp = jnp.pad(v, ((0, 0), (0, 0), (half, half + pad), (0, 0)))
    kspan = LOCAL_QBLOCK + 2 * half
    kidx = jnp.arange(nb)[:, None] * LOCAL_QBLOCK + jnp.arange(kspan)[None, :]
    kblk = kp[:, :, kidx]
    vblk = vp[:, :, kidx]
    s = jnp.einsum('nhbqd,nhbkd->nhbqk', qp, kblk).astype(jnp.float32) * ATTN_SCALE
    qpos = jnp.arange(nb)[:, None] * LOCAL_QBLOCK + jnp.arange(LOCAL_QBLOCK)[None, :]
    kpos = kidx - half
    rel = kpos[:, None, :] - qpos[:, :, None]
    valid = ((jnp.abs(rel) <= half) & (kpos[:, None, :] >= 0) & (kpos[:, None, :] < L)) | (qpos[:, :, None] >= L)
    dist = (dilation * jnp.abs(rel)).astype(jnp.float32)
    s = s - slopes[:, None, None, None] * dist[None]
    s = jnp.where(valid, s, -jnp.inf)
    lse = jax.nn.logsumexp(s, axis=-1)
    p = jnp.exp(s - lse[..., None]).astype(v.dtype)
    o = jnp.einsum('nhbqk,nhbkd->nhbqd', p, vblk).reshape(N, H, lp, Dh)[:, :, :L]
    return o, lse.reshape(N, H, lp)[:, :, :L]

def _dilated_attention(q, k, v, dilation, half, slopes):
    B, T, H, Dh = q.shape
    L = T // dilation

    def to_res(a):
        return a.reshape(B, L, dilation, H, Dh).transpose(0, 2, 3, 1, 4).reshape(B * dilation, H, L, Dh)

    o, lse = _banded_attention(to_res(q), to_res(k), to_res(v), half, dilation, slopes)
    o = o.reshape(B, dilation, H, L, Dh).transpose(0, 3, 1, 2, 4).reshape(B, T, H, Dh)
    lse = lse.reshape(B, dilation, H, L).transpose(0, 3, 1, 2).reshape(B, T, H)
    return o, lse

def _dilated_mixture(q, k, v, slopes):
    B, T, _ = q.shape
    shp = (B, T, NB_GROUPS, NB_HEADS_PER_GROUP, HEAD_DIM)
    q, k, v = q.reshape(shp), k.reshape(shp), v.reshape(shp)
    outs, lses = [], []
    for g, (window, dilation) in enumerate(DIL_PAIRS):
        half = window // (2 * dilation)
        sl = slopes[g * NB_HEADS_PER_GROUP:(g + 1) * NB_HEADS_PER_GROUP]
        o, lse = _dilated_attention(q[:, :, g], k[:, :, g], v[:, :, g], dilation, half, sl)
        outs.append(o)
        lses.append(lse)
    alpha = jax.nn.softmax(jnp.stack(lses, axis=0), axis=0)
    o = jnp.stack(outs, axis=0) * alpha[..., None].astype(outs[0].dtype)
    return o.transpose(1, 2, 0, 3, 4).reshape(B, T, NB_WIDTH)

def first_inputs(seed: int = 0) -> dict:
    key = jax.random.key(seed)
    ks = jax.random.split(key, 20)

    def nrm(k, shape, scale):
        return jax.random.normal(k, shape, jnp.float32) * scale

    def gain(k):
        return 1.0 + 0.05 * jax.random.normal(k, (DEPTH, D_MODEL), jnp.float32)

    return {
        'x': nrm(ks[0], (BATCH, SEQ, D_MODEL), 1.0),
        'ffn1_pre_g': gain(ks[1]),
        'ffn1_w_gate': nrm(ks[2], (DEPTH, D_MODEL, D_FF), D_MODEL ** -0.5),
        'ffn1_w_up': nrm(ks[3], (DEPTH, D_MODEL, D_FF), D_MODEL ** -0.5),
        'ffn1_w_down': nrm(ks[4], (DEPTH, D_FF, D_MODEL), D_FF ** -0.5),
        'ffn1_post_g': gain(ks[5]),
        'mix_pre_g': gain(ks[6]),
        'w_in': nrm(ks[7], (DEPTH, D_MODEL, N_IN), D_MODEL ** -0.5),
        'na_rpb': nrm(ks[8], (DEPTH, NA_HEADS, 2 * NA_ROWS - 1, 2 * NA_COLS - 1), 0.1),
        'w_branch_a': nrm(ks[9], (DEPTH, NA_WIDTH, D_MODEL), NA_WIDTH ** -0.5),
        'w_branch_b': nrm(ks[10], (DEPTH, NB_WIDTH, D_MODEL), NB_WIDTH ** -0.5),
        'w_out': nrm(ks[11], (DEPTH, D_MODEL, D_MODEL), D_MODEL ** -0.5),
        'mix_post_g': gain(ks[12]),
        'ffn2_pre_g': gain(ks[13]),
        'ffn2_w_gate': nrm(ks[14], (DEPTH, D_MODEL, D_FF), D_MODEL ** -0.5),
        'ffn2_w_up': nrm(ks[15], (DEPTH, D_MODEL, D_FF), D_MODEL ** -0.5),
        'ffn2_w_down': nrm(ks[16], (DEPTH, D_FF, D_MODEL), D_FF ** -0.5),
        'ffn2_post_g': gain(ks[17]),
    }

def first_block(x, ffn1_pre_g, ffn1_w_gate, ffn1_w_up, ffn1_w_down, ffn1_post_g,
              mix_pre_g, w_in, na_rpb, w_branch_a, w_branch_b, w_out, mix_post_g,
              ffn2_pre_g, ffn2_w_gate, ffn2_w_up, ffn2_w_down, ffn2_post_g):
    B, T, _ = x.shape
    slopes = jnp.exp2(-ALIBI_MAX_EXP * (jnp.arange(NB_HEADS, dtype=jnp.float32) + 1.0) / NB_HEADS)
    widths = [NA_WIDTH] * 3 + [NB_WIDTH] * 3 + [D_MODEL]
    splits = [int(s) for s in np.cumsum(widths)]
    for l in range(DEPTH):
        f = _swiglu(_rmsnorm(x, ffn1_pre_g[l]), ffn1_w_gate[l], ffn1_w_up[l], ffn1_w_down[l])
        x = x + 0.5 * _rmsnorm(f, ffn1_post_g[l])
        h = _rmsnorm(x, mix_pre_g[l])
        proj = h @ w_in[l]
        qa, ka, va, qb, kb, vb, gate_a, gate_b = jnp.split(proj, splits, axis=-1)
        ha = (B, T, NA_HEADS, HEAD_DIM)
        ya = _neighbourhood_attention(qa.reshape(ha), ka.reshape(ha), va.reshape(ha), na_rpb[l]) @ w_branch_a[l]
        yb = _dilated_mixture(qb, kb, vb, slopes) @ w_branch_b[l]
        merged = jax.nn.sigmoid(gate_a) * ya + jax.nn.sigmoid(gate_b) * yb
        x = x + _rmsnorm(merged @ w_out[l], mix_post_g[l])
        f = _swiglu(_rmsnorm(x, ffn2_pre_g[l]), ffn2_w_gate[l], ffn2_w_up[l], ffn2_w_down[l])
        x = x + 0.5 * _rmsnorm(f, ffn2_post_g[l])
    return x


DEPTH_2 = 2

PLE_DIM = 256
ROPE_THETA = 10000.0
EPS = 1e-6
NEG_INF = -1e30

A_HEADS = 8
A_KV_GROUPS = 2
A_CMP_LEN = 32
A_CMP_STRIDE = 16
A_CMP_HIDDEN = 256
A_SEL_LEN = 64
A_TOPK = 16
A_WINDOW = 512
A_Q_CHUNK = 128
A_FORCE_BONUS = 1e4

B_HEADS = 8
B_KV_HEADS = 2
B_WINDOW = 128
B_BLOCK = 128

C_HEADS = 8
C_Q_RANK = 256
C_KV_RANK = 256
C_NOPE = 64
C_ROPE = 32
C_V = 64
C_Q_BLOCK = 128

D_FF_2 = int(math.ceil(8 * D_MODEL / 3 / 256)) * 256

A_Q = A_HEADS * HEAD_DIM
A_KV = A_KV_GROUPS * HEAD_DIM
A_GATES = A_HEADS * 3
B_Q = B_HEADS * HEAD_DIM
B_KV = B_KV_HEADS * HEAD_DIM
IN_SIZES = (A_Q, A_KV, A_KV, A_KV, A_KV, A_KV, A_KV, A_GATES, B_Q, B_KV, B_KV, C_Q_RANK, C_KV_RANK, C_ROPE)
IN_COLS = sum(IN_SIZES)
A_OUT = A_HEADS * HEAD_DIM
B_OUT = B_HEADS * HEAD_DIM
C_OUT = C_HEADS * C_V


def rmsnorm(x, g):
    xf = x.astype(jnp.float32)
    y = xf * lax.rsqrt(jnp.mean(xf * xf, axis=-1, keepdims=True) + EPS)
    return (y * g.astype(jnp.float32)).astype(x.dtype)

def rope_tables(positions, dim):
    inv_freq = jnp.power(jnp.float32(ROPE_THETA), -jnp.arange(0, dim, 2, dtype=jnp.float32) / dim)
    ang = positions.astype(jnp.float32)[..., None] * inv_freq
    return jnp.cos(ang), jnp.sin(ang)

def apply_rope(x, cos, sin):
    half = x.shape[-1] // 2
    xf = x.astype(jnp.float32)
    x1, x2 = xf[..., :half], xf[..., half:]
    c, s = cos[:, :, None, :], sin[:, :, None, :]
    return jnp.concatenate([x1 * c - x2 * s, x2 * c + x1 * s], axis=-1).astype(x.dtype)

def masked_softmax(scores, mask):
    p = jax.nn.softmax(jnp.where(mask, scores, NEG_INF), axis=-1)
    return jnp.where(mask, p, 0.0)

def compress_blocks(t, tok, pos, w1, w2):
    B, _, G, dh = t.shape
    n_cmp, L = tok.shape
    blocks = t[:, tok] + pos[:, None, :].astype(t.dtype)
    flat = blocks.transpose(0, 1, 3, 2, 4).reshape(B, n_cmp, G, L * dh)
    return jax.nn.gelu(flat @ w1) @ w2

def nsa_attention(q, kc, vc, ks, vs, kw, vw, gate_logits, pos_k, w1_k, w2_k, pos_v, w1_v, w2_v):
    B, S = q.shape[0], q.shape[1]
    G, R, dh = A_KV_GROUPS, A_HEADS // A_KV_GROUPS, HEAD_DIM
    QC = A_Q_CHUNK
    scale = dh ** -0.5
    dt = q.dtype
    qg = q.reshape(B, S, G, R, dh)
    gates = jax.nn.sigmoid(gate_logits.astype(jnp.float32)).reshape(B, S, G, R, 3).astype(dt)
    n_cmp = (S - A_CMP_LEN) // A_CMP_STRIDE + 1
    tok = np.arange(n_cmp)[:, None] * A_CMP_STRIDE + np.arange(A_CMP_LEN)[None, :]
    k_cmp = compress_blocks(kc, tok, pos_k, w1_k, w2_k)
    v_cmp = compress_blocks(vc, tok, pos_v, w1_v, w2_v)
    cmp_end = jnp.asarray(tok[:, -1], jnp.int32)
    n_sel = S // A_SEL_LEN
    sel_map = np.zeros((n_cmp, n_sel), np.float32)
    np.add.at(sel_map, (np.repeat(np.arange(n_cmp), A_CMP_LEN), (tok // A_SEL_LEN).reshape(-1)), 1.0 / A_CMP_LEN)
    sel_map = jnp.asarray(sel_map)
    top_k = min(A_TOPK, n_sel)
    ks_blk = ks.transpose(0, 2, 1, 3).reshape(B, G, n_sel, A_SEL_LEN * dh)
    vs_blk = vs.transpose(0, 2, 1, 3).reshape(B, G, n_sel, A_SEL_LEN * dh)
    gather_blocks = jax.vmap(jax.vmap(lambda t, i: t[i]))
    kw_pad = jnp.pad(kw, ((0, 0), (A_WINDOW, 0), (0, 0), (0, 0)))
    vw_pad = jnp.pad(vw, ((0, 0), (A_WINDOW, 0), (0, 0), (0, 0)))
    blk_ids = jnp.arange(n_sel)

    def chunk(c):
        t0 = c * QC
        tq = t0 + jnp.arange(QC)
        qc = lax.dynamic_slice_in_dim(qg, t0, QC, axis=1)
        gc = lax.dynamic_slice_in_dim(gates, t0, QC, axis=1)
        s = jnp.einsum('bqgrd,bngd->bgrqn', qc, k_cmp).astype(jnp.float32) * scale
        p_cmp = masked_softmax(s, cmp_end[None, :] <= tq[:, None])
        o_cmp = jnp.einsum('bgrqn,bngd->bqgrd', p_cmp.astype(dt), v_cmp)
        imp = jnp.einsum('bgrqn,nj->bgqj', p_cmp, sel_map)
        cur = tq // A_SEL_LEN
        valid = blk_ids[None, :] <= cur[:, None]
        forced = (blk_ids[None, :] == 0) | (blk_ids[None, :] == cur[:, None]) | (blk_ids[None, :] == cur[:, None] - 1)
        imp = jnp.where(valid, imp + jnp.where(forced, A_FORCE_BONUS, 0.0), NEG_INF)
        _, top_idx = lax.top_k(imp, top_k)
        idx_flat = top_idx.reshape(B, G, QC * top_k)
        kb = gather_blocks(ks_blk, idx_flat).reshape(B, G, QC, top_k * A_SEL_LEN, dh)
        vb = gather_blocks(vs_blk, idx_flat).reshape(B, G, QC, top_k * A_SEL_LEN, dh)
        key_pos = (top_idx[..., None] * A_SEL_LEN + jnp.arange(A_SEL_LEN)).reshape(B, G, QC, top_k * A_SEL_LEN)
        m_sel = key_pos <= tq[None, None, :, None]
        s = jnp.einsum('bqgrd,bgqkd->bgrqk', qc, kb).astype(jnp.float32) * scale
        p_sel = masked_softmax(s, m_sel[:, :, None])
        o_sel = jnp.einsum('bgrqk,bgqkd->bqgrd', p_sel.astype(dt), vb)
        kwc = lax.dynamic_slice_in_dim(kw_pad, t0, QC + A_WINDOW, axis=1)
        vwc = lax.dynamic_slice_in_dim(vw_pad, t0, QC + A_WINDOW, axis=1)
        kp = t0 - A_WINDOW + jnp.arange(QC + A_WINDOW)
        m_win = (kp[None, :] <= tq[:, None]) & (kp[None, :] > tq[:, None] - A_WINDOW) & (kp[None, :] >= 0)
        s = jnp.einsum('bqgrd,bkgd->bgrqk', qc, kwc).astype(jnp.float32) * scale
        p_win = masked_softmax(s, m_win)
        o_win = jnp.einsum('bgrqk,bkgd->bqgrd', p_win.astype(dt), vwc)
        return gc[..., 0:1] * o_cmp + gc[..., 1:2] * o_sel + gc[..., 2:3] * o_win

    out = lax.map(chunk, jnp.arange(S // QC))
    return out.transpose(1, 0, 2, 3, 4, 5).reshape(B, S, A_HEADS * dh)

def swa_sink_attention(q, k, v, sinks):
    B, S = q.shape[0], q.shape[1]
    G, R, dh, BLK = B_KV_HEADS, B_HEADS // B_KV_HEADS, HEAD_DIM, B_BLOCK
    nb = S // BLK
    qb = q.reshape(B, nb, BLK, G, R, dh)

    def band(t):
        tb = t.reshape(B, nb, BLK, G, dh)
        prev = jnp.pad(tb, ((0, 0), (1, 0), (0, 0), (0, 0), (0, 0)))[:, :-1]
        return jnp.concatenate([prev, tb], axis=2)

    kb, vb = band(k), band(v)
    s = jnp.einsum('bnqgrd,bnkgd->bngrqk', qb, kb).astype(jnp.float32) * (dh ** -0.5)
    qi = jnp.arange(BLK)[:, None]
    kj = jnp.arange(2 * BLK)[None, :] - BLK
    rel = (kj <= qi) & (kj > qi - B_WINDOW)
    mask = rel[None] & ((jnp.arange(nb)[:, None, None] > 0) | (kj[None] >= 0))
    s = jnp.where(mask[None, :, None, None], s, NEG_INF)
    sink = jnp.broadcast_to(sinks.astype(jnp.float32).reshape(G, R)[None, None, :, :, None, None], s.shape[:-1] + (1,))
    p = jax.nn.softmax(jnp.concatenate([s, sink], axis=-1), axis=-1)[..., :-1]
    o = jnp.einsum('bngrqk,bnkgd->bnqgrd', p.astype(v.dtype), vb)
    return o.reshape(B, S, B_HEADS * dh)

def causal_block_attention(q, k, v, scale):
    B, S, H, _ = q.shape
    dv = v.shape[-1]
    key_pos = jnp.arange(S)

    def body(c):
        t0 = c * C_Q_BLOCK
        qb = lax.dynamic_slice_in_dim(q, t0, C_Q_BLOCK, axis=1)
        s = jnp.einsum('bqhd,bkhd->bhqk', qb, k).astype(jnp.float32) * scale
        mask = key_pos[None, :] <= (t0 + jnp.arange(C_Q_BLOCK))[:, None]
        p = jax.nn.softmax(jnp.where(mask, s, NEG_INF), axis=-1)
        return jnp.einsum('bhqk,bkhd->bqhd', p.astype(v.dtype), v)

    out = lax.map(body, jnp.arange(S // C_Q_BLOCK))
    return out.transpose(1, 0, 2, 3, 4).reshape(B, S, H * dv)

def mla_attention(cq, ckv, k_pe_raw, q_norm, w_q_up, kv_norm, w_kv_up, cos32, sin32):
    B, S = cq.shape[0], cq.shape[1]
    q = (rmsnorm(cq, q_norm) @ w_q_up).reshape(B, S, C_HEADS, C_NOPE + C_ROPE)
    q_nope, q_pe = q[..., :C_NOPE], apply_rope(q[..., C_NOPE:], cos32, sin32)
    kv = (rmsnorm(ckv, kv_norm) @ w_kv_up).reshape(B, S, C_HEADS, C_NOPE + C_V)
    k_nope, v = kv[..., :C_NOPE], kv[..., C_NOPE:]
    k_pe = apply_rope(k_pe_raw[:, :, None, :], cos32, sin32)
    qf = jnp.concatenate([q_nope, q_pe], axis=-1)
    kf = jnp.concatenate([k_nope, jnp.broadcast_to(k_pe, (B, S, C_HEADS, C_ROPE))], axis=-1)
    return causal_block_attention(qf, kf, v, (C_NOPE + C_ROPE) ** -0.5)

def hybrid_layer(x, p_i, rope64, rope32, mix_norm, w_in, a_cmp_pos_k, a_cmp_w1_k, a_cmp_w2_k,
                 a_cmp_pos_v, a_cmp_w1_v, a_cmp_w2_v, b_sinks, c_q_norm, c_w_q_up, c_kv_norm, c_w_kv_up,
                 w_branch_gate, w_branch_a, w_branch_b, w_branch_c, w_out, ffn_norm, w_ffn_gate, w_ffn_up,
                 w_ffn_down, ple_norm, w_ple_proj, w_ple_gate):
    B, S, _ = x.shape
    cos64, sin64 = rope64
    cos32, sin32 = rope32
    h = rmsnorm(x, mix_norm)
    z = h @ w_in
    split_points = [int(v) for v in np.cumsum(IN_SIZES)[:-1]]
    (a_q, a_kc, a_vc, a_ks, a_vs, a_kw, a_vw, a_g, b_q, b_k, b_v, c_cq, c_ckv, c_kpe) = jnp.split(z, split_points, axis=-1)

    def heads(t, n):
        return t.reshape(B, S, n, -1)

    def rot(t, n):
        return apply_rope(heads(t, n), cos64, sin64)

    G = A_KV_GROUPS
    o_a = nsa_attention(rot(a_q, A_HEADS), rot(a_kc, G), heads(a_vc, G), rot(a_ks, G), heads(a_vs, G),
                        rot(a_kw, G), heads(a_vw, G), a_g, a_cmp_pos_k, a_cmp_w1_k, a_cmp_w2_k,
                        a_cmp_pos_v, a_cmp_w1_v, a_cmp_w2_v)
    o_b = swa_sink_attention(rot(b_q, B_HEADS), rot(b_k, B_KV_HEADS), heads(b_v, B_KV_HEADS), b_sinks)
    o_c = mla_attention(c_cq, c_ckv, c_kpe, c_q_norm, c_w_q_up, c_kv_norm, c_w_kv_up, cos32, sin32)

    g = jax.nn.sigmoid((h @ w_branch_gate).astype(jnp.float32)).astype(x.dtype)
    g_a, g_b, g_c = jnp.split(g, 3, axis=-1)
    merged = g_a * (o_a @ w_branch_a) + g_b * (o_b @ w_branch_b) + g_c * (o_c @ w_branch_c)
    x = x + merged @ w_out

    h2 = rmsnorm(x, ffn_norm)
    x = x + (jax.nn.silu(h2 @ w_ffn_gate) * (h2 @ w_ffn_up)) @ w_ffn_down

    gate = jax.nn.sigmoid((rmsnorm(x, ple_norm) @ w_ple_gate).astype(jnp.float32)).astype(x.dtype)
    return x + gate * (p_i.astype(x.dtype) @ w_ple_proj)

def second_inputs(seed: int = 0) -> dict:
    key = jax.random.key(seed)
    ks = jax.random.split(key, 32)

    def dense(k, shape, fan_in):
        return jax.random.normal(k, shape, jnp.float32) * (fan_in ** -0.5)

    def gain(k, shape):
        return 1.0 + 0.05 * jax.random.normal(k, shape, jnp.float32)

    L, dh = A_CMP_LEN, HEAD_DIM
    return {
        "x": jax.random.normal(ks[0], (BATCH, SEQ, D_MODEL), jnp.float32),
        "p": jax.random.normal(ks[1], (DEPTH_2, BATCH, SEQ, PLE_DIM), jnp.float32),
        "positions": jnp.broadcast_to(jnp.arange(SEQ, dtype=jnp.int32)[None, :], (BATCH, SEQ)),
        "mix_norm": gain(ks[2], (DEPTH_2, D_MODEL)),
        "w_in": dense(ks[3], (DEPTH_2, D_MODEL, IN_COLS), D_MODEL),
        "a_cmp_pos_k": 0.2 * jax.random.normal(ks[4], (DEPTH_2, L, dh), jnp.float32),
        "a_cmp_w1_k": dense(ks[5], (DEPTH_2, L * dh, A_CMP_HIDDEN), L * dh),
        "a_cmp_w2_k": dense(ks[6], (DEPTH_2, A_CMP_HIDDEN, dh), A_CMP_HIDDEN),
        "a_cmp_pos_v": 0.2 * jax.random.normal(ks[7], (DEPTH_2, L, dh), jnp.float32),
        "a_cmp_w1_v": dense(ks[8], (DEPTH_2, L * dh, A_CMP_HIDDEN), L * dh),
        "a_cmp_w2_v": dense(ks[9], (DEPTH_2, A_CMP_HIDDEN, dh), A_CMP_HIDDEN),
        "b_sinks": 0.5 * jax.random.normal(ks[10], (DEPTH_2, B_HEADS), jnp.float32),
        "c_q_norm": gain(ks[11], (DEPTH_2, C_Q_RANK)),
        "c_w_q_up": dense(ks[12], (DEPTH_2, C_Q_RANK, C_HEADS * (C_NOPE + C_ROPE)), C_Q_RANK),
        "c_kv_norm": gain(ks[13], (DEPTH_2, C_KV_RANK)),
        "c_w_kv_up": dense(ks[14], (DEPTH_2, C_KV_RANK, C_HEADS * (C_NOPE + C_V)), C_KV_RANK),
        "w_branch_gate": dense(ks[15], (DEPTH_2, D_MODEL, 3 * D_MODEL), D_MODEL),
        "w_branch_a": dense(ks[16], (DEPTH_2, A_OUT, D_MODEL), A_OUT),
        "w_branch_b": dense(ks[17], (DEPTH_2, B_OUT, D_MODEL), B_OUT),
        "w_branch_c": dense(ks[18], (DEPTH_2, C_OUT, D_MODEL), C_OUT),
        "w_out": dense(ks[19], (DEPTH_2, D_MODEL, D_MODEL), D_MODEL),
        "ffn_norm": gain(ks[20], (DEPTH_2, D_MODEL)),
        "w_ffn_gate": dense(ks[21], (DEPTH_2, D_MODEL, D_FF_2), D_MODEL),
        "w_ffn_up": dense(ks[22], (DEPTH_2, D_MODEL, D_FF_2), D_MODEL),
        "w_ffn_down": dense(ks[23], (DEPTH_2, D_FF_2, D_MODEL), D_FF_2),
        "ple_norm": gain(ks[24], (DEPTH_2, D_MODEL)),
        "w_ple_proj": dense(ks[25], (DEPTH_2, PLE_DIM, D_MODEL), PLE_DIM),
        "w_ple_gate": dense(ks[26], (DEPTH_2, D_MODEL, D_MODEL), D_MODEL),
        "final_norm": gain(ks[27], (D_MODEL,)),
    }

def second_block(x, p, positions, mix_norm, w_in, a_cmp_pos_k, a_cmp_w1_k, a_cmp_w2_k, a_cmp_pos_v,
              a_cmp_w1_v, a_cmp_w2_v, b_sinks, c_q_norm, c_w_q_up, c_kv_norm, c_w_kv_up, w_branch_gate,
              w_branch_a, w_branch_b, w_branch_c, w_out, ffn_norm, w_ffn_gate, w_ffn_up, w_ffn_down,
              ple_norm, w_ple_proj, w_ple_gate, final_norm):
    rope64 = rope_tables(positions, HEAD_DIM)
    rope32 = rope_tables(positions, C_ROPE)
    for i in range(DEPTH_2):
        x = hybrid_layer(x, p[i], rope64, rope32, mix_norm[i], w_in[i], a_cmp_pos_k[i], a_cmp_w1_k[i],
                         a_cmp_w2_k[i], a_cmp_pos_v[i], a_cmp_w1_v[i], a_cmp_w2_v[i], b_sinks[i],
                         c_q_norm[i], c_w_q_up[i], c_kv_norm[i], c_w_kv_up[i], w_branch_gate[i],
                         w_branch_a[i], w_branch_b[i], w_branch_c[i], w_out[i], ffn_norm[i],
                         w_ffn_gate[i], w_ffn_up[i], w_ffn_down[i], ple_norm[i], w_ple_proj[i],
                         w_ple_gate[i])
    return rmsnorm(x, final_norm)


def setup_inputs(seed=0):
    out = dict(first_inputs(seed))
    for name, value in second_inputs(seed + 1).items():
        if name != "x":
            out[name + "_2"] = value
    return out


def reference(
    x, ffn1_pre_g, ffn1_w_gate, ffn1_w_up, ffn1_w_down, ffn1_post_g, mix_pre_g, w_in, na_rpb,
    w_branch_a, w_branch_b, w_out, mix_post_g, ffn2_pre_g, ffn2_w_gate, ffn2_w_up, ffn2_w_down,
    ffn2_post_g, p_2, positions_2, mix_norm_2, w_in_2, a_cmp_pos_k_2, a_cmp_w1_k_2,
    a_cmp_w2_k_2, a_cmp_pos_v_2, a_cmp_w1_v_2, a_cmp_w2_v_2, b_sinks_2, c_q_norm_2, c_w_q_up_2,
    c_kv_norm_2, c_w_kv_up_2, w_branch_gate_2, w_branch_a_2, w_branch_b_2, w_branch_c_2,
    w_out_2, ffn_norm_2, w_ffn_gate_2, w_ffn_up_2, w_ffn_down_2, ple_norm_2, w_ple_proj_2,
    w_ple_gate_2, final_norm_2,
):
    x = first_block(
        x, ffn1_pre_g, ffn1_w_gate, ffn1_w_up, ffn1_w_down, ffn1_post_g, mix_pre_g, w_in,
        na_rpb, w_branch_a, w_branch_b, w_out, mix_post_g, ffn2_pre_g, ffn2_w_gate, ffn2_w_up,
        ffn2_w_down, ffn2_post_g,
    )
    return second_block(
        x, p_2, positions_2, mix_norm_2, w_in_2, a_cmp_pos_k_2, a_cmp_w1_k_2, a_cmp_w2_k_2,
        a_cmp_pos_v_2, a_cmp_w1_v_2, a_cmp_w2_v_2, b_sinks_2, c_q_norm_2, c_w_q_up_2,
        c_kv_norm_2, c_w_kv_up_2, w_branch_gate_2, w_branch_a_2, w_branch_b_2, w_branch_c_2,
        w_out_2, ffn_norm_2, w_ffn_gate_2, w_ffn_up_2, w_ffn_down_2, ple_norm_2, w_ple_proj_2,
        w_ple_gate_2, final_norm_2,
    )


_drawn_inputs = setup_inputs


def setup_inputs(seed=0):
    import zlib

    import numpy as np

    out = dict(_drawn_inputs(seed))
    spreads = {}
    factors = {'ffn2_post_g': 3.46,
     'mix_norm_2': 4.234,
     'a_cmp_pos_k_2': 8.0,
     'b_sinks_2': 8.0,
     'c_q_norm_2': 8.0,
     'c_kv_norm_2': 8.0,
     'ple_norm_2': 7.033}
    for name, (base, spread) in spreads.items():
        noise = np.random.default_rng([zlib.crc32(name.encode()), seed]).standard_normal(out[name].shape)
        drawn = base * np.exp(spread * noise) if base else spread * noise
        out[name] = jnp.asarray(drawn.astype(out[name].dtype))
    for name, factor in factors.items():
        out[name] = (out[name] * factor).astype(out[name].dtype)
    return out
```

```python
from contextlib import ExitStack

import numpy as np

import concourse.bass as bass
from concourse import mybir

F32 = mybir.dt.float32
F32R = mybir.dt.float32r
I32 = mybir.dt.int32
ALU = mybir.AluOpType
ACT = mybir.ActivationFunctionType
AX = mybir.AxisListType.X

T = 512
DM = 1024
KC = 8
FF = 2816
FC = 22
EPS = 1e-6
NEG = -1e30
BIG = 3e38
BASE = 16512
K = 1024

GAINS = ["ffn1_pre", "ffn1_post", "mix_pre", "mix_post", "ffn2_pre", "ffn2_post",
         "mix2_0", "ffn_0", "ple_0", "mix2_1", "ffn_1", "ple_1", "final"]
CONST = {}
_at = 0
for _n, _w in (("ident", 128), ("perm", 128), ("permc", 96), ("colmask", 64), ("cmpneg", 128),
               ("cmp01", 128), ("sel", 256), ("invf", 2), ("sgn", 2), ("causal", 512), ("band", 256)):
    CONST[_n] = (_at, _w)
    _at += _w
NCONST = _at


class Noted:

    def matmul(self, *a, **k):
        return lambda e: e.matmul(*a, **k)

    def transpose(self, *a, **k):
        return lambda e: e.transpose(*a, **k)

    def activation(self, *a, **k):
        return lambda e: e.activation(*a, **k)

    def copy(self, *a, **k):
        return lambda e: e.copy(*a, **k)

    def tensor_copy(self, *a, **k):
        return lambda e: e.tensor_copy(*a, **k)

    def tensor_tensor(self, *a, **k):
        return lambda e: e.tensor_tensor(*a, **k)

    def tensor_scalar(self, *a, **k):
        return lambda e: e.tensor_scalar(*a, **k)

    def scalar_tensor_tensor(self, *a, **k):
        return lambda e: e.scalar_tensor_tensor(*a, **k)

    def tensor_tensor_reduce(self, *a, **k):
        return lambda e: e.tensor_tensor_reduce(*a, **k)

    def tensor_reduce(self, *a, **k):
        return lambda e: e.tensor_reduce(*a, **k)

    def reciprocal(self, *a, **k):
        return lambda e: e.reciprocal(*a, **k)

    def memset(self, *a, **k):
        return lambda e: e.memset(*a, **k)

    def dma_start(self, *a, **k):
        return lambda e: e.dma_start(*a, **k)


NOTED = Noted()


class Queue:

    def __init__(self, name):
        self.name = name
        self.items = []
        self.at = 0
        self.met = {}

    def need(self, toks):
        for tok in toks:
            if tok is None:
                continue
            if isinstance(tok, list):
                self.need(tok)
                continue
            s, v = tok
            if self.met.get(s, 0) < v:
                self.met[s] = v
                self.items.append(("wait", s, v))

    def do(self, fn, *toks, mark=True):
        self.need(toks)
        self.items.append(("do", fn(NOTED), (self.name, 1) if mark else None))
        if mark:
            self.at += 1
            return (self.name, self.at)
        return None

    def dma(self, fn, sem, total, *toks):
        self.need(toks)
        self.items.append(("do", fn(NOTED), (sem, 16)))
        return (sem, total)

    def play(self, eng, sems):
        for it in self.items:
            if it[0] == "wait":
                eng.wait_ge(sems[it[1]], it[2])
            else:
                ins = it[1](eng)
                if it[2] is not None:
                    ins.then_inc(sems[it[2][0]], it[2][1])


class Ring:

    def __init__(self, bufs):
        self.bufs = bufs
        self.last = [None] * len(bufs)
        self.n = 0
        self.out = set()

    def take(self):
        i = self.n % len(self.bufs)
        self.n += 1
        assert i not in self.out
        self.out.add(i)
        return i, self.bufs[i], self.last[i]

    def give(self, i, *toks):
        self.last[i] = list(toks)
        self.out.remove(i)


def program(nc, seq, D, out):
    pe, act, dve, pool, sp = (Queue(n) for n in ("pe", "act", "dve", "pool", "sp"))
    dsum = {}

    def dma(q, dst, src, *toks, sem="misc"):
        dsum[sem] = dsum.get(sem, 0) + 16
        return q.dma(lambda e: e.dma_start(dst, src), sem, dsum[sem], *toks)

    nmisc = [0]

    def load(dst, src, *toks):
        nmisc[0] += 1
        return dma(pool, dst, src, *toks, sem=f"m{nmisc[0] % 12}")

    def now():
        return [(q.name, q.at) for q in (pe, act, dve, pool) if q.at]

    names = [0]

    def at(shape, off, dt=F32):
        names[0] += 1
        return nc.alloc_sbuf_tensor_at(f"t{names[0]}_{'s' if seq is None else 'r'}", shape, dt,
                                       offset=BASE + off)

    RA = 92 * K
    MI = RA + 88 * K
    xT = at([128, KC, T], 0)
    hT = at([128, 2, KC, T], 16 * K, F32R)
    fT = at([128, KC, T], 16 * K)
    raw = [at([128, 1024], (48 + 4 * i) * K) for i in range(3)]
    spl = [at([128, 2, 1024], (60 + 8 * i) * K, F32R) for i in range(4)]
    con = at([128, NCONST], MI)
    o = MI + (NCONST * 4 + 31) // 32 * 32
    gn = at([128, len(GAINS), KC], o)
    gcn = at([128, 8], o + 416)
    gh = at([128, 2, KC], o + 448)
    ones = at([128, 128], o + 512)
    acc = at([128, T], o + 1024)
    rstd = at([128, T], o + 3 * K)
    st = at([128, 256], o + 5 * K)
    tmp = Ring([at([128, T], o + (6 + 2 * i) * K) for i in range(7)])
    assert o + 20 * K + BASE <= 229368
    Sr = Ring([at([128, T], RA + (78 + 2 * i) * K) for i in range(3)])
    PTr = Ring([at([128, T], RA + (84 + 2 * i) * K) for i in range(2)])
    banks = [nc.alloc_psum_tensor(f"bk{i}_{'s' if seq is None else 'r'}", [128, T], F32)
             for i in range(8)] if seq is not None else [None] * 8
    if seq is None:
        banks = [xT[:, i, :] for i in range(8)]
    PB = Ring(banks[0:4])
    OB = Ring(banks[4:8])

    def cn(name):
        a, w = CONST[name]
        return con[:, a:a + w]

    c_tok = dma(sp, con[:], D["const"], sem="c")
    g_tok = dma(sp, gn[:], D["gains"], sem="c")
    g_tok2 = dma(sp, gcn[:], D["cgains"], sem="c")
    x_tok = dma(sp, xT[:], D["xT"], sem="c")
    c_tok = g_tok = g_tok2 = x_tok = ("c", 64)
    one_tok = dve.do(lambda e: e.memset(ones[:], 1.0))
    gh_tok = [dve.do(lambda e, i=i, j=j: e.tensor_scalar(gh[:, i, :], gn[:, j, :], 0.5, None, ALU.mult),
                     g_tok) for i, j in ((0, 1), (1, 5))]

    units = []
    loaded, parted = [], []
    freed = {}
    AHEAD = 2

    def stream(u):
        if seq is None:
            return
        while len(loaded) <= min(u + AHEAD + 2, len(seq) - 1):
            i = len(loaded)
            if i >= 3 and len(parted) <= i - 3:
                part(i - 3)
            name, m, c0, n = seq[i]
            src = D[name][m, :, c0:c0 + n]
            w = parted[i - 3] if i >= 3 else None
            loaded.append(dma(sp, raw[i % 3][:, 0:n], src, w, sem=f"w{i % 3}"))
        while len(parted) <= min(u + AHEAD, len(seq) - 1):
            part(len(parted))

    def part(i):
        n = seq[i][3]
        hi = spl[i % 4][:, 0, 0:n]
        lo = spl[i % 4][:, 1, 0:n]
        r = raw[i % 3][:, 0:n]
        f = freed[i - 4] if i >= 4 else None
        a = act.do(lambda e: e.copy(hi, r), loaded[i], f)
        b = dve.do(lambda e: e.tensor_tensor(lo, r, hi.bitcast(F32), ALU.subtract), a, loaded[i], f)
        parted.append([a, b])

    def unit(name, m, c0, n):
        u = len(units)
        units.append((name, m, c0, n))
        stream(u)
        return u, spl[u % 4][:, 0, 0:n], spl[u % 4][:, 1, 0:n], (parted[u] if seq is not None else None)

    def mm3(o_, wh, wl, xh, xl, start, stop, *toks):
        pe.do(lambda e: e.matmul(o_, wh, xh, start=start, stop=False), *toks, mark=False)
        pe.do(lambda e: e.matmul(o_, wh, xl, start=False, stop=False), mark=False)
        return lambda mark: pe.do(lambda e: e.matmul(o_, wl, xh, start=False, stop=stop), mark=mark)

    def dense(parts, xs, M=128):
        b, bank, bt = PB.take()
        for i, (name, m, c0, chunks) in enumerate(parts):
            u, wh, wl, wt = unit(name, m, c0, len(chunks) * M)
            for j, c in enumerate(chunks):
                xh, xl, xt = xs(c)
                last = j == len(chunks) - 1
                tok = mm3(bank[0:M, :], wh[:, j * M:(j + 1) * M], wl[:, j * M:(j + 1) * M], xh, xl,
                          i == 0 and j == 0, last and i == len(parts) - 1, wt, xt, bt)(last)
            freed[u] = tok
        return b, bank, tok

    def split(hi, lo, src, *toks):
        a = act.do(lambda e: e.copy(hi, src), *toks)
        b = dve.do(lambda e: e.tensor_tensor(lo, src, hi.bitcast(F32), ALU.subtract), a, *toks)
        return [a, b]

    acc_free = [None]
    rstd_free = [None]

    def square_in(src, first, *toks):
        if first:
            t = act.do(lambda e: e.activation(acc[:], src, ACT.Square), acc_free[0], *toks)
            return t, t
        i, q, f = tmp.take()
        a = act.do(lambda e: e.activation(q[:], src, ACT.Square), f, *toks)
        d = pool.do(lambda e: e.tensor_tensor(acc[:], acc[:], q[:], ALU.add), a, acc_tok[0])
        tmp.give(i, d)
        return d, a

    acc_tok = [None]

    def rms(width, tok):
        b, bank, bt = PB.take()
        t = pe.do(lambda e: e.matmul(bank[:], ones[:], acc[:], start=True, stop=True), bt, tok, one_tok)
        acc_free[0] = t
        a = dve.do(lambda e: e.tensor_scalar(rstd[:], bank[:], 1.0 / width, EPS, ALU.mult, ALU.add),
                   t, rstd_free[0])
        PB.give(b, a)
        a = act.do(lambda e: e.activation(rstd[:], rstd[:], ACT.Ln), a)
        return act.do(lambda e: e.activation(rstd[:], rstd[:], ACT.Exp, scale=-0.5), a)

    def sumsq(srcs, toks):
        reads = []
        for c, s in enumerate(srcs):
            acc_tok[0], r = square_in(s, c == 0, toks[c])
            reads.append(r)
        return reads

    def scaled(srcs, dst, gain, rt, toks, *free):
        res = []
        for c, s in enumerate(srcs):
            i, h, f = tmp.take()
            g = gain(c)
            a = dve.do(lambda e, h=h, s=s, g=g: e.scalar_tensor_tensor(h[:], s, g, rstd[:], ALU.mult, ALU.mult),
                       f, rt, toks[c], g_tok)
            w = split(dst(0, c), dst(1, c), h[:], a, *free)
            tmp.give(i, *w)
            res.append(w)
        rstd_free[0] = dve_last()
        return res

    def dve_last():
        return (dve.name, dve.at)

    def prenorm(gi, xt, sq=None):
        if sq is None:
            sumsq([xT[:, c, :] for c in range(KC)], xt)
        rt = rms(DM, acc_tok[0])
        free = now()
        return scaled([xT[:, c, :] for c in range(KC)], lambda p, c: hT[:, p, c, :],
                      lambda c: gn[:, gi, c:c + 1], rt, xt, free)

    def hs(toks):
        return lambda c: (hT[:, 0, c, :], hT[:, 1, c, :], toks[c])

    def ratio(dst, e1, num, a, *toks):
        p = pool.do(lambda e: e.tensor_scalar(e1, e1, 1.0, None, ALU.add), a)
        r = dve.do(lambda e: e.reciprocal(e1, e1), p)
        return dve.do(lambda e: e.tensor_tensor(dst, num, e1, ALU.mult), r, *toks)

    def sigmul(dst, gbank, other, gtok, *toks, gate_free):
        i, e1, f = tmp.take()
        a = act.do(lambda e: e.activation(e1[:], gbank[:], ACT.Exp, scale=-1.0), gtok, f)
        gate_free(a)
        d = ratio(dst, e1[:], other, a, *toks)
        tmp.give(i, d)
        return d

    def down(name, nk, xs, post, each=None):
        for m in range(KC):
            parts = [(name, m, c0 * 128, list(range(c0, min(c0 + 8, nk)))) for c0 in range(0, nk, 8)]
            b, bank, tok = dense(parts, xs)
            PB.give(b, *post(m, bank, tok))

    def add_post(free):
        ft = []

        def post(m, bank, tok):
            a = act.do(lambda e: e.copy(fT[:, m, :], bank[:]), tok, free)
            acc_tok[0], r = square_in(fT[:, m, :], m == 0, a)
            ft.append(a)
            return [a]
        return post, ft

    def postnorm(gain, ft, xt):
        rt = rms(DM, acc_tok[0])
        new = []
        for c in range(KC):
            i, h, f = tmp.take()
            a = dve.do(lambda e, c=c, h=h: e.scalar_tensor_tensor(h[:], fT[:, c, :], gain(c), rstd[:],
                                                                 ALU.mult, ALU.mult), f, rt, ft[c], g_tok, gh_tok)
            b = dve.do(lambda e, c=c, h=h: e.tensor_tensor(xT[:, c, :], xT[:, c, :], h[:], ALU.add), a, xt[c])
            tmp.give(i, b)
            acc_tok[0], r = square_in(xT[:, c, :], c == 0, b)
            new.append([b, r])
        rstd_free[0] = dve_last()
        return new

    def ffn(name, ht, hook=None):
        free = now()
        hid = at([128, 2, FC, T], RA, F32R)
        toks = []
        for j in range(FC):
            bg, g, tg = dense([(name + "_g", j, 0, list(range(8)))], hs(ht))
            bu, u_, tu = dense([(name + "_u", j, 0, list(range(8)))], hs(ht))
            i, s, f = tmp.take()
            ie, e1, fe = tmp.take()
            a = act.do(lambda e, g=g, e1=e1: e.activation(e1[:], g[:], ACT.Exp, scale=-1.0), tg, fe)
            d = ratio(s[:], e1[:], g[:], a, f)
            PB.give(bg, d)
            tmp.give(ie, d)
            d = dve.do(lambda e, u_=u_, s=s: e.tensor_tensor(s[:], s[:], u_[:], ALU.mult), d, tu)
            PB.give(bu, d)
            w = split(hid[:, 0, j, :], hid[:, 1, j, :], s[:], d, free, rope_done if j >= 10 else None)
            tmp.give(i, *w)
            toks.append(w)
            if hook is not None and j == 1:
                hook()
        return lambda c: (hid[:, 0, c, :], hid[:, 1, c, :], toks[c])

    flip = [0]

    def attend(us):
        n = len(us)
        st_ = [dict() for _ in us]
        for s in range(n + 3):
            if s < n:
                U, X = us[s], st_[s]
                if U.get("pre"):
                    U["pre"]()
                w = U["w"]
                b, bank, bt = PB.take()
                q, k = U["q"](), U["k"]()
                t = pe.do(lambda e, bank=bank, q=q, k=k, w=w: e.matmul(bank[:, 0:w], q, k, start=True, stop=True),
                          bt, U["qk"]())
                i, S, f = Sr.take()
                X.update(S=S, i=i)
                d = dve.do(lambda e, U=U, S=S, bank=bank, w=w: e.tensor_tensor_reduce(
                    S[:, 0:w], bank[:, 0:w], U["table"], -U["scale"], U.get("init", BIG), ALU.add, ALU.min,
                    U["nm"]), t, f, U.get("tt"))
                PB.give(b, d)
                X["e"] = act.do(lambda e, U=U, S=S, w=w: e.activation(
                    S[:, 0:w], S[:, 0:w], ACT.Exp, bias=U["nm"], scale=-1.0, accum_out=U["sm"]), d)
                X["d"] = d
            if 0 <= s - 2 < n:
                U, X = us[s - 2], st_[s - 2]
                w, S = U["w"], X["S"]
                b, bank, bt = PB.take()
                for j in range(w // 128):
                    t = pe.do(lambda e, bank=bank, S=S, j=j: e.transpose(
                        bank[:, j * 128:(j + 1) * 128], S[:, j * 128:(j + 1) * 128], cn("ident")),
                        bt, X["e"], c_tok, mark=j == w // 128 - 1)
                Sr.give(X["i"], t)
                i, PT, f = PTr.take()
                flip[0] += 1
                q = act if flip[0] % 3 == 0 else dve
                if q is act:
                    d = act.do(lambda e, PT=PT, bank=bank, w=w: e.copy(PT[:, 0:w], bank[:, 0:w]), t, f)
                else:
                    d = dve.do(lambda e, PT=PT, bank=bank, w=w: e.tensor_copy(PT[:, 0:w], bank[:, 0:w]), t, f)
                PB.give(b, d)
                X.update(PT=PT, pi=i, p=d)
            if 0 <= s - 3 < n:
                U, X = us[s - 3], st_[s - 3]
                if U.get("open"):
                    U["open"]()
                vs, o_ = U["v"](), U["o"]()
                for j, v in enumerate(vs):
                    t = pe.do(lambda e, j=j, v=v, X=X, o_=o_, m=len(vs): e.matmul(
                        o_, X["PT"][:, j * 128:(j + 1) * 128], v, start=j == 0, stop=j == m - 1),
                        X["p"], U["vt"](), U["ot"](), mark=j == len(vs) - 1)
                PTr.give(X["pi"], t)
                X["t"] = t
                if U.get("done"):
                    U["done"](t)

    def to_features(src, ncol, dst, *toks):
        b, bank, bt = PB.take()
        for c in range(ncol // 128):
            t = pe.do(lambda e, c=c: e.transpose(bank[:, c * 128:(c + 1) * 128], src[:, c * 128:(c + 1) * 128],
                                                 cn("ident")), bt, c_tok, *toks, mark=c == ncol // 128 - 1)
        PB.give(b, *dst(bank, t))
        return t

    def split_out(oT, qt, n=4):
        res = []

        def dst(bank, t):
            src = bank[:, 0:n * 128].rearrange("p (c t) -> p c t", c=n)
            w = split(oT[:, 0, :, qt * 128:(qt + 1) * 128], oT[:, 1, :, qt * 128:(qt + 1) * 128], src, t,
                      oT_free[0])
            res.extend(w)
            return w
        return dst, res

    oT_free = [None]
    S_NM, S_SM = 0, 64
    nm = lambda i: st[:, S_NM + i:S_NM + i + 1]
    sm = lambda i: st[:, S_SM + i:S_SM + i + 1]

    def heads8(bank, rs, *toks, out_):
        return dve.do(lambda e: e.tensor_tensor(
            out_[:].rearrange("p (h d) -> p h d", h=8), bank[:].rearrange("p (h d) -> p h d", h=8),
            rs.unsqueeze(2).broadcast_to([128, 8, 64]), ALU.mult), *toks)

    def project(name, m, xs, dst, *free, view=lambda a: a, M=128):
        b, bank, tok = dense([(name, m, 0, list(range(8)))], xs, M)
        d = act.do(lambda e: e.copy(dst, view(bank[0:M, :])), tok, *free)
        PB.give(b, d)
        return d

    def tokens_first(name, ncol, per, xs, dst, *free, toks_of=None, nk=8):
        if toks_of is None:
            toks_of = lambda a, t: a[:, t * 128:(t + 1) * 128]
        bs = [OB.take() for _ in range(4)]
        for k0 in range(0, nk, per):
            u, wh, wl, wt = unit(name, 0, k0 * ncol, per * ncol)
            for j in range(per):
                xh, xl, xt = xs(k0 + j)
                for t in range(4):
                    last = j == per - 1 and t == 3
                    o_ = bs[t][1][:, 0:ncol]
                    s, e_ = k0 + j == 0, k0 + j == nk - 1
                    a, b_ = wh[:, j * ncol:(j + 1) * ncol], wl[:, j * ncol:(j + 1) * ncol]
                    hh, hl = toks_of(xh, t), toks_of(xl, t)
                    pe.do(lambda e, o_=o_, hh=hh, a=a, s=s: e.matmul(o_, hh, a, start=s, stop=False),
                          wt, xt, bs[t][2], mark=False)
                    pe.do(lambda e, o_=o_, hh=hh, b_=b_: e.matmul(o_, hh, b_, start=False, stop=False), mark=False)
                    tok = pe.do(lambda e, o_=o_, hl=hl, a=a, e_=e_: e.matmul(o_, hl, a, start=False, stop=e_))
                    if e_:
                        d = act.do(lambda e, t=t, o_=o_: e.copy(dst(t), o_), tok, *free)
                        OB.give(bs[t][0], d)
            freed[u] = tok
        return d

    xt = [x_tok] * KC
    ht = prenorm(0, xt)

    rope_done = []

    rope_tok = []

    def rope_tables():
        pi_ = at([128, T], RA + 64 * K, I32)
        pf = at([128, T], RA + 66 * K)
        ang = at([128, T], RA + 68 * K)
        y = at([128, T], RA + 70 * K)
        ki = at([128, T], RA + 72 * K, I32)
        kf = at([128, T], RA + 74 * K)
        r = [at([128, T], RA + (76 + 2 * i) * K) for i in range(4)]
        a = load(pi_[:], D["positions"].partition_broadcast(128), now())
        a = dve.do(lambda e: e.tensor_copy(pf[:], pi_[:]), a)
        prev = None
        for w in range(2):
            ang_t = dve.do(lambda e, w=w: e.tensor_scalar(ang[:], pf[:], cn("invf")[:, w:w + 1], None, ALU.mult),
                           a, c_tok, prev)
            for j, (frac, ph) in enumerate(((0.25, float(np.pi / 2)), (0.0, 0.0))):
                d = r[2 * w + j]
                x = dve.do(lambda e, frac=frac: e.tensor_scalar(y[:], ang[:], float(1 / (2 * np.pi)), frac,
                                                               ALU.mult, ALU.add), ang_t, dve_last())
                x = dve.do(lambda e: e.tensor_copy(ki[:], y[:]), x)
                x = dve.do(lambda e: e.tensor_copy(kf[:], ki[:]), x)
                c1, c2, c3 = 6.28125, 0.0019340515136718750, float(2 * np.pi - 6.28125 - 0.0019340515136718750)
                x = dve.do(lambda e: e.scalar_tensor_tensor(y[:], kf[:], -c1, ang[:], ALU.mult, ALU.add), x)
                x = dve.do(lambda e: e.scalar_tensor_tensor(y[:], kf[:], -c2, y[:], ALU.mult, ALU.add), x)
                x = dve.do(lambda e: e.scalar_tensor_tensor(y[:], kf[:], -c3, y[:], ALU.mult, ALU.add), x)
                x = dve.do(lambda e, ph=ph: e.tensor_scalar(y[:], y[:], ph, 3.1415925, ALU.add, ALU.min), x)
                x = dve.do(lambda e: e.tensor_scalar(y[:], y[:], -3.1415925, None, ALU.max), x)
                x = act.do(lambda e, d=d: e.activation(d[:], y[:], ACT.Sin), x)
                if j == 1:
                    x = dve.do(lambda e, d=d, w=w: e.tensor_scalar(d[:], d[:], cn("sgn")[:, w:w + 1], None,
                                                                   ALU.mult), x)
                elif w == 1:
                    x = dve.do(lambda e, d=d: e.memset(d[0:64, :], 1.0), x)
                prev = x
                dve.need([x])
                rope_tok.append(load(D["rope"][2 * w + j], d[:], x))
                rope_done.append(rope_tok[-1])

    xs = ffn("f1", ht, hook=rope_tables)
    post, ft = add_post(now())
    down("f1_d", FC, xs, post)
    xt = postnorm(lambda c: gh[:, 0, c:c + 1], ft, xt)
    ht = prenorm(2, xt, sq=True)

    H = hs(ht)
    fr = now()
    oa = at([128, 2, 4, T], RA, F32R)
    qa = at([128, 4, T], RA + 16 * K)
    ka = at([128, 4, T], RA + 24 * K)
    va = at([128, 4, T], RA + 32 * K)
    rp = at([120, 127], RA + 60 * K)
    BT = Ring([at([128, 14, 64], RA + 40 * K + i * 3584) for i in range(2)])
    z = dve.do(lambda e: e.memset(rp[:], 0.0), fr, rope_done)
    z = load(rp[:, 48:79], D["rpb"], z)
    z = load(D["rpbs"].ap().rearrange("(a c b) -> a c b", b=127, c=64),
             rp[:].unsqueeze(1).broadcast_to([120, 64, 127]), z)
    qt_, kt_ = [], []
    for m in range(4):
        qt_.append(project("qka", m, H, qa[:, m, :], fr))
    for m in range(4):
        kt_.append(project("qka", 4 + m, H, ka[:, m, :], fr))
    v_t = tokens_first("va", 512, 2, H, lambda t: va[:, t, :], fr)
    ob4 = {}
    bt_ = {}

    def na_table(h):
        i, bt, f = BT.take()
        w = None
        for a in range(2):
            src = bass.AP(D["rpbs"], (h * 15 + (1 - a)) * 8128 + 63, [[126, 64], [8128, 14], [1, 64]])
            w = load(bt[64 * a:64 * a + 64, :, :], src, z, f, w)
        d = dve.do(lambda e: e.scalar_tensor_tensor(
            bt[:], bt[:], 8.0, cn("colmask").unsqueeze(1).broadcast_to([128, 14, 64]), ALU.mult, ALU.add),
            w, c_tok)
        bt_[h] = (i, bt, d)

    na_table(0)
    na_table(1)
    na_us = []
    for h in range(8):
        for qt in range(4):
            p0 = 64 * (h % 2)

            def opn(h=h, qt=qt):
                if h == 0:
                    ob4[qt] = OB.take()

            def done(t, h=h, qt=qt):
                if qt == 3:
                    BT.give(bt_[h][0], *now())
                    if h + 2 < 8:
                        na_table(h + 2)
                if h == 7:
                    ob4[qt] = ob4[qt] + (t,)

            na_us.append(dict(
                w=512, q=lambda h=h, qt=qt, p0=p0: qa[p0:p0 + 64, h // 2, qt * 128:(qt + 1) * 128],
                k=lambda h=h, p0=p0: ka[p0:p0 + 64, h // 2, :], qk=lambda h=h: [qt_[h // 2], kt_[h // 2]],
                scale=0.125, nm=nm(qt * 8 + h), sm=sm(qt * 8 + h), open=opn, done=done,
                v=lambda h=h: [va[:, j, h * 64:(h + 1) * 64] for j in range(4)], vt=lambda: v_t,
                o=lambda h=h, qt=qt: ob4[qt][1][:, h * 64:(h + 1) * 64], ot=lambda qt=qt: ob4[qt][2]))

            def setup(U=na_us[-1], h=h, qt=qt):
                U["table"] = bt_[h][1][:, 6 - 2 * qt:14 - 2 * qt, :].rearrange("p j k -> p (j k)")
                U["tt"] = bt_[h][2]
            na_us[-1]["pre"] = setup
    attend(na_us)
    oa_t = []
    oT_free[0] = fr
    for qt in range(4):
        rs = st[:, 128:136]
        d = dve.do(lambda e, qt=qt: e.reciprocal(rs, st[:, S_SM + qt * 8:S_SM + qt * 8 + 8]), now())
        i, os_, f = tmp.take()
        d = heads8(ob4[qt][1], rs, d, f, ob4[qt][3], out_=os_)
        OB.give(ob4[qt][0], d)
        dst, res = split_out(oa, qt)
        tmp.give(i, to_features(os_, 512, dst, d))
        oa_t += res

    fr = now()
    obf = at([128, 6, T], RA + 40 * K)
    tb = at([128, 4, 640], RA + 52 * K)
    stm = at([4, 6, T], RA + 62 * K)
    tb_t = load(tb[:], D["dil"], fr)

    def perm_tile(a, g, t):
        if g == 0:
            return a[:, t * 128:(t + 1) * 128]
        return a.rearrange("p (l r) -> p r l", r=4)[:, t, :]

    def perm_all(a, g):
        return a if g == 0 else a.rearrange("p (l r) -> p r l", r=4)

    def shaped(a, g):
        return a if g == 0 else a.rearrange("p (r l) -> p r l", r=4)

    stm_t = []
    obf_t = []
    for g in range(3):
        o0 = RA + 16 * K + (g % 2) * 12 * K
        qg = at([128, 2, T], o0)
        kg = at([128, 2, T], o0 + 4 * K)
        vg = at([128, 4, 256], o0 + 8 * K)
        frg = fr if g < 2 else now()
        qt_ = [project("qb", 2 * g + c, H, shaped(qg[:, c, :], g), frg, view=lambda a, g=g: perm_all(a, g))
               for c in range(2)]
        kt_ = [project("kb", 2 * g + c, H, shaped(kg[:, c, :], g), frg, view=lambda a, g=g: perm_all(a, g))
               for c in range(2)]
        v_t = tokens_first(f"vb{g}", 256, 4, H, lambda t: vg[:, t, :], frg, toks_of=lambda a, t, g=g: perm_tile(a, g, t))
        us = []
        obk = {}
        for t in range(4):
            for hh in range(4):
                if g == 0:
                    a, b = max(0, t - 1), min(4, t + 2)
                    tab = tb[:, hh, (a - t + 1) * 128:(b - t + 1) * 128]
                else:
                    a, b = t, t + 1
                    tab = tb[:, hh, 256 + g * 128:384 + g * 128]
                p0 = 64 * (hh % 2)

                def opn(t=t, hh=hh):
                    if hh == 0:
                        obk[t] = OB.take()

                def done(tok, t=t, hh=hh, g=g, obk=obk):
                    if hh < 3:
                        return
                    rs = st[:, 128 + 4 * t:132 + 4 * t]
                    d = dve.do(lambda e: e.reciprocal(rs, st[:, S_SM + 4 * t:S_SM + 4 * t + 4]), now())
                    i, os_, f = tmp.take()
                    bank = obk[t][1]
                    d = dve.do(lambda e: e.tensor_tensor(
                        os_[:, 0:256].rearrange("p (h d) -> p h d", h=4),
                        bank[:, 0:256].rearrange("p (h d) -> p h d", h=4),
                        rs.unsqueeze(2).broadcast_to([128, 4, 64]), ALU.mult), d, f, tok)
                    OB.give(obk[t][0], d)

                    def dst(bk, tk):
                        for c in range(2):
                            o_ = perm_tile(obf[:, 2 * g + c, :], g, t)
                            s_ = bk[:, c * 128:(c + 1) * 128]
                            a_ = act.do(lambda e, o_=o_, s_=s_: e.copy(o_, s_), tk, fr)
                        obf_t.append(a_)
                        return [a_]
                    tmp.give(i, to_features(os_, 256, dst, d))
                    b, bk, bt = PB.take()
                    for k_, s0 in ((0, S_NM), (1, S_SM)):
                        tk = pe.do(lambda e, k_=k_, s0=s0: e.transpose(
                            bk[0:4, k_ * 128:(k_ + 1) * 128], st[:, s0 + 4 * t:s0 + 4 * t + 4], cn("ident")), bt,
                            d, now())
                    for k_ in range(2):
                        o_ = perm_tile(stm[:, 2 * g + k_, :], g, t)
                        s_ = bk[0:4, k_ * 128:(k_ + 1) * 128]
                        a_ = act.do(lambda e, o_=o_, s_=s_: e.copy(o_, s_), tk, fr)
                    PB.give(b, a_)
                    stm_t.append(a_)

                us.append(dict(
                    w=(b - a) * 128, q=lambda t=t, hh=hh, p0=p0, qg=qg: qg[p0:p0 + 64, hh // 2, t * 128:(t + 1) * 128],
                    k=lambda a=a, b=b, hh=hh, p0=p0, kg=kg: kg[p0:p0 + 64, hh // 2, a * 128:b * 128],
                    qk=lambda hh=hh, qt_=qt_, kt_=kt_: [qt_[hh // 2], kt_[hh // 2]], scale=0.125, table=tab, tt=tb_t,
                    nm=nm(4 * t + hh), sm=sm(4 * t + hh), open=opn, done=done,
                    v=lambda a=a, b=b, hh=hh, vg=vg: [vg[:, j, hh * 64:(hh + 1) * 64] for j in range(a, b)],
                    vt=lambda v_t=v_t: v_t, o=lambda t=t, hh=hh, obk=obk: obk[t][1][:, hh * 64:(hh + 1) * 64],
                    ot=lambda t=t, obk=obk: obk[t][2]))
        attend(us)

    i0, t0, f0 = tmp.take()
    w = t0[0:4, :]
    al = [stm_t]
    a = dve.do(lambda e: e.tensor_tensor(w, stm[:, 0, :], stm[:, 2, :], ALU.min), stm_t, f0)
    a = dve.do(lambda e: e.tensor_tensor(w, w, stm[:, 4, :], ALU.min), a)
    for g in range(3):
        b = dve.do(lambda e, g=g: e.tensor_tensor(stm[:, 2 * g, :], w, stm[:, 2 * g, :], ALU.subtract), a)
        b = act.do(lambda e, g=g: e.activation(stm[:, 2 * g, :], stm[:, 2 * g, :], ACT.Exp), b)
        c = dve.do(lambda e, g=g: e.tensor_tensor(stm[:, 2 * g + 1, :], stm[:, 2 * g, :], stm[:, 2 * g + 1, :],
                                                  ALU.mult), b)
    a = dve.do(lambda e: e.tensor_tensor(w, stm[:, 1, :], stm[:, 3, :], ALU.add), c)
    a = dve.do(lambda e: e.tensor_tensor(w, w, stm[:, 5, :], ALU.add), a)
    a = dve.do(lambda e: e.reciprocal(w, w), a)
    for g in range(3):
        al = dve.do(lambda e, g=g: e.tensor_tensor(stm[:, 2 * g + 1, :], stm[:, 2 * g + 1, :], w, ALU.mult), a)
    tmp.give(i0, al)
    fr = now()
    ob = at([128, 2, 6, T], RA + 16 * K, F32R)
    ob_t = []
    for c6 in range(6):
        b, bank, bt = PB.take()
        t = pe.do(lambda e, c6=c6, bank=bank: e.matmul(
            bank[:], cn("sel")[0:4, (c6 % 2) * 128:(c6 % 2 + 1) * 128], stm[:, 2 * (c6 // 2) + 1, :],
            start=True, stop=True), bt, al, c_tok)
        i, s, f = tmp.take()
        d = dve.do(lambda e, c6=c6, s=s, bank=bank: e.tensor_tensor(s[:], bank[:], obf[:, c6, :], ALU.mult),
                   t, f, obf_t)
        PB.give(b, d)
        wv = split(ob[:, 0, c6, :], ob[:, 1, c6, :], s[:], d, fr)
        tmp.give(i, *wv)
        ob_t.append(wv)

    def merge(mg, fr, branches, H):
        toks = []
        for m in range(KC):
            acc_i = None
            for n, (gname, g0, parts, xs_) in enumerate(branches):
                bg, gb, tg = dense([(gname, g0 + m, 0, list(range(8)))], H)
                bo, bb, to = dense([(nm_, m, c0, ch) for nm_, c0, ch in parts], xs_)
                i, s, f = tmp.take()
                d = sigmul(s[:], gb, bb[:], tg, to, f, gate_free=lambda a, bg=bg: PB.give(bg, a))
                PB.give(bo, d)
                if acc_i is None:
                    acc_i, s0 = i, s
                else:
                    d = dve.do(lambda e, s=s, s0=s0: e.tensor_tensor(s0[:], s0[:], s[:], ALU.add), d)
                    tmp.give(i, d)
            w_ = split(mg[:, 0, m, :], mg[:, 1, m, :], s0[:], d, fr)
            tmp.give(acc_i, *w_)
            toks.append(w_)
        return lambda c: (mg[:, 0, c, :], mg[:, 1, c, :], toks[c])

    fr = now()
    mg = at([128, 2, KC, T], RA + 40 * K, F32R)
    xs = merge(mg, fr, [
        ("ga", 0, [("bra", 0, list(range(4)))], lambda c: (oa[:, 0, c, :], oa[:, 1, c, :], oa_t)),
        ("gb", 0, [("brb", 0, list(range(6)))], lambda c: (ob[:, 0, c, :], ob[:, 1, c, :], ob_t[c]))], H)
    post, ft = add_post(now())
    down("wo", KC, xs, post)
    xt = postnorm(lambda c: gn[:, 3, c:c + 1], ft, xt)
    ht = prenorm(4, xt, sq=True)
    xs = ffn("f2", ht)
    post, ft = add_post(now())
    down("f2_d", FC, xs, post)
    xt = postnorm(lambda c: gh[:, 1, c:c + 1], ft, xt)

    def rope(src_bank, b, tok, dst, M, cs, sn, permn, tr, *free):
        iy, y, fy = tmp.take()
        a = act.do(lambda e: e.copy(y[0:M, :], src_bank[0:M, :]), tok, fy)
        PB.give(b, a)
        b2, bk2, bt2 = PB.take()
        t = pe.do(lambda e: e.matmul(bk2[0:M, :], cn(permn)[0:M, :], y[0:M, :], start=True, stop=True),
                  bt2, a, c_tok)
        ir, r, f_r = tmp.take()
        d1 = dve.do(lambda e: e.tensor_tensor(r[0:M, :], bk2[0:M, :], sn[0:M, :], ALU.mult), t, f_r, tr)
        PB.give(b2, d1)
        d2 = pool.do(lambda e: e.tensor_tensor(y[0:M, :], y[0:M, :], cs[0:M, :], ALU.mult), a, t, tr)
        if callable(dst):
            d = dve.do(lambda e: e.tensor_tensor(r[0:M, :], y[0:M, :], r[0:M, :], ALU.add), d1, d2)
            w_ = dst(r, d)
            tmp.give(ir, *w_)
            tmp.give(iy, d)
            return w_
        d = dve.do(lambda e: e.tensor_tensor(dst, y[0:M, :], r[0:M, :], ALU.add), d1, d2, *free)
        tmp.give(ir, d)
        tmp.give(iy, d)
        return [d]

    def causal_units(qf, kf, qk, vf, vt, obank, hq, h, qt, scale, col, **kw):
        w = (qt + 1) * 128
        return dict(w=w, q=qf, k=kf, qk=qk, scale=scale, table=cn("causal")[:, 384 - qt * 128:512], tt=c_tok,
                    nm=nm(col), sm=sm(col), v=vf, vt=vt, **kw)

    for L in range(2):
        ht = prenorm(6 + 3 * L, xt, sq=True)
        H = hs(ht)
        fr = now()
        s_ = str(L)
        oc = at([128, 2, 4, T], RA, F32R)
        ob = at([128, 2, 4, T], RA + 16 * K, F32R)
        oa = at([128, 2, 4, T], RA + 32 * K, F32R)
        rt_ = at([128, 4, T], RA + 48 * K)
        r_t = [load(rt_[:, i, :], D["rope"][i], fr, rope_tok[i]) for i in range(4)]
        cl = at([128, 2, 4, T], RA + 16 * K, F32R)
        cv = at([128, 4, T], RA + 32 * K)
        qf = Ring([at([96, T], RA + (40 + 2 * i) * K) for i in range(2)])
        kf = Ring([at([96, T], RA + (44 + 2 * i) * K) for i in range(2)])
        cf = at([128, 4, T], RA + 56 * K)
        ct = []
        for m in range(4):
            ct.append(project("clat" + s_, m, H, cf[:, m, :], fr))
        clt = []
        for n in range(2):
            sumsq([cf[:, 2 * n + c, :] for c in range(2)], ct[2 * n:2 * n + 2])
            rt = rms(256, acc_tok[0])
            clt += scaled([cf[:, 2 * n + c, :] for c in range(2)], lambda p, c, n=n: cl[:, p, 2 * n + c, :],
                          lambda c, n=n: gcn[:, 4 * L + 2 * n + c:4 * L + 2 * n + c + 1], rt,
                          ct[2 * n:2 * n + 2], fr)
        b, bank, tok = dense([("kpe" + s_, 0, 0, list(range(8)))], H, 96)

        def kpe(r, d):
            return [dve.do(lambda e, i=i: e.tensor_copy(kf.bufs[i][64:96, :], r[64:96, :]), d, fr)
                    for i in range(2)]
        kp_t = rope(bank, b, tok, kpe, 96, rt_[:, 2, :], rt_[:, 3, :], "permc", r_t[2:4])
        CX = lambda n: (lambda c: (cl[:, 0, 2 * n + c, :], cl[:, 1, 2 * n + c, :], clt[2 * n + c]))
        v_t = tokens_first("cv" + s_, 512, 2, CX(1), lambda t: cv[:, t, :], fr, nk=2)
        hd = {}
        ob4 = {}
        us = []

        def head_in(h):
            if h % 2 == 0:
                hd["u"] = unit("cup" + s_, h // 2, 0, 640)
            u, wh, wl, wt = hd["u"]
            c0 = 320 * (h % 2)
            res = []
            for n, M in ((0, 96), (1, 64)):
                b, bank, bt = PB.take()
                for c in range(2):
                    xh, xl, xt_ = CX(n)(c)
                    a_ = c0 + 192 * n + c * M
                    tok = mm3(bank[0:M, :], wh[:, a_:a_ + M], wl[:, a_:a_ + M], xh, xl, c == 0, c == 1,
                              wt, xt_, bt)(c == 1)
                res.append((b, bank, tok))
            freed[u] = tok
            iq, q_, fq = qf.take()
            ik, k_, fk = kf.take()
            b, bank, tok = res[1]
            kt = act.do(lambda e: e.copy(k_[0:64, :], bank[0:64, :]), tok, fk, fr)
            PB.give(b, kt)
            b, bank, tok = res[0]
            qt2 = rope(bank, b, tok, q_[:], 96, rt_[:, 2, :], rt_[:, 3, :], "permc", r_t[2:4], fq, fr)
            hd[h] = (iq, q_, ik, k_, [kt, qt2, kp_t])

        for h in range(8):
            for qt in range(4):
                def pre(h=h, qt=qt):
                    if qt == 0:
                        head_in(h)

                def opn(h=h, qt=qt):
                    if h == 0:
                        ob4[qt] = OB.take()

                def done(t, h=h, qt=qt):
                    if qt == 3:
                        qf.give(hd[h][0], t)
                        kf.give(hd[h][2], t)
                    if h == 7:
                        ob4[qt] = ob4[qt] + (t,)
                us.append(causal_units(
                    lambda h=h, qt=qt: hd[h][1][:, qt * 128:(qt + 1) * 128],
                    lambda h=h, qt=qt: hd[h][3][:, 0:(qt + 1) * 128], lambda h=h: hd[h][4],
                    lambda h=h, qt=qt: [cv[:, j, h * 64:(h + 1) * 64] for j in range(qt + 1)],
                    lambda: v_t, None, None, h, qt, float(96 ** -0.5), qt * 8 + h, pre=pre, open=opn, done=done,
                    o=lambda h=h, qt=qt: ob4[qt][1][:, h * 64:(h + 1) * 64], ot=lambda qt=qt: ob4[qt][2]))
        attend(us)
        oT_free[0] = fr
        oc_t = []
        for qt in range(4):
            rs = st[:, 128:136]
            d = dve.do(lambda e, qt=qt: e.reciprocal(rs, st[:, S_SM + qt * 8:S_SM + qt * 8 + 8]), now())
            i, os_, f = tmp.take()
            d = heads8(ob4[qt][1], rs, d, f, ob4[qt][3], out_=os_)
            OB.give(ob4[qt][0], d)
            dst, res = split_out(oc, qt)
            tmp.give(i, to_features(os_, 512, dst, d))
            oc_t += res

        fr = now()
        va = at([128, 4, 408], RA + 71 * K)
        qb = at([128, 4, T], RA + 56 * K)
        kb = at([128, 2, T], RA + 64 * K)
        snk = st[:, 136:144]
        nsk = st[:, 144:152]
        s_t = load(snk, D["sinks"][L], fr)
        s_t = dve.do(lambda e: e.tensor_scalar(nsk, snk, -1.0, None, ALU.mult), s_t)
        v_t = tokens_first("v2" + s_, 408, 2, H, lambda t: va[:, t, :], fr)

        def roped(name, m, dst):
            b, bank, tok = dense([(name, m, 0, list(range(8)))], H)
            return rope(bank, b, tok, dst, 128, rt_[:, 0, :], rt_[:, 1, :], "perm", r_t[0:2], fr)

        kt_ = [roped("kb2" + s_, m, kb[:, m, :]) for m in range(2)]
        qt_ = [roped("qb2" + s_, m, qb[:, m, :]) for m in range(4)]
        us = []
        obk = {}
        ob_t = []
        oT_free[0] = fr
        for qt in range(4):
            for h in range(8):
                a = max(0, qt - 1)
                p0 = 64 * (h % 2)

                def opn(qt=qt, h=h):
                    if h == 0:
                        obk[qt] = OB.take()

                def done(tok, qt=qt, h=h):
                    if h < 7:
                        return
                    es, rs = st[:, 152 + 8 * 0:160], st[:, 128:136]
                    c = qt * 8
                    d = dve.do(lambda e: e.tensor_tensor(es, snk, st[:, S_NM + c:S_NM + c + 8], ALU.add), now())
                    d = act.do(lambda e: e.activation(es, es, ACT.Exp), d)
                    d = dve.do(lambda e: e.tensor_tensor(rs, es, st[:, S_SM + c:S_SM + c + 8], ALU.add), d)
                    d = dve.do(lambda e: e.reciprocal(rs, rs), d)
                    i, os_, f = tmp.take()
                    d = heads8(obk[qt][1], rs, d, f, tok, out_=os_)
                    OB.give(obk[qt][0], d)
                    dst, res = split_out(ob, qt)
                    tmp.give(i, to_features(os_, 512, dst, d))
                    ob_t.extend(res)
                us.append(dict(
                    w=(qt + 1 - a) * 128, q=lambda qt=qt, h=h, p0=p0: qb[p0:p0 + 64, h // 2, qt * 128:(qt + 1) * 128],
                    k=lambda qt=qt, a=a, h=h, p0=p0: kb[p0:p0 + 64, h // 4, a * 128:(qt + 1) * 128],
                    qk=lambda h=h: [qt_[h // 2], kt_[h // 4]], scale=0.125,
                    table=cn("band")[:, (a - qt + 1) * 128:256], tt=[c_tok, s_t], init=nsk[:, h:h + 1],
                    nm=nm(qt * 8 + h), sm=sm(qt * 8 + h), open=opn, done=done,
                    v=lambda qt=qt, a=a, h=h: [va[:, j, 256 + (h // 4) * 64:320 + (h // 4) * 64]
                                               for j in range(a, qt + 1)],
                    vt=lambda: v_t, o=lambda qt=qt, h=h: obk[qt][1][:, h * 64:(h + 1) * 64],
                    ot=lambda qt=qt: obk[qt][2]))
        attend(us)

        fr = now()
        k2 = [at([128, 2, 2, 560], RA + o_ * K, F32R) for o_ in (32, 56)]
        w2 = at([128, 2, 192], RA + 41 * K)
        pos = at([128, 2, 32], RA + 43 * K)
        kcm = at([128, 64], RA + 68 * K)
        hid = at([128, 2, 2, 34], RA + 68 * K + 256)
        bd = at([128, 2, 256], RA + 69 * K)
        w2_t = load(w2[:], D["w2"][L], fr)
        p_t = load(pos[:], D["cpos"][L], fr)
        bd_t = dve.do(lambda e: e.memset(bd[:], 0.0), fr)
        for kv in range(2):
            K2 = k2[kv]
            z = dve.do(lambda e, K2=K2: e.memset(K2[:, :, :, 543:560].bitcast(F32), 0.0), fr)
            kt2 = []
            for g in range(2):
                def put(r, d, K2=K2, g=g):
                    w_ = []
                    for p0, sh in ((0, 0), (64, 1)):
                        w_ += split(K2[p0:p0 + 64, 0, g, 0:512 - sh], K2[p0:p0 + 64, 1, g, 0:512 - sh],
                                    r[p0:p0 + 64, sh:512], d, fr)
                    return w_
                if kv == 0:
                    kt2 += roped("kc" + s_, g, put)
                else:
                    b, bank, tok = dense([("kc" + s_, 2 + g, 0, list(range(8)))], H)
                    w_ = put(bank, tok)
                    PB.give(b, *w_)
                    kt2 += w_
                for p0, sh in ((0, 0), (64, 1)):
                    kt2 += split(K2[p0:p0 + 64, 0, g, 512 - sh:544 - sh], K2[p0:p0 + 64, 1, g, 512 - sh:544 - sh],
                                 pos[p0:p0 + 64, kv, :], p_t, z)
            bb = [PB.take() for _ in range(2)]
            for j4 in range(4):
                u, wh, wl, wt = unit("cw1" + s_, kv, j4 * 1024, 1024)
                for jj in range(4):
                    j = j4 * 4 + jj
                    for ch in range(2):
                        o_ = bb[ch][1][:, 0:68].rearrange("p (g n) -> p g n", g=2)
                        xh, xl = (K2[:, p, :, 2 * j:2 * j + 529].rearrange("p g n -> p g n")[:, :, 0:529:16]
                                  for p in range(2))
                        a_ = jj * 256 + ch * 128
                        tok = mm3(o_, wh[:, a_:a_ + 128], wl[:, a_:a_ + 128], xh, xl, j == 0, j == 15,
                                  wt, kt2, bb[ch][2])(True)
                freed[u] = tok
            i, xx, f = tmp.take()
            i2, yy, f2 = tmp.take()
            rd = []
            hb = st[:, 160:162]
            for ch in range(2):
                bank = bb[ch][1]
                x_ = xx[:, ch * 68:ch * 68 + 68]
                d = dve.do(lambda e, ch=ch, bank=bank: e.tensor_copy(hb[:, ch:ch + 1], bank[:, 32:33]), tok,
                           dve_last())
                d = dve.do(lambda e, ch=ch, bank=bank, x_=x_: e.tensor_scalar(x_, bank[:, 0:68], hb[:, ch:ch + 1],
                                                                             None, ALU.add), d, f)
                PB.give(bb[ch][0], d)
            X_, Y_ = xx[:, 0:136], yy[:, 0:136]
            d = dve.do(lambda e, X_=X_, Y_=Y_: e.tensor_tensor(Y_, X_, X_, ALU.mult), d, f2)
            d = dve.do(lambda e, Y_=Y_: e.tensor_scalar(Y_, Y_, 0.044715, 1.0, ALU.mult, ALU.add), d)
            d = dve.do(lambda e, X_=X_, Y_=Y_: e.tensor_tensor(Y_, Y_, X_, ALU.mult), d)
            d = dve.do(lambda e, Y_=Y_: e.tensor_scalar(Y_, Y_, -50.0, None, ALU.max), d)
            d = act.do(lambda e, Y_=Y_: e.activation(Y_, Y_, ACT.Exp, scale=-2.0 * 0.7978845608028654), d)
            H_ = hid[:].rearrange("p c g n -> p (c g n)")
            d = ratio(H_, Y_, X_, d, fr, (pe.name, pe.at))
            tmp.give(i, d)
            tmp.give(i2, d)
            if kv == 0:
                b, bank, bt = PB.take()
                for ch in range(2):
                    tok = pe.do(lambda e, ch=ch, bank=bank: e.matmul(
                        bank[:, 0:64].rearrange("p (g n) -> p g n", g=2), w2[:, ch, 0:128],
                        hid[:, ch, :, 0:32], start=ch == 0, stop=ch == 1), bt, d, w2_t)
                kc_t = act.do(lambda e, bank=bank: e.copy(kcm[:], bank[:, 0:64]), tok, fr)
                PB.give(b, kc_t)
            else:
                i3, hr, f3 = tmp.take()
                for ch in range(2):
                    for g in range(2):
                        c = (2 * ch + g) * 128
                        d = dve.do(lambda e: e.tensor_copy(
                            hr[:, c:c + 128].rearrange("p (r n) -> p r n", r=4),
                            hid[:, ch, g, 0:32].unsqueeze(1).broadcast_to([128, 4, 32])), d, f3)
                for g in range(2):
                    b, bank, bt = PB.take()
                    for ch in range(2):
                        lh = hr[:, (2 * ch + g) * 128:(2 * ch + g + 1) * 128]
                        tok = pe.do(lambda e, ch=ch, lh=lh, bank=bank: e.matmul(
                            bank[:, 0:64], lh, w2[:, ch, 128:192], start=ch == 0, stop=ch == 1), bt, d, w2_t)
                    for r in range(4):
                        vc_t = act.do(lambda e, r=r, g=g, bank=bank: e.copy(
                            bd[32 * r:32 * r + 32, g, 64 * r:64 * r + 64], bank[32 * r:32 * r + 32, 0:64]), tok, bd_t)
                    PB.give(b, vc_t)
                tmp.give(i3, tok)

        fr = now()
        qq = at([128, 4, T], RA + 56 * K)
        ks = at([128, 2, T], RA + 64 * K)
        kw_ = at([128, 2, T], RA + 52 * K)
        qt_ = [roped("qa2" + s_, m, qq[:, m, :]) for m in range(4)]
        ks_t = [roped("ks" + s_, m, ks[:, m, :]) for m in range(2)]
        kw_t = [roped("ks" + s_, 2 + m, kw_[:, m, :]) for m in range(2)]
        sg = at([128, 4, 24], RA + 44 * K)
        sgt = act.do(lambda e: e.activation(sg[:], va[:, :, 384:408], ACT.Exp, scale=-1.0), fr, v_t)
        sgt = dve.do(lambda e: e.tensor_scalar(sg[:], sg[:], 1.0, None, ALU.add), sgt)
        sgs = at([128, 4, 24], RA + 77 * K + 512)
        sgt = dve.do(lambda e: e.reciprocal(sgs[:], sg[:]), sgt, fr)
        oT_free[0] = [sgt, fr]
        oa_t = []
        us = []
        obk = {}
        for qt in range(4):
            for kind in range(2):
                for h in range(8):
                    p0 = 64 * (h % 2)
                    kk, kkt = (ks, ks_t) if kind == 0 else (kw_, kw_t)
                    col = kind * 8 + h + 16 * (qt % 2)

                    def cmp_part(qt=qt):
                        ob_ = OB.take()
                        b, bank, bt = PB.take()
                        tok = None
                        for h in (0, 2, 4, 6, 1, 3, 5, 7):
                            p0 = 64 * (h % 2)
                            tok = pe.do(lambda e, h=h, p0=p0: e.matmul(
                                bank[:, h * 32:h * 32 + 32], qq[p0:p0 + 64, h // 2, qt * 128:(qt + 1) * 128],
                                kcm[p0:p0 + 64, (h // 4) * 32:(h // 4) * 32 + 32], start=True, stop=True),
                                bt, qt_[h // 2], kc_t, tok if h == 1 else None)
                        i, S, f = tmp.take()
                        S3 = S[:, 0:256].rearrange("p (h n) -> p h n", h=8)
                        mk = cn("cmpneg")[:, qt * 32:qt * 32 + 32].unsqueeze(1).broadcast_to([128, 8, 32])
                        m01 = cn("cmp01")[:, qt * 32:qt * 32 + 32].unsqueeze(1).broadcast_to([128, 8, 32])
                        d = dve.do(lambda e: e.scalar_tensor_tensor(
                            S3, bank[:, 0:256].rearrange("p (h n) -> p h n", h=8), 0.125, mk, ALU.mult, ALU.add),
                            tok, f, c_tok)
                        PB.give(b, d)
                        mx, sx = st[:, 168:176], st[:, 176 + 8 * (qt % 2):184 + 8 * (qt % 2)]
                        d = dve.do(lambda e: e.tensor_reduce(mx, S3, AX, ALU.max), d)
                        d = dve.do(lambda e: e.tensor_tensor(S3, S3, mx.unsqueeze(2).broadcast_to([128, 8, 32]),
                                                             ALU.subtract), d)
                        d = act.do(lambda e: e.activation(S[:, 0:256], S[:, 0:256], ACT.Exp), d)
                        d = dve.do(lambda e: e.tensor_reduce(sx, S3, AX, ALU.add), d)
                        d = dve.do(lambda e: e.tensor_tensor(S3, S3, m01, ALU.mult), d)
                        b, bank2, bt = PB.take()
                        for g in range(2):
                            tok = pe.do(lambda e, g=g: e.transpose(bank2[:, g * 128:(g + 1) * 128],
                                                                   S[:, g * 128:(g + 1) * 128], cn("ident")), bt, d)
                        tmp.give(i, tok)
                        ip, PT, f = tmp.take()
                        d = dve.do(lambda e: e.tensor_copy(PT[:, 0:256], bank2[:, 0:256]), tok, f)
                        PB.give(b, d)
                        for g in range(2):
                            tok = pe.do(lambda e, g=g: e.matmul(ob_[1][:, g * 256:(g + 1) * 256],
                                                                PT[:, g * 128:(g + 1) * 128], bd[:, g, :],
                                                                start=True, stop=True), d, ob_[2], vc_t)
                        tmp.give(ip, tok)
                        obk[qt] = [ob_ + (tok,)]

                    def opn(qt=qt, kind=kind, h=h, f_=cmp_part):
                        if h == 0:
                            if kind == 0:
                                f_()
                            obk[qt].append(OB.take())

                    def done(tok, qt=qt, kind=kind, h=h):
                        if h < 7:
                            return
                        obk[qt][1 + kind] = obk[qt][1 + kind] + (tok,)
                        if kind == 0:
                            return
                        c = 16 * (qt % 2)
                        rs = st[:, 192:216]
                        g3 = sgs[:, qt, :].rearrange("p (h j) -> p j h", j=3)
                        d = dve.do(lambda e: e.reciprocal(rs[:, 0:8], st[:, 176 + 8 * (qt % 2):184 + 8 * (qt % 2)]),
                                   now())
                        d = dve.do(lambda e: e.reciprocal(rs[:, 8:24], st[:, S_SM + c:S_SM + c + 16]), d)
                        d = dve.do(lambda e: e.tensor_tensor(rs.rearrange("p (j h) -> p j h", j=3),
                                                             rs.rearrange("p (j h) -> p j h", j=3), g3, ALU.mult),
                                   d, sgt)
                        i, os_, f = tmp.take()
                        i2, o2, f2 = tmp.take()
                        dd = heads8(obk[qt][0][1], rs[:, 0:8], d, f, obk[qt][0][3], out_=os_)
                        OB.give(obk[qt][0][0], dd)
                        for j in range(1, 3):
                            de = heads8(obk[qt][j][1], rs[:, 8 * j:8 * j + 8], d, f2, dve_last(), obk[qt][j][3],
                                        out_=o2)
                            OB.give(obk[qt][j][0], de)
                            dd = dve.do(lambda e: e.tensor_tensor(os_[:], os_[:], o2[:], ALU.add), de, dd)
                        tmp.give(i2, dd)
                        dst, res = split_out(oa, qt)
                        tmp.give(i, to_features(os_, 512, dst, dd))
                        oa_t.extend(res)

                    us.append(causal_units(
                        lambda h=h, qt=qt, p0=p0: qq[p0:p0 + 64, h // 2, qt * 128:(qt + 1) * 128],
                        lambda h=h, qt=qt, p0=p0, kk=kk: kk[p0:p0 + 64, h // 4, 0:(qt + 1) * 128],
                        lambda h=h, kkt=kkt: [qt_[h // 2], kkt[h // 4]],
                        lambda h=h, qt=qt, kind=kind: [va[:, j, kind * 128 + (h // 4) * 64:kind * 128 + (h // 4) * 64 + 64]
                                                       for j in range(qt + 1)],
                        lambda: v_t, None, None, h, qt, 0.125, col, open=opn, done=done,
                        o=lambda qt=qt, kind=kind, h=h: obk[qt][1 + kind][1][:, h * 64:(h + 1) * 64],
                        ot=lambda qt=qt, kind=kind: obk[qt][1 + kind][2]))
        attend(us)

        fr = now()
        mg = at([128, 2, KC, T], RA + 48 * K, F32R)
        r4 = list(range(4))
        xs = merge(mg, fr, [
            ("gate" + s_, 0, [("br2a" + s_, 0, r4)], lambda c: (oa[:, 0, c, :], oa[:, 1, c, :], oa_t)),
            ("gate" + s_, 8, [("br2b" + s_, 0, r4)], lambda c: (ob[:, 0, c, :], ob[:, 1, c, :], ob_t)),
            ("gate" + s_, 16, [("br2c" + s_, 0, r4)], lambda c: (oc[:, 0, c, :], oc[:, 1, c, :], oc_t))], H)

        def residual():
            new = []

            def post(m, bank, tok):
                d = dve.do(lambda e: e.tensor_tensor(xT[:, m, :], xT[:, m, :], bank[:], ALU.add), tok, xt[m])
                acc_tok[0], r = square_in(xT[:, m, :], m == 0, d)
                new.append([d, r])
                return [d]
            return post, new
        post, new = residual()
        down("wo2" + s_, KC, xs, post)
        xt = new
        ht = prenorm(7 + 3 * L, xt, sq=True)
        xs = ffn("f3" + s_, ht)
        post, new = residual()
        down("f3" + s_ + "_d", FC, xs, post)
        xt = new
        ht = prenorm(8 + 3 * L, xt, sq=True)
        H = hs(ht)
        fr = now()
        pf = at([128, 2, T], RA + 12 * K)
        ps = at([128, 2, 2, T], RA, F32R)
        a = load(pf[:], D["ple"][L], fr)
        p_t = [split(ps[:, 0, c, :], ps[:, 1, c, :], pf[:, c, :], a, fr) for c in range(2)]
        new = []
        for m in range(KC):
            bg, gb, tg = dense([("plg" + s_, m, 0, list(range(8)))], H)
            bo, bb_, to = dense([("plp" + s_, m, 0, [0, 1])], lambda c: (ps[:, 0, c, :], ps[:, 1, c, :], p_t[c]))
            i, s, f = tmp.take()
            d = sigmul(s[:], gb, bb_[:], tg, to, f, gate_free=lambda a, bg=bg: PB.give(bg, a))
            PB.give(bo, d)
            d = dve.do(lambda e, m=m, s=s: e.tensor_tensor(xT[:, m, :], xT[:, m, :], s[:], ALU.add), d, xt[m])
            tmp.give(i, d)
            acc_tok[0], r = square_in(xT[:, m, :], m == 0, d)
            new.append([d, r])
        xt = new

    rt = rms(DM, acc_tok[0])
    outs = []
    for c in range(KC):
        i, h, f = tmp.take()
        a = dve.do(lambda e, c=c, h=h: e.scalar_tensor_tensor(h[:], xT[:, c, :], gn[:, 12, c:c + 1], rstd[:],
                                                              ALU.mult, ALU.mult), f, rt, xt[c])
        w = dma(sp, out[c], h[:], a, sem=f"o{c}")
        tmp.give(i, w)
        outs.append(w)
    sp.need(outs)
    sp.need(rope_done)
    sp.need([("m" + str(i), dsum[f"m{i}"]) for i in range(12)])
    return units, (pe, act, dve, pool, sp), sorted(dsum)


def build(nc, D, out):
    D = dict(D)
    D["rope"] = nc.dram_tensor("rope_scratch", [4, 128, T], F32).ap()
    D["rpbs"] = nc.dram_tensor("rpb_scratch", [120 * 8128], F32)
    seq = program(nc, None, D, out)[0]
    with ExitStack() as ctx:
        _, queues, names = program(nc, seq, D, out)
        pe, act, dve, pool, sp = queues
        sems = {n: ctx.enter_context(nc.semaphore("s_" + n)) for n in ["pe", "act", "dve", "pool"] + names}
        block = ctx.enter_context(nc.Block())

        @block.sync
        def _(eng):
            sp.play(eng, sems)

        @block.gpsimd
        def _(eng):
            pool.play(eng, sems)

        @block.scalar
        def _(eng):
            act.play(eng, sems)

        @block.vector
        def _(eng):
            dve.play(eng, sems)

        @block.tensor
        def _(eng):
            pe.play(eng, sems)


def _fm(w, cols=None):
    w = w if cols is None else w[:, cols]
    k, m = w.shape
    return np.ascontiguousarray(w.reshape(k // 128, 128, m // 128, 128).transpose(2, 1, 0, 3)).reshape(m // 128, 128, k)


def _tf(w):
    k, n = w.shape
    return np.ascontiguousarray(w.reshape(k // 128, 128, n).transpose(1, 0, 2)).reshape(1, 128, -1)


def _dup(w):
    return _fm(np.concatenate([w[:, 0:64], w[:, 0:64], w[:, 64:128], w[:, 64:128]], axis=1))


def _rows(x):
    t, n = x.shape
    return np.ascontiguousarray(x.T.reshape(n // 128, 128, t).transpose(1, 0, 2))


def _constants():
    c = np.zeros((128, NCONST), np.float32)

    def put(name, a):
        o_, w = CONST[name]
        c[0:a.shape[0], o_:o_ + a.shape[1]] = a
    p = np.arange(128)
    put("ident", np.eye(128, dtype=np.float32))
    swap = np.where(p % 64 < 32, p + 32, p - 32)
    put("perm", (p[:, None] == swap[None, :]).astype(np.float32))
    q = np.arange(96)
    sw = np.where(q < 80, q + 16, q - 16)
    put("permc", ((q[:, None] == sw[None, :]) & (q[None, :] >= 64)).astype(np.float32))
    col = np.arange(64)
    c0 = np.clip(p % 64 - 8, 0, 48)
    ok = (col[None, :] >= c0[:, None]) & (col[None, :] < c0[:, None] + 16)
    put("colmask", np.where(ok, 0.0, NEG).astype(np.float32))
    n = np.arange(32)
    end = np.where(n < 31, n * 16 + 31, 10 ** 6)
    tq = np.arange(4)[None, :, None] * 128 + p[:, None, None]
    okc = (end[None, None, :] <= tq).reshape(128, 128)
    put("cmpneg", np.where(okc, 0.0, NEG).astype(np.float32))
    put("cmp01", okc.astype(np.float32))
    sel = np.zeros((4, 2, 128), np.float32)
    for ch in range(2):
        for i in range(128):
            sel[2 * ch + i // 64, ch, i] = 1.0
    put("sel", sel.reshape(4, 256))
    f = np.float32
    i64 = np.power(f(10000.0), -np.arange(0, 64, 2, dtype=f) / f(64)).astype(f)
    i32 = np.power(f(10000.0), -np.arange(0, 32, 2, dtype=f) / f(32)).astype(f)
    put("invf", np.stack([i64[p % 32], np.where((p >= 64) & (p < 96), i32[p % 16], f(0))], 1).astype(f))
    put("sgn", np.stack([np.where(p % 64 < 32, -1.0, 1.0), np.where(p % 32 < 16, -1.0, 1.0)], 1).astype(f))
    ca = np.zeros((128, 512), f)
    ca[:, 384:] = np.where(p[None, :] <= p[:, None], 0.0, NEG)
    put("causal", ca)
    kj = np.arange(256) - 128
    okb = (kj[None, :] <= p[:, None]) & (kj[None, :] > p[:, None] - 128)
    put("band", np.where(okb, 0.0, NEG).astype(f))
    slopes = np.exp2(f(-8.0) * (np.arange(12, dtype=f) + f(1)) / f(12)).astype(f)
    dil = np.zeros((128, 4, 640), f)
    for hh in range(4):
        r = np.abs(np.arange(384)[None, :] - 128 - p[:, None])
        dil[:, hh, 0:384] = np.where(r <= 64, -slopes[hh] * r.astype(f) * f(8), NEG)
        r = np.abs(p[None, :] - p[:, None])
        dil[:, hh, 384:512] = np.where(r <= 64, -slopes[4 + hh] * (4 * r).astype(f) * f(8), NEG)
        dil[:, hh, 512:640] = np.where(r % 4 == 0, -slopes[8 + hh] * (4 * r).astype(f) * f(8), NEG)
    return c, dil


def kernel(**inputs):
    import concourse.bacc as bacc
    from concourse.bass_utils import run_bass_kernel_spmd

    I = {k: np.asarray(v) for k, v in inputs.items()}
    A = {}
    A["xT"] = _rows(I["x"][0])
    A["const"], A["dil"] = _constants()
    gains = [I["ffn1_pre_g"][0], I["ffn1_post_g"][0], I["mix_pre_g"][0], I["mix_post_g"][0], I["ffn2_pre_g"][0],
             I["ffn2_post_g"][0]]
    for l in range(2):
        gains += [I["mix_norm_2"][l], I["ffn_norm_2"][l], I["ple_norm_2"][l]]
    gains.append(I["final_norm_2"])
    A["gains"] = np.ascontiguousarray(np.stack(gains).reshape(len(GAINS), KC, 128).transpose(2, 0, 1))
    cg = np.concatenate([np.concatenate([I["c_q_norm_2"][l], I["c_kv_norm_2"][l]]) for l in range(2)])
    A["cgains"] = np.ascontiguousarray(cg.reshape(8, 128).T)
    A["positions"] = np.ascontiguousarray(I["positions_2"])
    A["rpb"] = np.ascontiguousarray(I["na_rpb"][0].reshape(120, 31))
    A["sinks"] = np.ascontiguousarray(np.broadcast_to(I["b_sinks_2"][:, None, :], (2, 128, 8)))
    for n, p in (("f1", "ffn1"), ("f2", "ffn2")):
        A[n + "_g"], A[n + "_u"], A[n + "_d"] = (_fm(I[f"{p}_w_{k}"][0]) for k in ("gate", "up", "down"))
    w = I["w_in"][0]
    A["qka"] = _fm(w[:, 0:1024])
    A["va"] = _tf(w[:, 1024:1536])
    A["qb"] = _fm(w[:, 1536:2304])
    A["kb"] = _fm(w[:, 2304:3072])
    for g in range(3):
        A[f"vb{g}"] = _tf(w[:, 3072 + 256 * g:3328 + 256 * g])
    A["ga"] = _fm(w[:, 3840:4864])
    A["gb"] = _fm(w[:, 4864:5888])
    A["bra"], A["brb"], A["wo"] = _fm(I["w_branch_a"][0]), _fm(I["w_branch_b"][0]), _fm(I["w_out"][0])
    for l in range(2):
        s = str(l)
        w = I["w_in_2"][l]
        A["clat" + s] = _fm(w[:, 2072:2584])
        kpe = np.concatenate([np.zeros((DM, 64), np.float32), w[:, 2584:2616]], 1)
        A["kpe" + s] = _tf(kpe)
        up = I["c_w_q_up_2"][l].reshape(2, 128, 8, 96)
        kv = I["c_w_kv_up_2"][l].reshape(2, 128, 8, 128)
        hq = up.transpose(2, 1, 0, 3).reshape(8, 128, 192)
        hk = kv[..., 0:64].transpose(2, 1, 0, 3).reshape(8, 128, 128)
        hh = np.concatenate([hq, hk], 2).reshape(4, 2, 128, 320).transpose(0, 2, 1, 3)
        A["cup" + s] = np.ascontiguousarray(hh).reshape(4, 128, 640)
        A["cv" + s] = np.ascontiguousarray(kv[..., 64:128].transpose(1, 0, 2, 3)).reshape(1, 128, 1024)
        A["v2" + s] = _tf(np.concatenate([w[:, 896:1024], w[:, 1152:1280], w[:, 1944:2072], w[:, 1280:1304]], 1))
        A["qb2" + s] = _fm(w[:, 1304:1816])
        A["kb2" + s] = _dup(w[:, 1816:1944])
        A["kc" + s] = np.concatenate([_dup(w[:, 512:640]), _dup(w[:, 640:768])])
        A["qa2" + s] = _fm(w[:, 0:512])
        A["ks" + s] = np.concatenate([_dup(w[:, 768:896]), _dup(w[:, 1024:1152])])
        A["cw1" + s] = np.concatenate([_tf(I["a_cmp_w1_k_2"][l]), _tf(I["a_cmp_w1_v_2"][l])])
        A["gate" + s] = _fm(I["w_branch_gate_2"][l])
        for b in "abc":
            A["br2" + b + s] = _fm(I[f"w_branch_{b}_2"][l])
        A["wo2" + s] = _fm(I["w_out_2"][l])
        for a, b in (("_g", "gate"), ("_u", "up"), ("_d", "down")):
            A["f3" + s + a] = _fm(I[f"w_ffn_{b}_2"][l])
        A["plg" + s] = _fm(I["w_ple_gate_2"][l])
        A["plp" + s] = _fm(I["w_ple_proj_2"][l])
    w2 = []
    for l in range(2):
        k = I["a_cmp_w2_k_2"][l].reshape(2, 128, 64)
        v = I["a_cmp_w2_v_2"][l].reshape(2, 128, 64)
        w2.append(np.concatenate([k, k, v], 2).transpose(1, 0, 2))
    A["w2"] = np.ascontiguousarray(np.stack(w2))
    pos = np.stack([I["a_cmp_pos_k_2"], I["a_cmp_pos_v_2"]], 1).transpose(0, 3, 1, 2)
    A["cpos"] = np.ascontiguousarray(np.concatenate([pos, pos], 1))
    A["ple"] = np.stack([_rows(I["p_2"][l, 0]) for l in range(2)])

    nc = bacc.Bacc("TRN2", target_bir_lowering=False, num_devices=1)
    D = {n: nc.dram_tensor("in_" + n, a.shape, mybir.dt.from_np(a.dtype), kind="ExternalInput").ap()
         for n, a in A.items()}
    out = nc.dram_tensor("out_0", (KC, 128, T), F32, kind="ExternalOutput").ap()
    build(nc, D, out)
    r = run_bass_kernel_spmd(nc, [{"in_" + n: a for n, a in A.items()}], core_ids=[0])
    y = r.results[0]["out_0"]
    return np.ascontiguousarray(y.reshape(DM, T).T).reshape(1, T, DM)
```

```python
from contextlib import ExitStack

import numpy as np

import concourse.bass as bass
from concourse import mybir

F32 = mybir.dt.float32
F32R = mybir.dt.float32r
I32 = mybir.dt.int32
ALU = mybir.AluOpType
ACT = mybir.ActivationFunctionType
AX = mybir.AxisListType.X

T = 512
DM = 1024
KC = 8
FF = 2816
FC = 22
EPS = 1e-6
NEG = -1e30
BIG = 3e38
BASE = 16512
K = 1024

GAINS = ["ffn1_pre", "ffn1_post", "mix_pre", "mix_post", "ffn2_pre", "ffn2_post",
         "mix2_0", "ffn_0", "ple_0", "mix2_1", "ffn_1", "ple_1", "final"]
CONST = {}
_at = 0
for _n, _w in (("ident", 128), ("perm", 128), ("permc", 96), ("colmask", 64), ("cmpneg", 128),
               ("cmp01", 128), ("sel", 256), ("invf", 2), ("sgn", 2), ("causal", 512), ("band", 256)):
    CONST[_n] = (_at, _w)
    _at += _w
NCONST = _at


class Noted:

    def matmul(self, *a, **k):
        return lambda e: e.matmul(*a, **k)

    def transpose(self, *a, **k):
        return lambda e: e.transpose(*a, **k)

    def activation(self, *a, **k):
        return lambda e: e.activation(*a, **k)

    def copy(self, *a, **k):
        return lambda e: e.copy(*a, **k)

    def tensor_copy(self, *a, **k):
        return lambda e: e.tensor_copy(*a, **k)

    def tensor_tensor(self, *a, **k):
        return lambda e: e.tensor_tensor(*a, **k)

    def tensor_scalar(self, *a, **k):
        return lambda e: e.tensor_scalar(*a, **k)

    def scalar_tensor_tensor(self, *a, **k):
        return lambda e: e.scalar_tensor_tensor(*a, **k)

    def tensor_tensor_reduce(self, *a, **k):
        return lambda e: e.tensor_tensor_reduce(*a, **k)

    def tensor_reduce(self, *a, **k):
        return lambda e: e.tensor_reduce(*a, **k)

    def reciprocal(self, *a, **k):
        return lambda e: e.reciprocal(*a, **k)

    def memset(self, *a, **k):
        return lambda e: e.memset(*a, **k)

    def dma_start(self, *a, **k):
        return lambda e: e.dma_start(*a, **k)


NOTED = Noted()


class Queue:

    def __init__(self, name):
        self.name = name
        self.items = []
        self.at = 0
        self.met = {}

    def need(self, toks):
        for tok in toks:
            if tok is None:
                continue
            if isinstance(tok, list):
                self.need(tok)
                continue
            s, v = tok
            if self.met.get(s, 0) < v:
                self.met[s] = v
                self.items.append(("wait", s, v))

    def do(self, fn, *toks, mark=True):
        self.need(toks)
        self.items.append(("do", fn(NOTED), (self.name, 1) if mark else None))
        if mark:
            self.at += 1
            return (self.name, self.at)
        return None

    def dma(self, fn, sem, total, *toks):
        self.need(toks)
        self.items.append(("do", fn(NOTED), (sem, 16)))
        return (sem, total)

    def play(self, eng, sems):
        for it in self.items:
            if it[0] == "wait":
                eng.wait_ge(sems[it[1]], it[2])
            else:
                ins = it[1](eng)
                if it[2] is not None:
                    ins.then_inc(sems[it[2][0]], it[2][1])


class Ring:

    def __init__(self, bufs):
        self.bufs = bufs
        self.last = [None] * len(bufs)
        self.n = 0
        self.out = set()

    def take(self):
        i = self.n % len(self.bufs)
        self.n += 1
        assert i not in self.out
        self.out.add(i)
        return i, self.bufs[i], self.last[i]

    def give(self, i, *toks):
        self.last[i] = list(toks)
        self.out.remove(i)


def program(nc, seq, D, out):
    pe, act, dve, pool, sp = (Queue(n) for n in ("pe", "act", "dve", "pool", "sp"))
    dsum = {}

    def dma(q, dst, src, *toks, sem="misc"):
        dsum[sem] = dsum.get(sem, 0) + 16
        return q.dma(lambda e: e.dma_start(dst, src), sem, dsum[sem], *toks)

    nmisc = [0]

    def load(dst, src, *toks):
        nmisc[0] += 1
        return dma(pool, dst, src, *toks, sem=f"m{nmisc[0] % 12}")

    def now():
        return [(q.name, q.at) for q in (pe, act, dve, pool) if q.at]

    names = [0]

    def at(shape, off, dt=F32):
        names[0] += 1
        return nc.alloc_sbuf_tensor_at(f"t{names[0]}_{'s' if seq is None else 'r'}", shape, dt,
                                       offset=BASE + off)

    RA = 92 * K
    MI = RA + 88 * K
    xT = at([128, KC, T], 0)
    hT = at([128, 2, KC, T], 16 * K, F32R)
    fT = at([128, KC, T], 16 * K)
    raw = [at([128, 1024], (48 + 4 * i) * K) for i in range(3)]
    spl = [at([128, 2, 1024], (60 + 8 * i) * K, F32R) for i in range(4)]
    con = at([128, NCONST], MI)
    o = MI + (NCONST * 4 + 31) // 32 * 32
    gn = at([128, len(GAINS), KC], o)
    gcn = at([128, 8], o + 416)
    gh = at([128, 2, KC], o + 448)
    ones = at([128, 128], o + 512)
    acc = at([128, T], o + 1024)
    rstd = at([128, T], o + 3 * K)
    st = at([128, 256], o + 5 * K)
    tmp = Ring([at([128, T], o + (6 + 2 * i) * K) for i in range(6)])
    assert o + 20 * K + BASE <= 229368
    Sr = Ring([at([128, T], RA + (78 + 2 * i) * K) for i in range(3)] + [at([128, T], o + 18 * K)])
    PTr = Ring([at([128, T], RA + (84 + 2 * i) * K) for i in range(2)])
    banks = [nc.alloc_psum_tensor(f"bk{i}_{'s' if seq is None else 'r'}", [128, T], F32)
             for i in range(8)] if seq is not None else [None] * 8
    if seq is None:
        banks = [xT[:, i, :] for i in range(8)]
    PB = Ring(banks[0:4])
    OB = Ring(banks[4:8])

    def cn(name):
        a, w = CONST[name]
        return con[:, a:a + w]

    c_tok = dma(sp, con[:], D["const"], sem="c")
    g_tok = dma(sp, gn[:], D["gains"], sem="c")
    g_tok2 = dma(sp, gcn[:], D["cgains"], sem="c")
    x_tok = dma(sp, xT[:], D["xT"], sem="c")
    c_tok = g_tok = g_tok2 = x_tok = ("c", 64)
    one_tok = dve.do(lambda e: e.memset(ones[:], 1.0))
    half = st[:, 228:232]
    half_tok = dve.do(lambda e: e.memset(half, -0.5))
    gh_tok = [dve.do(lambda e, i=i, j=j: e.tensor_scalar(gh[:, i, :], gn[:, j, :], 0.5, None, ALU.mult),
                     g_tok) for i, j in ((0, 1), (1, 5))]

    units = []
    loaded, parted = [], []
    freed = {}
    AHEAD = 2

    def stream(u):
        if seq is None:
            return
        while len(loaded) <= min(u + AHEAD + 2, len(seq) - 1):
            i = len(loaded)
            if i >= 3 and len(parted) <= i - 3:
                part(i - 3)
            name, m, c0, n = seq[i]
            src = D[name][m, :, c0:c0 + n]
            w = parted[i - 3] if i >= 3 else None
            loaded.append(dma(sp, raw[i % 3][:, 0:n], src, w, sem=f"w{i % 3}"))
        while len(parted) <= min(u + AHEAD, len(seq) - 1):
            part(len(parted))

    def part(i):
        n = seq[i][3]
        hi = spl[i % 4][:, 0, 0:n]
        lo = spl[i % 4][:, 1, 0:n]
        r = raw[i % 3][:, 0:n]
        f = freed[i - 4] if i >= 4 else None
        a = act.do(lambda e: e.copy(hi, r), loaded[i], f)
        b = dve.do(lambda e: e.tensor_tensor(lo, r, hi.bitcast(F32), ALU.subtract), a, loaded[i], f)
        parted.append([a, b])

    def unit(name, m, c0, n):
        u = len(units)
        units.append((name, m, c0, n))
        stream(u)
        return u, spl[u % 4][:, 0, 0:n], spl[u % 4][:, 1, 0:n], (parted[u] if seq is not None else None)

    def mm3(o_, wh, wl, xh, xl, start, stop, *toks):
        pe.do(lambda e: e.matmul(o_, wh, xh, start=start, stop=False), *toks, mark=False)
        pe.do(lambda e: e.matmul(o_, wh, xl, start=False, stop=False), mark=False)
        return lambda mark: pe.do(lambda e: e.matmul(o_, wl, xh, start=False, stop=stop), mark=mark)

    def dense(parts, xs, M=128):
        b, bank, bt = PB.take()
        for i, (name, m, c0, chunks) in enumerate(parts):
            u, wh, wl, wt = unit(name, m, c0, len(chunks) * M)
            for j, c in enumerate(chunks):
                xh, xl, xt = xs(c)
                last = j == len(chunks) - 1
                tok = mm3(bank[0:M, :], wh[:, j * M:(j + 1) * M], wl[:, j * M:(j + 1) * M], xh, xl,
                          i == 0 and j == 0, last and i == len(parts) - 1, wt, xt, bt)(last)
            freed[u] = tok
        return b, bank, tok

    def split(hi, lo, src, *toks):
        a = act.do(lambda e: e.copy(hi, src), *toks)
        b = dve.do(lambda e: e.tensor_tensor(lo, src, hi.bitcast(F32), ALU.subtract), a, *toks)
        return [a, b]

    acc_free = [None]
    rstd_free = [None]

    def square_in(src, first, *toks):
        if first:
            t = act.do(lambda e: e.activation(acc[:], src, ACT.Square), acc_free[0], *toks)
            return t, t
        i, q, f = tmp.take()
        a = act.do(lambda e: e.activation(q[:], src, ACT.Square), f, *toks)
        d = pool.do(lambda e: e.tensor_tensor(acc[:], acc[:], q[:], ALU.add), a, acc_tok[0])
        tmp.give(i, d)
        return d, a

    acc_tok = [None]

    def rms(width, tok):
        b, bank, bt = PB.take()
        for c in range(4):
            t = pe.do(lambda e: e.matmul(bank[:, c:c + 1], acc[:, c * 128:(c + 1) * 128], ones[:, 0:1],
                                         start=True, stop=True), bt, tok, one_tok, mark=c == 3)
        acc_free[0] = t
        v = st[:, 224:228]
        a = dve.do(lambda e: e.tensor_scalar(v, bank[:, 0:4], 1.0 / width, EPS, ALU.mult, ALU.add),
                   t, rstd_free[0])
        PB.give(b, a)
        a = pool.do(lambda e: e.tensor_tensor(v, v, half, ALU.pow), a, half_tok)
        b, bank, bt = PB.take()
        i, dg, f = tmp.take()
        for c in range(4):
            d = dve.do(lambda e: e.tensor_scalar(dg[:, c * 128:(c + 1) * 128], cn("ident"), v[:, c:c + 1], None,
                                                 ALU.mult), a, f, c_tok)
            t = pe.do(lambda e: e.matmul(bank[:, c * 128:(c + 1) * 128], ones[:], dg[:, c * 128:(c + 1) * 128],
                                         start=True, stop=True), d, bt, mark=c == 3)
        tmp.give(i, t)
        d = act.do(lambda e: e.copy(rstd[:], bank[:]), t, rstd_free[0])
        PB.give(b, d)
        return d

    def sumsq(srcs, toks):
        reads = []
        for c, s in enumerate(srcs):
            acc_tok[0], r = square_in(s, c == 0, toks[c])
            reads.append(r)
        return reads

    def scaled(srcs, dst, gain, rt, toks, *free):
        res = []
        for c, s in enumerate(srcs):
            i, h, f = tmp.take()
            g = gain(c)
            a = dve.do(lambda e, h=h, s=s, g=g: e.scalar_tensor_tensor(h[:], s, g, rstd[:], ALU.mult, ALU.mult),
                       f, rt, toks[c], g_tok)
            w = split(dst(0, c), dst(1, c), h[:], a, *free)
            tmp.give(i, *w)
            res.append(w)
        rstd_free[0] = dve_last()
        return res

    def dve_last():
        return (dve.name, dve.at)

    def prenorm(gi, xt, sq=None):
        if sq is None:
            sumsq([xT[:, c, :] for c in range(KC)], xt)
        rt = rms(DM, acc_tok[0])
        free = now()
        return scaled([xT[:, c, :] for c in range(KC)], lambda p, c: hT[:, p, c, :],
                      lambda c: gn[:, gi, c:c + 1], rt, xt, free)

    def hs(toks):
        return lambda c: (hT[:, 0, c, :], hT[:, 1, c, :], toks[c])

    def sigmul(dst, gbank, other, gtok, *toks, gate_free):
        i, e1, f = tmp.take()
        a = act.do(lambda e: e.activation(e1[:], gbank[:], ACT.Tanh, scale=0.5), gtok, f)
        gate_free(a)
        d = dve.do(lambda e: e.scalar_tensor_tensor(dst, e1[:], 1.0, other, ALU.add, ALU.mult), a, *toks)
        tmp.give(i, d)
        return d

    def down(name, nk, xs, post, each=None):
        for m in range(KC):
            parts = [(name, m, c0 * 128, list(range(c0, min(c0 + 8, nk)))) for c0 in range(0, nk, 8)]
            b, bank, tok = dense(parts, xs)
            PB.give(b, *post(m, bank, tok))

    def add_post(free):
        ft = []

        def post(m, bank, tok):
            a = act.do(lambda e: e.copy(fT[:, m, :], bank[:]), tok, free)
            acc_tok[0], r = square_in(fT[:, m, :], m == 0, a)
            ft.append(a)
            return [a]
        return post, ft

    def postnorm(gain, ft, xt):
        rt = rms(DM, acc_tok[0])
        new = []
        for c in range(KC):
            i, h, f = tmp.take()
            a = dve.do(lambda e, c=c, h=h: e.scalar_tensor_tensor(h[:], fT[:, c, :], gain(c), rstd[:],
                                                                 ALU.mult, ALU.mult), f, rt, ft[c], g_tok, gh_tok)
            b = dve.do(lambda e, c=c, h=h: e.tensor_tensor(xT[:, c, :], xT[:, c, :], h[:], ALU.add), a, xt[c])
            tmp.give(i, b)
            acc_tok[0], r = square_in(xT[:, c, :], c == 0, b)
            new.append([b, r])
        rstd_free[0] = dve_last()
        return new

    def ffn(name, ht, hook=None):
        free = now()
        hid = at([128, 2, FC, T], RA, F32R)
        toks = []
        for j in range(FC):
            bg, g, tg = dense([(name + "_g", j, 0, list(range(8)))], hs(ht))
            bu, u_, tu = dense([(name + "_u", j, 0, list(range(8)))], hs(ht))
            i, s, f = tmp.take()
            ie, e1, fe = tmp.take()
            a = act.do(lambda e, g=g, e1=e1: e.activation(e1[:], g[:], ACT.Tanh, scale=0.5), tg, fe)
            d = dve.do(lambda e: e.scalar_tensor_tensor(s[:], e1[:], 1.0, g[:], ALU.add, ALU.mult), a, f)
            PB.give(bg, d)
            tmp.give(ie, d)
            d = dve.do(lambda e: e.scalar_tensor_tensor(s[:], s[:], 0.5, u_[:], ALU.mult, ALU.mult), d, tu)
            PB.give(bu, d)
            w = split(hid[:, 0, j, :], hid[:, 1, j, :], s[:], d, free, rope_done if j >= 10 else None)
            tmp.give(i, *w)
            toks.append(w)
            if hook is not None and j == 1:
                hook()
        return lambda c: (hid[:, 0, c, :], hid[:, 1, c, :], toks[c])

    flip = [0]

    def attend(us):
        n = len(us)
        st_ = [dict() for _ in us]
        for s in range(n + 4):
            if s < n:
                X = st_[s]
                for U in us[s]:
                    if U.get("pre"):
                        U["pre"]()
                b, bank, bt = PB.take()
                i, S, f = Sr.take()
                o_ = 0
                for U in us[s]:
                    U["at"] = o_
                    q, k, w = U["q"](), U["k"](), U["w"]
                    t = pe.do(lambda e: e.matmul(bank[:, o_:o_ + w], q, k, start=True, stop=True),
                              bt, U["qk"](), mark=U is us[s][-1])
                    o_ += w
                for U in us[s]:
                    if U.get("after"):
                        U["after"](t)
                assert o_ <= 512
                X.update(S=S, i=i, w=o_)
                ds, es = [], []
                for U in us[s]:
                    c, w = U["at"], U["w"]
                    ds.append(dve.do(lambda e: e.tensor_tensor_reduce(
                        S[:, c:c + w], bank[:, c:c + w], U["table"], -U["scale"], U.get("init", BIG),
                        ALU.add, ALU.min, U["nm"]), t, f, U.get("tt")))
                PB.give(b, ds[-1])
                for U, d in zip(us[s], ds):
                    c, w = U["at"], U["w"]
                    es.append(act.do(lambda e: e.activation(
                        S[:, c:c + w], S[:, c:c + w], ACT.Exp, bias=U["nm"], scale=-1.0, accum_out=U["sm"]), d))
                X["es"] = es
                if us[s][0].get("extra"):
                    X["x"] = us[s][0]["extra"](us[s], es, ds)
            if 0 <= s - 1 < n:
                X, B = st_[s - 1], us[s - 1]
                S, w, nh = X["S"], X["w"], len(B)
                sm_, rs_ = B[0]["sms"](nh), B[0]["rss"](nh)
                d = dve.do(lambda e: e.reciprocal(rs_, sm_), X["es"], X.get("x"), B[0].get("rst"))
                if B[0].get("gate"):
                    g_, gt = B[0]["gate"](nh)
                    d = dve.do(lambda e: e.tensor_tensor(rs_, rs_, g_, ALU.mult), d, gt)
                X["p"] = dve.do(lambda e: e.tensor_tensor(
                    S[:, 0:w].rearrange("p (h k) -> p h k", h=nh), S[:, 0:w].rearrange("p (h k) -> p h k", h=nh),
                    rs_.unsqueeze(2).broadcast_to([128, nh, w // nh]), ALU.mult), d)
            if 0 <= s - 3 < n:
                X = st_[s - 3]
                w, S = X["w"], X["S"]
                b, bank, bt = PB.take()
                for j in range(w // 128):
                    t = pe.do(lambda e: e.transpose(
                        bank[:, j * 128:(j + 1) * 128], S[:, j * 128:(j + 1) * 128], cn("ident")),
                        bt, X["p"], c_tok, mark=j == w // 128 - 1)
                Sr.give(X["i"], t)
                i, PT, f = PTr.take()
                d = act.do(lambda e: e.copy(PT[:, 0:w], bank[:, 0:w]), t, f)
                PB.give(b, d)
                X.update(PT=PT, pi=i, p=d)
            if 0 <= s - 4 < n:
                X = st_[s - 4]
                for U in us[s - 4]:
                    if U.get("open"):
                        U["open"]()
                    vs, o_ = U["v"](), U["o"]()
                    add = U.get("add", False)
                    for j, v in enumerate(vs):
                        c = U["at"] + j * 128
                        t = pe.do(lambda e: e.matmul(o_, v, X["PT"][:, c:c + 128], start=j == 0 and not add,
                                                     stop=j == len(vs) - 1, skip_group_check=add),
                                  X["p"], U["vt"](), U["ot"](), mark=j == len(vs) - 1)
                    U["t"] = t
                PTr.give(X["pi"], t)
                for U in us[s - 4]:
                    if U.get("done"):
                        U["done"](U["t"])

    def batches(us):
        res = []
        for U in us:
            L_ = res[-1][-1] if res else None
            if res and (U["row"], U["w"]) == (L_["row"], L_["w"]) and (len(res[-1]) + 1) * U["w"] <= 512:
                res[-1].append(U)
            else:
                res.append([U])
        return res

    def split_out(oT, bank, qt, *toks):
        return split(oT[:, 0, :, qt * 128:(qt + 1) * 128], oT[:, 1, :, qt * 128:(qt + 1) * 128],
                     bank[:].rearrange("p (c t) -> p c t", c=4), oT_free[0], *toks)

    def head_out(bank, h):
        return bank[64 * (h % 2):64 * (h % 2) + 64, (h // 2) * 128:(h // 2) * 128 + 128]

    def columns(base, h, step):
        return lambda n: st[:, base + h:base + h + step * (n - 1) + 1:step]

    oT_free = [None]
    S_NM, S_SM, S_RS = 0, 32, 64
    nm = lambda i: st[:, S_NM + i:S_NM + i + 1]
    sm = lambda i: st[:, S_SM + i:S_SM + i + 1]

    def project(name, m, xs, dst, *free, view=lambda a: a, M=128):
        b, bank, tok = dense([(name, m, 0, list(range(8)))], xs, M)
        d = act.do(lambda e: e.copy(dst, view(bank[0:M, :])), tok, *free)
        PB.give(b, d)
        return d

    def tokens_first(name, ncol, per, xs, dst, *free, toks_of=None, nk=8):
        if toks_of is None:
            toks_of = lambda a, t: a[:, t * 128:(t + 1) * 128]
        bs = [OB.take() for _ in range(4)]
        for k0 in range(0, nk, per):
            u, wh, wl, wt = unit(name, 0, k0 * ncol, per * ncol)
            for j in range(per):
                xh, xl, xt = xs(k0 + j)
                for t in range(4):
                    last = j == per - 1 and t == 3
                    o_ = bs[t][1][:, 0:ncol]
                    s, e_ = k0 + j == 0, k0 + j == nk - 1
                    a, b_ = wh[:, j * ncol:(j + 1) * ncol], wl[:, j * ncol:(j + 1) * ncol]
                    hh, hl = toks_of(xh, t), toks_of(xl, t)
                    pe.do(lambda e, o_=o_, hh=hh, a=a, s=s: e.matmul(o_, hh, a, start=s, stop=False),
                          wt, xt, bs[t][2], mark=False)
                    pe.do(lambda e, o_=o_, hh=hh, b_=b_: e.matmul(o_, hh, b_, start=False, stop=False), mark=False)
                    tok = pe.do(lambda e, o_=o_, hl=hl, a=a, e_=e_: e.matmul(o_, hl, a, start=False, stop=e_))
                    if e_:
                        d = act.do(lambda e, t=t, o_=o_: e.copy(dst(t), o_), tok, *free)
                        OB.give(bs[t][0], d)
            freed[u] = tok
        return d

    xt = [x_tok] * KC
    ht = prenorm(0, xt)

    rope_done = []

    rope_tok = []

    def rope_tables():
        pi_ = at([128, T], RA + 64 * K, I32)
        pf = at([128, T], RA + 66 * K)
        ang = at([128, T], RA + 68 * K)
        y = at([128, T], RA + 70 * K)
        ki = at([128, T], RA + 72 * K, I32)
        kf = at([128, T], RA + 74 * K)
        r = [at([128, T], RA + (76 + 2 * i) * K) for i in range(4)]
        a = load(pi_[:], D["positions"].partition_broadcast(128), now())
        a = dve.do(lambda e: e.tensor_copy(pf[:], pi_[:]), a)
        prev = None
        for w in range(2):
            ang_t = dve.do(lambda e, w=w: e.tensor_scalar(ang[:], pf[:], cn("invf")[:, w:w + 1], None, ALU.mult),
                           a, c_tok, prev)
            for j, (frac, ph) in enumerate(((0.25, float(np.pi / 2)), (0.0, 0.0))):
                d = r[2 * w + j]
                x = dve.do(lambda e, frac=frac: e.tensor_scalar(y[:], ang[:], float(1 / (2 * np.pi)), frac,
                                                               ALU.mult, ALU.add), ang_t, dve_last())
                x = dve.do(lambda e: e.tensor_copy(ki[:], y[:]), x)
                x = dve.do(lambda e: e.tensor_copy(kf[:], ki[:]), x)
                c1, c2, c3 = 6.28125, 0.0019340515136718750, float(2 * np.pi - 6.28125 - 0.0019340515136718750)
                x = dve.do(lambda e: e.scalar_tensor_tensor(y[:], kf[:], -c1, ang[:], ALU.mult, ALU.add), x)
                x = dve.do(lambda e: e.scalar_tensor_tensor(y[:], kf[:], -c2, y[:], ALU.mult, ALU.add), x)
                x = dve.do(lambda e: e.scalar_tensor_tensor(y[:], kf[:], -c3, y[:], ALU.mult, ALU.add), x)
                x = dve.do(lambda e, ph=ph: e.tensor_scalar(y[:], y[:], ph, 3.1415925, ALU.add, ALU.min), x)
                x = dve.do(lambda e: e.tensor_scalar(y[:], y[:], -3.1415925, None, ALU.max), x)
                x = act.do(lambda e, d=d: e.activation(d[:], y[:], ACT.Sin), x)
                if j == 1:
                    x = dve.do(lambda e, d=d, w=w: e.tensor_scalar(d[:], d[:], cn("sgn")[:, w:w + 1], None,
                                                                   ALU.mult), x)
                elif w == 1:
                    x = dve.do(lambda e, d=d: e.memset(d[0:64, :], 1.0), x)
                prev = x
                dve.need([x])
                rope_tok.append(load(D["rope"][2 * w + j], d[:], x))
                rope_done.append(rope_tok[-1])

    xs = ffn("f1", ht, hook=rope_tables)
    post, ft = add_post(now())
    down("f1_d", FC, xs, post)
    xt = postnorm(lambda c: gh[:, 0, c:c + 1], ft, xt)
    ht = prenorm(2, xt, sq=True)

    H = hs(ht)
    fr = now()
    oa = at([128, 2, 4, T], RA, F32R)
    qa = at([128, 4, T], RA + 16 * K)
    ka = at([128, 4, T], RA + 24 * K)
    va = at([128, 4, T], RA + 32 * K)
    rp = at([120, 127], RA + 60 * K)
    BT = Ring([at([128, 14, 64], RA + 40 * K + i * 3584) for i in range(2)])
    z = dve.do(lambda e: e.memset(rp[:], 0.0), fr, rope_done)
    z = load(rp[:, 48:79], D["rpb"], z)
    z = load(D["rpbs"].ap().rearrange("(a c b) -> a c b", b=127, c=64),
             rp[:].unsqueeze(1).broadcast_to([120, 64, 127]), z)
    qt_, kt_ = [], []
    for m in range(4):
        qt_.append(project("qka", m, H, qa[:, m, :], fr))
    for m in range(4):
        kt_.append(project("qka", 4 + m, H, ka[:, m, :], fr))
    v_t = tokens_first("va", 512, 2, H, lambda t: va[:, t, :], fr)
    ob4 = {}
    bt_ = {}

    def na_table(h):
        i, bt, f = BT.take()
        w = None
        for a in range(2):
            src = bass.AP(D["rpbs"], (h * 15 + (1 - a)) * 8128 + 63, [[126, 64], [8128, 14], [1, 64]])
            w = load(bt[64 * a:64 * a + 64, :, :], src, z, f, w)
        d = dve.do(lambda e: e.scalar_tensor_tensor(
            bt[:], bt[:], 8.0, cn("colmask").unsqueeze(1).broadcast_to([128, 14, 64]), ALU.mult, ALU.add),
            w, c_tok)
        bt_[h] = (i, bt, d)

    na_table(0)
    na_table(1)
    na_us = []
    for h in range(8):
        for qt in range(4):
            p0 = 64 * (h % 2)

            def opn(h=h, qt=qt):
                if h == 0:
                    ob4[qt] = OB.take()

            def done(t, h=h, qt=qt):
                if qt == 3:
                    BT.give(bt_[h][0], *now())
                    if h + 2 < 8:
                        na_table(h + 2)
                if h == 7:
                    w_ = split_out(oa, ob4[qt][1], qt, t)
                    OB.give(ob4[qt][0], *w_)
                    oa_t.extend(w_)

            na_us.append(dict(
                row=p0, w=512, q=lambda h=h, qt=qt, p0=p0: qa[p0:p0 + 64, h // 2, qt * 128:(qt + 1) * 128],
                k=lambda h=h, p0=p0: ka[p0:p0 + 64, h // 2, :], qk=lambda h=h: [qt_[h // 2], kt_[h // 2]],
                scale=0.125, nm=nm(qt * 8 + h), sm=sm(qt * 8 + h), open=opn, done=done,
                sms=columns(S_SM, qt * 8 + h, 1), rss=columns(S_RS, qt * 8 + h, 1),
                v=lambda h=h: [va[:, j, h * 64:(h + 1) * 64] for j in range(4)], vt=lambda: v_t,
                o=lambda h=h, qt=qt: head_out(ob4[qt][1], h), ot=lambda qt=qt: ob4[qt][2]))

            def setup(U=na_us[-1], h=h, qt=qt):
                U["table"] = bt_[h][1][:, 6 - 2 * qt:14 - 2 * qt, :].rearrange("p j k -> p (j k)")
                U["tt"] = bt_[h][2]
            na_us[-1]["pre"] = setup
    oa_t = []
    oT_free[0] = fr
    attend(batches(na_us))

    fr = now()
    obf = at([128, 6, T], RA + 40 * K)
    tb = at([128, 4, 640], RA + 52 * K)
    stm = at([4, 6, T], RA + 62 * K)
    tb_t = load(tb[:], D["dil"], fr)

    def perm_tile(a, g, t):
        if g == 0:
            return a[:, t * 128:(t + 1) * 128]
        return a.rearrange("p (l r) -> p r l", r=4)[:, t, :]

    def perm_all(a, g):
        return a if g == 0 else a.rearrange("p (l r) -> p r l", r=4)

    def shaped(a, g):
        return a if g == 0 else a.rearrange("p (r l) -> p r l", r=4)

    stm_t = []
    obf_t = []
    for g in range(3):
        o0 = RA + 16 * K + (g % 2) * 12 * K
        qg = at([128, 2, T], o0)
        kg = at([128, 2, T], o0 + 4 * K)
        vg = at([128, 4, 256], o0 + 8 * K)
        frg = fr if g < 2 else now()
        qt_ = [project("qb", 2 * g + c, H, shaped(qg[:, c, :], g), frg, view=lambda a, g=g: perm_all(a, g))
               for c in range(2)]
        kt_ = [project("kb", 2 * g + c, H, shaped(kg[:, c, :], g), frg, view=lambda a, g=g: perm_all(a, g))
               for c in range(2)]
        v_t = tokens_first(f"vb{g}", 256, 4, H, lambda t: vg[:, t, :], frg, toks_of=lambda a, t, g=g: perm_tile(a, g, t))
        us = []
        obk = {}
        order = [(t, hh) for t in range(4) for hh in (0, 2, 1, 3)]
        if g > 0:
            order = [(t, hh) for t2 in (0, 2) for par in (0, 1) for t in (t2, t2 + 1) for hh in (par, par + 2)]
        seen = {}

        def dil_cols(base, g, t, hh):
            return lambda n: st[:, base + 4 * t + hh:base + 4 * t + hh + 2 * (n - 1) + 1:2]

        for t, hh in order:
            if True:
                if g == 0:
                    a, b = max(0, t - 1), min(4, t + 2)
                    tab = tb[:, hh, (a - t + 1) * 128:(b - t + 1) * 128]
                else:
                    a, b = t, t + 1
                    tab = tb[:, hh, 256 + g * 128:384 + g * 128]
                p0 = 64 * (hh % 2)

                def opn(t=t, hh=hh):
                    if t not in obk:
                        obk[t] = OB.take()

                def done(tok, t=t, hh=hh, g=g, obk=obk, seen=seen):
                    seen[t] = seen.get(t, 0) + 1
                    if seen[t] < 4:
                        return
                    for c in range(2):
                        o_ = perm_tile(obf[:, 2 * g + c, :], g, t)
                        a_ = act.do(lambda e: e.copy(o_, obk[t][1][:, c * 128:(c + 1) * 128]), tok, fr)
                    OB.give(obk[t][0], a_)
                    obf_t.append(a_)
                    b, bk, bt = PB.take()
                    for k_, s0 in ((0, S_NM), (1, S_SM)):
                        tk = pe.do(lambda e, k_=k_, s0=s0: e.transpose(
                            bk[0:4, k_ * 128:(k_ + 1) * 128], st[:, s0 + 4 * t:s0 + 4 * t + 4], cn("ident")), bt,
                            now())
                    for k_ in range(2):
                        o_ = perm_tile(stm[:, 2 * g + k_, :], g, t)
                        s_ = bk[0:4, k_ * 128:(k_ + 1) * 128]
                        a_ = act.do(lambda e, o_=o_, s_=s_: e.copy(o_, s_), tk, fr)
                    PB.give(b, a_)
                    stm_t.append(a_)

                us.append(dict(
                    row=p0, w=(b - a) * 128, q=lambda t=t, hh=hh, p0=p0, qg=qg: qg[p0:p0 + 64, hh // 2, t * 128:(t + 1) * 128],
                    k=lambda a=a, b=b, hh=hh, p0=p0, kg=kg: kg[p0:p0 + 64, hh // 2, a * 128:b * 128],
                    qk=lambda hh=hh, qt_=qt_, kt_=kt_: [qt_[hh // 2], kt_[hh // 2]], scale=0.125, table=tab, tt=tb_t,
                    nm=nm(4 * t + hh), sm=sm(4 * t + hh), open=opn, done=done,
                    v=lambda a=a, b=b, hh=hh, vg=vg: [vg[:, j, hh * 64:(hh + 1) * 64] for j in range(a, b)],
                    vt=lambda v_t=v_t: v_t, o=lambda t=t, hh=hh, obk=obk: head_out(obk[t][1], hh),
                    sms=dil_cols(S_SM, g, t, hh), rss=dil_cols(S_RS, g, t, hh),
                    ot=lambda t=t, obk=obk: obk[t][2]))
        attend(batches(us))

    i0, t0, f0 = tmp.take()
    w = t0[0:4, :]
    al = [stm_t]
    a = dve.do(lambda e: e.tensor_tensor(w, stm[:, 0, :], stm[:, 2, :], ALU.min), stm_t, f0)
    a = dve.do(lambda e: e.tensor_tensor(w, w, stm[:, 4, :], ALU.min), a)
    for g in range(3):
        b = dve.do(lambda e, g=g: e.tensor_tensor(stm[:, 2 * g, :], w, stm[:, 2 * g, :], ALU.subtract), a)
        b = act.do(lambda e, g=g: e.activation(stm[:, 2 * g, :], stm[:, 2 * g, :], ACT.Exp), b)
        c = dve.do(lambda e, g=g: e.tensor_tensor(stm[:, 2 * g + 1, :], stm[:, 2 * g, :], stm[:, 2 * g + 1, :],
                                                  ALU.mult), b)
    a = dve.do(lambda e: e.tensor_tensor(w, stm[:, 1, :], stm[:, 3, :], ALU.add), c)
    a = dve.do(lambda e: e.tensor_tensor(w, w, stm[:, 5, :], ALU.add), a)
    a = dve.do(lambda e: e.reciprocal(w, w), a)
    for g in range(3):
        al = dve.do(lambda e, g=g: e.tensor_tensor(stm[:, 2 * g + 1, :], stm[:, 2 * g + 1, :], w, ALU.mult), a)
    tmp.give(i0, al)
    fr = now()
    ob = at([128, 2, 6, T], RA + 16 * K, F32R)
    ob_t = []
    for c6 in range(6):
        b, bank, bt = PB.take()
        t = pe.do(lambda e, c6=c6, bank=bank: e.matmul(
            bank[:], cn("sel")[0:4, (c6 % 2) * 128:(c6 % 2 + 1) * 128], stm[:, 2 * (c6 // 2) + 1, :],
            start=True, stop=True), bt, al, c_tok)
        i, s, f = tmp.take()
        d = dve.do(lambda e, c6=c6, s=s, bank=bank: e.tensor_tensor(s[:], bank[:], obf[:, c6, :], ALU.mult),
                   t, f, obf_t)
        PB.give(b, d)
        wv = split(ob[:, 0, c6, :], ob[:, 1, c6, :], s[:], d, fr)
        tmp.give(i, *wv)
        ob_t.append(wv)

    def merge(mg, fr, branches, H):
        toks = []
        for m in range(KC):
            acc_i = None
            for n, (gname, g0, parts, xs_) in enumerate(branches):
                bg, gb, tg = dense([(gname, g0 + m, 0, list(range(8)))], H)
                bo, bb, to = dense([(nm_, m, c0, ch) for nm_, c0, ch in parts], xs_)
                i, s, f = tmp.take()
                d = sigmul(s[:], gb, bb[:], tg, to, f, gate_free=lambda a, bg=bg: PB.give(bg, a))
                PB.give(bo, d)
                if acc_i is None:
                    acc_i, s0 = i, s
                else:
                    d = dve.do(lambda e, s=s, s0=s0: e.tensor_tensor(s0[:], s0[:], s[:], ALU.add), d)
                    tmp.give(i, d)
            d = pool.do(lambda e: e.tensor_scalar(s0[:], s0[:], 0.5, None, ALU.mult), d)
            w_ = split(mg[:, 0, m, :], mg[:, 1, m, :], s0[:], d, fr)
            tmp.give(acc_i, *w_)
            toks.append(w_)
        return lambda c: (mg[:, 0, c, :], mg[:, 1, c, :], toks[c])

    fr = now()
    mg = at([128, 2, KC, T], RA + 40 * K, F32R)
    xs = merge(mg, fr, [
        ("ga", 0, [("bra", 0, list(range(4)))], lambda c: (oa[:, 0, c, :], oa[:, 1, c, :], oa_t)),
        ("gb", 0, [("brb", 0, list(range(6)))], lambda c: (ob[:, 0, c, :], ob[:, 1, c, :], ob_t[c]))], H)
    post, ft = add_post(now())
    down("wo", KC, xs, post)
    xt = postnorm(lambda c: gn[:, 3, c:c + 1], ft, xt)
    ht = prenorm(4, xt, sq=True)
    xs = ffn("f2", ht)
    post, ft = add_post(now())
    down("f2_d", FC, xs, post)
    xt = postnorm(lambda c: gh[:, 1, c:c + 1], ft, xt)

    def rope(src_bank, b, tok, dst, M, cs, sn, permn, tr, *free):
        iy, y, fy = tmp.take()
        a = act.do(lambda e: e.copy(y[0:M, :], src_bank[0:M, :]), tok, fy)
        PB.give(b, a)
        b2, bk2, bt2 = PB.take()
        t = pe.do(lambda e: e.matmul(bk2[0:M, :], cn(permn)[0:M, :], y[0:M, :], start=True, stop=True),
                  bt2, a, c_tok)
        ir, r, f_r = tmp.take()
        d1 = dve.do(lambda e: e.tensor_tensor(r[0:M, :], bk2[0:M, :], sn[0:M, :], ALU.mult), t, f_r, tr)
        PB.give(b2, d1)
        d2 = pool.do(lambda e: e.tensor_tensor(y[0:M, :], y[0:M, :], cs[0:M, :], ALU.mult), a, t, tr)
        if callable(dst):
            d = dve.do(lambda e: e.tensor_tensor(r[0:M, :], y[0:M, :], r[0:M, :], ALU.add), d1, d2)
            w_ = dst(r, d)
            tmp.give(ir, *w_)
            tmp.give(iy, d)
            return w_
        d = dve.do(lambda e: e.tensor_tensor(dst, y[0:M, :], r[0:M, :], ALU.add), d1, d2, *free)
        tmp.give(ir, d)
        tmp.give(iy, d)
        return [d]

    def causal_units(qf, kf, qk, vf, vt, obank, hq, h, qt, scale, col, **kw):
        w = (qt + 1) * 128
        return dict(w=w, q=qf, k=kf, qk=qk, scale=scale, table=cn("causal")[:, 384 - qt * 128:512], tt=c_tok,
                    nm=nm(col), sm=sm(col), v=vf, vt=vt, **kw)

    for L in range(2):
        ht = prenorm(6 + 3 * L, xt, sq=True)
        H = hs(ht)
        fr = now()
        s_ = str(L)
        oc = at([128, 2, 4, T], RA, F32R)
        ob = at([128, 2, 4, T], RA + 16 * K, F32R)
        oa = at([128, 2, 4, T], RA + 32 * K, F32R)
        rt_ = at([128, 4, T], RA + 48 * K)
        r_t = [load(rt_[:, i, :], D["rope"][i], fr, rope_tok[i]) for i in range(4)]
        cl = at([128, 2, 4, T], RA + 16 * K, F32R)
        cv = at([128, 4, T], RA + 32 * K)
        qf = Ring([at([96, T], RA + (40 + 2 * i) * K) for i in range(4)])
        kf = Ring([at([96, T], RA + (56 + 2 * i) * K) for i in range(4)])
        cf = at([128, 4, T], RA + 64 * K)
        ct = []
        for m in range(4):
            ct.append(project("clat" + s_, m, H, cf[:, m, :], fr))
        clt = []
        for n in range(2):
            sumsq([cf[:, 2 * n + c, :] for c in range(2)], ct[2 * n:2 * n + 2])
            rt = rms(256, acc_tok[0])
            clt += scaled([cf[:, 2 * n + c, :] for c in range(2)], lambda p, c, n=n: cl[:, p, 2 * n + c, :],
                          lambda c, n=n: gcn[:, 4 * L + 2 * n + c:4 * L + 2 * n + c + 1], rt,
                          ct[2 * n:2 * n + 2], fr)
        b, bank, tok = dense([("kpe" + s_, 0, 0, list(range(8)))], H, 96)

        def kpe(r, d):
            return [dve.do(lambda e, i=i: e.tensor_copy(kf.bufs[i][64:96, :], r[64:96, :]), d, fr)
                    for i in range(4)]
        kp_t = rope(bank, b, tok, kpe, 96, rt_[:, 2, :], rt_[:, 3, :], "permc", r_t[2:4])
        CX = lambda n: (lambda c: (cl[:, 0, 2 * n + c, :], cl[:, 1, 2 * n + c, :], clt[2 * n + c]))
        v_t = tokens_first("cv" + s_, 512, 2, CX(1), lambda t: cv[:, t, :], fr, nk=2)
        hd = {}
        ob4 = {}
        us = []

        def head_in(h):
            if h % 2 == 0:
                hd["u"] = unit("cup" + s_, h // 2, 0, 640)
            u, wh, wl, wt = hd["u"]
            c0 = 320 * (h % 2)
            res = []
            for n, M in ((0, 96), (1, 64)):
                b, bank, bt = PB.take()
                for c in range(2):
                    xh, xl, xt_ = CX(n)(c)
                    a_ = c0 + 192 * n + c * M
                    tok = mm3(bank[0:M, :], wh[:, a_:a_ + M], wl[:, a_:a_ + M], xh, xl, c == 0, c == 1,
                              wt, xt_, bt)(c == 1)
                res.append((b, bank, tok))
            freed[u] = tok
            iq, q_, fq = qf.take()
            ik, k_, fk = kf.take()
            b, bank, tok = res[1]
            kt = act.do(lambda e: e.copy(k_[0:64, :], bank[0:64, :]), tok, fk, fr)
            PB.give(b, kt)
            b, bank, tok = res[0]
            qt2 = rope(bank, b, tok, q_[:], 96, rt_[:, 2, :], rt_[:, 3, :], "permc", r_t[2:4], fq, fr)
            hd[h] = (iq, q_, ik, k_, [kt, qt2, kp_t])

        oc_t = []
        oT_free[0] = fr
        for h, qt in [(2 * hp + j, qt) for hp in range(4) for qt in range(4) for j in range(2)]:
            if True:
                def pre(h=h, qt=qt):
                    if h < 2 and qt == 0:
                        head_in(h)
                    if qt == 2 and h < 6:
                        head_in(h + 2)

                def after(t, h=h, qt=qt):
                    if qt == 3:
                        qf.give(hd[h][0], t)
                        kf.give(hd[h][2], t)

                def opn(h=h, qt=qt):
                    if h == 0:
                        ob4[qt] = OB.take()

                def done(t, h=h, qt=qt):
                    if h == 7:
                        w_ = split_out(oc, ob4[qt][1], qt, t)
                        OB.give(ob4[qt][0], *w_)
                        oc_t.extend(w_)
                us.append(causal_units(
                    lambda h=h, qt=qt: hd[h][1][:, qt * 128:(qt + 1) * 128],
                    lambda h=h, qt=qt: hd[h][3][:, 0:(qt + 1) * 128], lambda h=h: hd[h][4],
                    lambda h=h, qt=qt: [cv[:, j, h * 64:(h + 1) * 64] for j in range(qt + 1)],
                    lambda: v_t, None, None, h, qt, float(96 ** -0.5), qt * 8 + h, row=0, pre=pre,
                    after=after, sms=columns(S_SM, qt * 8 + h, 1), rss=columns(S_RS, qt * 8 + h, 1), open=opn, done=done,
                    o=lambda h=h, qt=qt: head_out(ob4[qt][1], h), ot=lambda qt=qt: ob4[qt][2]))
        attend(batches(us))

        fr = now()
        va = at([128, 4, 408], RA + 71 * K)
        qb = at([128, 4, T], RA + 56 * K)
        kb = at([128, 2, T], RA + 64 * K)
        snk = st[:, 136:144]
        nsk = st[:, 144:152]
        esk = st[:, 96:128]
        s_t = load(snk, D["sinks"][L], fr)
        s_t = dve.do(lambda e: e.tensor_scalar(nsk, snk, -1.0, None, ALU.mult), s_t)
        v_t = tokens_first("v2" + s_, 408, 2, H, lambda t: va[:, t, :], fr)

        def roped(name, m, dst):
            b, bank, tok = dense([(name, m, 0, list(range(8)))], H)
            return rope(bank, b, tok, dst, 128, rt_[:, 0, :], rt_[:, 1, :], "perm", r_t[0:2], fr)

        kt_ = [roped("kb2" + s_, m, kb[:, m, :]) for m in range(2)]
        qt_ = [roped("qb2" + s_, m, qb[:, m, :]) for m in range(4)]
        us = []
        obk = {}
        ob_t = []
        oT_free[0] = fr
        for qt in range(4):
            for h in (0, 2, 4, 6, 1, 3, 5, 7):
                a = max(0, qt - 1)
                p0 = 64 * (h % 2)

                def opn(qt=qt, h=h):
                    if h == 0:
                        obk[qt] = OB.take()

                def done(tok, qt=qt, h=h):
                    if h != 7:
                        return
                    w_ = split_out(ob, obk[qt][1], qt, now())
                    OB.give(obk[qt][0], *w_)
                    ob_t.extend(w_)

                def extra(batch, es, ds, qt=qt, h=h):
                    n = len(batch)
                    c = qt * 8 + h
                    col = lambda a: a[:, c:c + 2 * n - 1:2]
                    x = dve.do(lambda e: e.tensor_tensor(col(esk), snk[:, h:h + 2 * n - 1:2], col(st), ALU.add), ds)
                    x = act.do(lambda e: e.activation(col(esk), col(esk), ACT.Exp), x)
                    sm_ = columns(S_SM, c, 2)(n)
                    return dve.do(lambda e: e.tensor_tensor(sm_, sm_, col(esk), ALU.add), x, es)

                us.append(dict(
                    row=p0, w=(qt + 1 - a) * 128, q=lambda qt=qt, h=h, p0=p0: qb[p0:p0 + 64, h // 2, qt * 128:(qt + 1) * 128],
                    k=lambda qt=qt, a=a, h=h, p0=p0: kb[p0:p0 + 64, h // 4, a * 128:(qt + 1) * 128],
                    qk=lambda h=h: [qt_[h // 2], kt_[h // 4]], scale=0.125,
                    table=cn("band")[:, (a - qt + 1) * 128:256], tt=[c_tok, s_t], init=nsk[:, h:h + 1],
                    nm=nm(qt * 8 + h), sm=sm(qt * 8 + h), open=opn, done=done,
                    v=lambda qt=qt, a=a, h=h: [va[:, j, 256 + (h // 4) * 64:320 + (h // 4) * 64]
                                               for j in range(a, qt + 1)],
                    vt=lambda: v_t, o=lambda qt=qt, h=h: head_out(obk[qt][1], h), extra=extra,
                    sms=columns(S_SM, qt * 8 + h, 2), rss=columns(S_RS, qt * 8 + h, 2),
                    ot=lambda qt=qt: obk[qt][2]))
        attend(batches(us))

        fr = now()
        k2 = [at([128, 2, 2, 560], RA + o_ * K, F32R) for o_ in (32, 56)]
        w2 = at([128, 2, 192], RA + 41 * K)
        pos = at([128, 2, 32], RA + 43 * K)
        kcm = at([128, 64], RA + 68 * K)
        hids = [at([128, 2, 2, 34], RA + 68 * K + 256), at([128, 2, 2, 34], RA + 44 * K)]
        bd = at([128, 2, 256], RA + 69 * K)
        w2_t = load(w2[:], D["w2"][L], fr)
        p_t = load(pos[:], D["cpos"][L], fr)
        bd_t = dve.do(lambda e: e.memset(bd[:], 0.0), fr)
        kt2 = [[], []]
        for kv in range(2):
            K2 = k2[kv]
            z = dve.do(lambda e: e.memset(K2[:, :, :, 543:560].bitcast(F32), 0.0), fr)
            for g in range(2):
                def put(r, d, K2=K2, g=g):
                    w_ = []
                    for p0, sh in ((0, 0), (64, 1)):
                        w_ += split(K2[p0:p0 + 64, 0, g, 0:512 - sh], K2[p0:p0 + 64, 1, g, 0:512 - sh],
                                    r[p0:p0 + 64, sh:512], d, fr)
                    return w_
                if kv == 0:
                    kt2[kv] += roped("kc" + s_, g, put)
                else:
                    b, bank, tok = dense([("kc" + s_, 2 + g, 0, list(range(8)))], H)
                    w_ = put(bank, tok)
                    PB.give(b, *w_)
                    kt2[kv] += w_
                for p0, sh in ((0, 0), (64, 1)):
                    kt2[kv] += split(K2[p0:p0 + 64, 0, g, 512 - sh:544 - sh], K2[p0:p0 + 64, 1, g, 512 - sh:544 - sh],
                                     pos[p0:p0 + 64, kv, :], p_t, z)
        hid_t = []
        for kv in range(2):
            K2 = k2[kv]
            bb = [PB.take() for _ in range(2)]
            for j4 in range(4):
                u, wh, wl, wt = unit("cw1" + s_, kv, j4 * 1024, 1024)
                for jj in range(4):
                    j = j4 * 4 + jj
                    for ch in range(2):
                        o_ = bb[ch][1][:, 0:68].rearrange("p (g n) -> p g n", g=2)
                        xh, xl = (K2[:, p, :, 2 * j:2 * j + 529:16] for p in range(2))
                        a_ = jj * 256 + ch * 128
                        tok = mm3(o_, wh[:, a_:a_ + 128], wl[:, a_:a_ + 128], xh, xl, j == 0, j == 15,
                                  wt, kt2[kv], bb[ch][2])(True)
                freed[u] = tok
            i, xx, f = tmp.take()
            i2, yy, f2 = tmp.take()
            hb = st[:, 160 + 2 * kv:162 + 2 * kv]
            for ch in range(2):
                bank = bb[ch][1]
                x_ = xx[:, ch * 68:ch * 68 + 68]
                d = dve.do(lambda e: e.tensor_copy(hb[:, ch:ch + 1], bank[:, 32:33]), tok, dve_last())
                d = dve.do(lambda e: e.tensor_scalar(x_, bank[:, 0:68], hb[:, ch:ch + 1], None, ALU.add), d, f)
                PB.give(bb[ch][0], d)
            X_, Y_ = xx[:, 0:136], yy[:, 0:136]
            d = dve.do(lambda e: e.tensor_tensor(Y_, X_, X_, ALU.mult), d, f2)
            d = dve.do(lambda e: e.tensor_scalar(Y_, Y_, 0.044715, 1.0, ALU.mult, ALU.add), d)
            d = dve.do(lambda e: e.tensor_tensor(Y_, Y_, X_, ALU.mult), d)
            d = act.do(lambda e: e.activation(Y_, Y_, ACT.Tanh, scale=0.7978845608028654), d)
            d = dve.do(lambda e: e.tensor_scalar(Y_, Y_, 0.5, 0.5, ALU.mult, ALU.add), d)
            H_ = hids[kv][:].rearrange("p c g n -> p (c g n)")
            d = dve.do(lambda e: e.tensor_tensor(H_, Y_, X_, ALU.mult), d, fr)
            tmp.give(i, d)
            tmp.give(i2, d)
            hid_t.append(d)

        fr2 = now()
        qq = at([128, 4, T], RA + 56 * K)
        ks = at([128, 2, T], RA + 64 * K)
        kw_ = at([128, 2, T], RA + 52 * K)
        fr = fr2
        qt_ = [roped("qa2" + s_, m, qq[:, m, :]) for m in range(2)]
        b, bank, bt = PB.take()
        for ch in range(2):
            tok = pe.do(lambda e: e.matmul(
                bank[:, 0:64].rearrange("p (g n) -> p g n", g=2), w2[:, ch, 0:128],
                hids[0][:, ch, :, 0:32], start=ch == 0, stop=ch == 1), bt, hid_t[0], w2_t)
        kc_t = act.do(lambda e: e.copy(kcm[:], bank[:, 0:64]), tok, fr2)
        PB.give(b, kc_t)
        i3, hr, f3 = tmp.take()
        for ch in range(2):
            for g in range(2):
                c = (2 * ch + g) * 128
                d = dve.do(lambda e: e.tensor_copy(
                    hr[:, c:c + 128].rearrange("p (r n) -> p r n", r=4),
                    hids[1][:, ch, g, 0:32].unsqueeze(1).broadcast_to([128, 4, 32])), hid_t[1], f3)
        for g in range(2):
            b, bank, bt = PB.take()
            for ch in range(2):
                lh = hr[:, (2 * ch + g) * 128:(2 * ch + g + 1) * 128]
                tok = pe.do(lambda e: e.matmul(
                    bank[:, 0:64], lh, w2[:, ch, 128:192], start=ch == 0, stop=ch == 1), bt, d, w2_t)
            for r in range(4):
                vc_t = act.do(lambda e: e.copy(
                    bd[32 * r:32 * r + 32, g, 64 * r:64 * r + 64], bank[32 * r:32 * r + 32, 0:64]), tok, bd_t)
            PB.give(b, vc_t)
        tmp.give(i3, tok)
        qt_ += [roped("qa2" + s_, m, qq[:, m, :]) for m in (2, 3)]
        ks_t = [roped("ks" + s_, m, ks[:, m, :]) for m in range(2)]
        kw_t = [roped("ks" + s_, 2 + m, kw_[:, m, :]) for m in range(2)]
        sg = at([128, 4, 24], RA + 45 * K)
        sgt = act.do(lambda e: e.activation(sg[:], va[:, :, 384:408], ACT.Tanh, scale=0.5), fr, v_t)
        sgs = at([128, 4, 24], RA + 77 * K + 512)
        sgt = dve.do(lambda e: e.tensor_scalar(sgs[:], sg[:], 0.5, 0.5, ALU.mult, ALU.add), sgt, fr)
        oT_free[0] = [sgt, fr]
        oa_t = []
        us = []
        obk = {}
        for qt in range(4):
            for kind in range(2):
                for h in (0, 2, 4, 6, 1, 3, 5, 7):
                    p0 = 64 * (h % 2)
                    kk, kkt = (ks, ks_t) if kind == 0 else (kw_, kw_t)
                    col = kind * 8 + h + 16 * (qt % 2)

                    def cmp_part(qt=qt):
                        ob_ = OB.take()
                        b, bank, bt = PB.take()
                        tok = None
                        for h in (0, 2, 4, 6, 1, 3, 5, 7):
                            p0 = 64 * (h % 2)
                            tok = pe.do(lambda e, h=h, p0=p0: e.matmul(
                                bank[:, h * 32:h * 32 + 32], qq[p0:p0 + 64, h // 2, qt * 128:(qt + 1) * 128],
                                kcm[p0:p0 + 64, (h // 4) * 32:(h // 4) * 32 + 32], start=True, stop=True),
                                bt, qt_[h // 2], kc_t, tok if h == 1 else None)
                        i, S, f = tmp.take()
                        S3 = S[:, 0:256].rearrange("p (h n) -> p h n", h=8)
                        mk = cn("cmpneg")[:, qt * 32:qt * 32 + 32].unsqueeze(1).broadcast_to([128, 8, 32])
                        m01 = cn("cmp01")[:, qt * 32:qt * 32 + 32].unsqueeze(1).broadcast_to([128, 8, 32])
                        d = dve.do(lambda e: e.scalar_tensor_tensor(
                            S3, bank[:, 0:256].rearrange("p (h n) -> p h n", h=8), 0.125, mk, ALU.mult, ALU.add),
                            tok, f, c_tok)
                        PB.give(b, d)
                        mx, sx = st[:, 168:176], st[:, 176:184]
                        d = dve.do(lambda e: e.tensor_reduce(mx, S3, AX, ALU.max), d)
                        d = dve.do(lambda e: e.tensor_tensor(S3, S3, mx.unsqueeze(2).broadcast_to([128, 8, 32]),
                                                             ALU.subtract), d)
                        d = act.do(lambda e: e.activation(S[:, 0:256], S[:, 0:256], ACT.Exp), d)
                        x = dve.do(lambda e: e.tensor_reduce(sx, S3, AX, ALU.add), d)
                        x = dve.do(lambda e: e.reciprocal(sx, sx), x)
                        x = dve.do(lambda e: e.tensor_tensor(sx, sx, sgs[:, qt, 0:24:3], ALU.mult), x, sgt)
                        d = dve.do(lambda e: e.tensor_tensor(S3, S3, m01, ALU.mult), x)
                        d = dve.do(lambda e: e.tensor_tensor(S3, S3, sx.unsqueeze(2).broadcast_to([128, 8, 32]),
                                                             ALU.mult), d)
                        b, bank2, bt = PB.take()
                        for g in range(2):
                            tok = pe.do(lambda e, g=g: e.transpose(bank2[:, g * 128:(g + 1) * 128],
                                                                   S[:, g * 128:(g + 1) * 128], cn("ident")), bt, d)
                        tmp.give(i, tok)
                        ip, PT, f = tmp.take()
                        d = dve.do(lambda e: e.tensor_copy(PT[:, 0:256], bank2[:, 0:256]), tok, f)
                        PB.give(b, d)
                        for g in range(2):
                            for c in range(2):
                                ch = 2 * g + c
                                tok = pe.do(lambda e: e.matmul(
                                    ob_[1][:, ch * 128:(ch + 1) * 128], bd[:, g, c * 128:(c + 1) * 128],
                                    PT[:, g * 128:(g + 1) * 128], start=ch == 0, stop=ch == 3,
                                    skip_group_check=True), d, ob_[2], vc_t)
                        tmp.give(ip, tok)
                        obk[qt] = ob_

                    def opn(qt=qt, kind=kind, h=h, f_=cmp_part):
                        if h == 0 and kind == 0 and qt == 0:
                            f_(0)
                        if h == 0 and kind == 1 and qt < 3:
                            f_(qt + 1)

                    def done(tok, qt=qt, kind=kind, h=h):
                        if h != 7 or kind == 0:
                            return
                        w_ = split_out(oa, obk[qt][1], qt, tok)
                        OB.give(obk[qt][0], *w_)
                        oa_t.extend(w_)

                    def gate(n, qt=qt, kind=kind, h=h):
                        c = 3 * h + kind + 1
                        return sgs[:, qt, c:c + 6 * (n - 1) + 1:6], sgt

                    us.append(causal_units(
                        lambda h=h, qt=qt, p0=p0: qq[p0:p0 + 64, h // 2, qt * 128:(qt + 1) * 128],
                        lambda h=h, qt=qt, p0=p0, kk=kk: kk[p0:p0 + 64, h // 4, 0:(qt + 1) * 128],
                        lambda h=h, kkt=kkt: [qt_[h // 2], kkt[h // 4]],
                        lambda h=h, qt=qt, kind=kind: [va[:, j, kind * 128 + (h // 4) * 64:kind * 128 + (h // 4) * 64 + 64]
                                                       for j in range(qt + 1)],
                        lambda: v_t, None, None, h, qt, 0.125, col, open=opn, done=done, row=p0,
                        add=True, gate=gate, sms=columns(S_SM, col, 2), rss=columns(S_RS, col, 2),
                        o=lambda qt=qt, h=h: head_out(obk[qt][1], h), ot=lambda qt=qt: obk[qt][2]))
        attend(batches(us))

        fr = now()
        mg = at([128, 2, KC, T], RA + 48 * K, F32R)
        r4 = list(range(4))
        xs = merge(mg, fr, [
            ("gate" + s_, 0, [("br2a" + s_, 0, r4)], lambda c: (oa[:, 0, c, :], oa[:, 1, c, :], oa_t)),
            ("gate" + s_, 8, [("br2b" + s_, 0, r4)], lambda c: (ob[:, 0, c, :], ob[:, 1, c, :], ob_t)),
            ("gate" + s_, 16, [("br2c" + s_, 0, r4)], lambda c: (oc[:, 0, c, :], oc[:, 1, c, :], oc_t))], H)

        def residual():
            new = []

            def post(m, bank, tok):
                d = dve.do(lambda e: e.tensor_tensor(xT[:, m, :], xT[:, m, :], bank[:], ALU.add), tok, xt[m])
                acc_tok[0], r = square_in(xT[:, m, :], m == 0, d)
                new.append([d, r])
                return [d]
            return post, new
        post, new = residual()
        down("wo2" + s_, KC, xs, post)
        xt = new
        ht = prenorm(7 + 3 * L, xt, sq=True)
        xs = ffn("f3" + s_, ht)
        post, new = residual()
        down("f3" + s_ + "_d", FC, xs, post)
        xt = new
        ht = prenorm(8 + 3 * L, xt, sq=True)
        H = hs(ht)
        fr = now()
        pf = at([128, 2, T], RA + 12 * K)
        ps = at([128, 2, 2, T], RA, F32R)
        a = load(pf[:], D["ple"][L], fr)
        p_t = [split(ps[:, 0, c, :], ps[:, 1, c, :], pf[:, c, :], a, fr) for c in range(2)]
        new = []
        for m in range(KC):
            bg, gb, tg = dense([("plg" + s_, m, 0, list(range(8)))], H)
            bo, bb_, to = dense([("plp" + s_, m, 0, [0, 1])], lambda c: (ps[:, 0, c, :], ps[:, 1, c, :], p_t[c]))
            i, s, f = tmp.take()
            d = sigmul(s[:], gb, bb_[:], tg, to, f, gate_free=lambda a, bg=bg: PB.give(bg, a))
            PB.give(bo, d)
            d = dve.do(lambda e: e.scalar_tensor_tensor(xT[:, m, :], s[:], 0.5, xT[:, m, :], ALU.mult, ALU.add),
                       d, xt[m])
            tmp.give(i, d)
            acc_tok[0], r = square_in(xT[:, m, :], m == 0, d)
            new.append([d, r])
        xt = new

    rt = rms(DM, acc_tok[0])
    outs = []
    for c in range(KC):
        i, h, f = tmp.take()
        a = dve.do(lambda e, c=c, h=h: e.scalar_tensor_tensor(h[:], xT[:, c, :], gn[:, 12, c:c + 1], rstd[:],
                                                              ALU.mult, ALU.mult), f, rt, xt[c])
        w = dma(sp, out[c], h[:], a, sem=f"o{c}")
        tmp.give(i, w)
        outs.append(w)
    sp.need(outs)
    sp.need(rope_done)
    sp.need([("m" + str(i), dsum[f"m{i}"]) for i in range(12)])
    return units, (pe, act, dve, pool, sp), sorted(dsum)


def build(nc, D, out):
    D = dict(D)
    D["rope"] = nc.dram_tensor("rope_scratch", [4, 128, T], F32).ap()
    D["rpbs"] = nc.dram_tensor("rpb_scratch", [120 * 8128], F32)
    seq = program(nc, None, D, out)[0]
    with ExitStack() as ctx:
        _, queues, names = program(nc, seq, D, out)
        pe, act, dve, pool, sp = queues
        sems = {n: ctx.enter_context(nc.semaphore("s_" + n)) for n in ["pe", "act", "dve", "pool"] + names}
        block = ctx.enter_context(nc.Block())

        @block.sync
        def _(eng):
            sp.play(eng, sems)

        @block.gpsimd
        def _(eng):
            pool.play(eng, sems)

        @block.scalar
        def _(eng):
            act.play(eng, sems)

        @block.vector
        def _(eng):
            dve.play(eng, sems)

        @block.tensor
        def _(eng):
            pe.play(eng, sems)


def _fm(w, cols=None):
    w = w if cols is None else w[:, cols]
    k, m = w.shape
    return np.ascontiguousarray(w.reshape(k // 128, 128, m // 128, 128).transpose(2, 1, 0, 3)).reshape(m // 128, 128, k)


def _tf(w):
    k, n = w.shape
    return np.ascontiguousarray(w.reshape(k // 128, 128, n).transpose(1, 0, 2)).reshape(1, 128, -1)


def _dup(w):
    return _fm(np.concatenate([w[:, 0:64], w[:, 0:64], w[:, 64:128], w[:, 64:128]], axis=1))


def _rows(x):
    t, n = x.shape
    return np.ascontiguousarray(x.T.reshape(n // 128, 128, t).transpose(1, 0, 2))


def _constants():
    c = np.zeros((128, NCONST), np.float32)

    def put(name, a):
        o_, w = CONST[name]
        c[0:a.shape[0], o_:o_ + a.shape[1]] = a
    p = np.arange(128)
    put("ident", np.eye(128, dtype=np.float32))
    swap = np.where(p % 64 < 32, p + 32, p - 32)
    put("perm", (p[:, None] == swap[None, :]).astype(np.float32))
    q = np.arange(96)
    sw = np.where(q < 80, q + 16, q - 16)
    put("permc", ((q[:, None] == sw[None, :]) & (q[None, :] >= 64)).astype(np.float32))
    col = np.arange(64)
    c0 = np.clip(p % 64 - 8, 0, 48)
    ok = (col[None, :] >= c0[:, None]) & (col[None, :] < c0[:, None] + 16)
    put("colmask", np.where(ok, 0.0, NEG).astype(np.float32))
    n = np.arange(32)
    end = np.where(n < 31, n * 16 + 31, 10 ** 6)
    tq = np.arange(4)[None, :, None] * 128 + p[:, None, None]
    okc = (end[None, None, :] <= tq).reshape(128, 128)
    put("cmpneg", np.where(okc, 0.0, NEG).astype(np.float32))
    put("cmp01", okc.astype(np.float32))
    sel = np.zeros((4, 2, 128), np.float32)
    for ch in range(2):
        for i in range(128):
            sel[2 * ch + i // 64, ch, i] = 1.0
    put("sel", sel.reshape(4, 256))
    f = np.float32
    i64 = np.power(f(10000.0), -np.arange(0, 64, 2, dtype=f) / f(64)).astype(f)
    i32 = np.power(f(10000.0), -np.arange(0, 32, 2, dtype=f) / f(32)).astype(f)
    put("invf", np.stack([i64[p % 32], np.where((p >= 64) & (p < 96), i32[p % 16], f(0))], 1).astype(f))
    put("sgn", np.stack([np.where(p % 64 < 32, -1.0, 1.0), np.where(p % 32 < 16, -1.0, 1.0)], 1).astype(f))
    ca = np.zeros((128, 512), f)
    ca[:, 384:] = np.where(p[None, :] <= p[:, None], 0.0, NEG)
    put("causal", ca)
    kj = np.arange(256) - 128
    okb = (kj[None, :] <= p[:, None]) & (kj[None, :] > p[:, None] - 128)
    put("band", np.where(okb, 0.0, NEG).astype(f))
    slopes = np.exp2(f(-8.0) * (np.arange(12, dtype=f) + f(1)) / f(12)).astype(f)
    dil = np.zeros((128, 4, 640), f)
    for hh in range(4):
        r = np.abs(np.arange(384)[None, :] - 128 - p[:, None])
        dil[:, hh, 0:384] = np.where(r <= 64, -slopes[hh] * r.astype(f) * f(8), NEG)
        r = np.abs(p[None, :] - p[:, None])
        dil[:, hh, 384:512] = np.where(r <= 64, -slopes[4 + hh] * (4 * r).astype(f) * f(8), NEG)
        dil[:, hh, 512:640] = np.where(r % 4 == 0, -slopes[8 + hh] * (4 * r).astype(f) * f(8), NEG)
    return c, dil


def kernel(**inputs):
    import concourse.bacc as bacc
    from concourse.bass_utils import run_bass_kernel_spmd

    I = {k: np.asarray(v) for k, v in inputs.items()}
    A = {}
    A["xT"] = _rows(I["x"][0])
    A["const"], A["dil"] = _constants()
    gains = [I["ffn1_pre_g"][0], I["ffn1_post_g"][0], I["mix_pre_g"][0], I["mix_post_g"][0], I["ffn2_pre_g"][0],
             I["ffn2_post_g"][0]]
    for l in range(2):
        gains += [I["mix_norm_2"][l], I["ffn_norm_2"][l], I["ple_norm_2"][l]]
    gains.append(I["final_norm_2"])
    A["gains"] = np.ascontiguousarray(np.stack(gains).reshape(len(GAINS), KC, 128).transpose(2, 0, 1))
    cg = np.concatenate([np.concatenate([I["c_q_norm_2"][l], I["c_kv_norm_2"][l]]) for l in range(2)])
    A["cgains"] = np.ascontiguousarray(cg.reshape(8, 128).T)
    A["positions"] = np.ascontiguousarray(I["positions_2"])
    A["rpb"] = np.ascontiguousarray(I["na_rpb"][0].reshape(120, 31))
    A["sinks"] = np.ascontiguousarray(np.broadcast_to(I["b_sinks_2"][:, None, :], (2, 128, 8)))
    for n, p in (("f1", "ffn1"), ("f2", "ffn2")):
        A[n + "_g"], A[n + "_u"], A[n + "_d"] = (_fm(I[f"{p}_w_{k}"][0]) for k in ("gate", "up", "down"))
    w = I["w_in"][0]
    A["qka"] = _fm(w[:, 0:1024])
    A["va"] = _tf(w[:, 1024:1536])
    A["qb"] = _fm(w[:, 1536:2304])
    A["kb"] = _fm(w[:, 2304:3072])
    for g in range(3):
        A[f"vb{g}"] = _tf(w[:, 3072 + 256 * g:3328 + 256 * g])
    A["ga"] = _fm(w[:, 3840:4864])
    A["gb"] = _fm(w[:, 4864:5888])
    A["bra"], A["brb"], A["wo"] = _fm(I["w_branch_a"][0]), _fm(I["w_branch_b"][0]), _fm(I["w_out"][0])
    for l in range(2):
        s = str(l)
        w = I["w_in_2"][l]
        A["clat" + s] = _fm(w[:, 2072:2584])
        kpe = np.concatenate([np.zeros((DM, 64), np.float32), w[:, 2584:2616]], 1)
        A["kpe" + s] = _tf(kpe)
        up = I["c_w_q_up_2"][l].reshape(2, 128, 8, 96)
        kv = I["c_w_kv_up_2"][l].reshape(2, 128, 8, 128)
        hq = up.transpose(2, 1, 0, 3).reshape(8, 128, 192)
        hk = kv[..., 0:64].transpose(2, 1, 0, 3).reshape(8, 128, 128)
        hh = np.concatenate([hq, hk], 2).reshape(4, 2, 128, 320).transpose(0, 2, 1, 3)
        A["cup" + s] = np.ascontiguousarray(hh).reshape(4, 128, 640)
        A["cv" + s] = np.ascontiguousarray(kv[..., 64:128].transpose(1, 0, 2, 3)).reshape(1, 128, 1024)
        A["v2" + s] = _tf(np.concatenate([w[:, 896:1024], w[:, 1152:1280], w[:, 1944:2072], w[:, 1280:1304]], 1))
        A["qb2" + s] = _fm(w[:, 1304:1816])
        A["kb2" + s] = _dup(w[:, 1816:1944])
        A["kc" + s] = np.concatenate([_dup(w[:, 512:640]), _dup(w[:, 640:768])])
        A["qa2" + s] = _fm(w[:, 0:512])
        A["ks" + s] = np.concatenate([_dup(w[:, 768:896]), _dup(w[:, 1024:1152])])
        A["cw1" + s] = np.concatenate([_tf(I["a_cmp_w1_k_2"][l]), _tf(I["a_cmp_w1_v_2"][l])])
        A["gate" + s] = _fm(I["w_branch_gate_2"][l])
        for b in "abc":
            A["br2" + b + s] = _fm(I[f"w_branch_{b}_2"][l])
        A["wo2" + s] = _fm(I["w_out_2"][l])
        for a, b in (("_g", "gate"), ("_u", "up"), ("_d", "down")):
            A["f3" + s + a] = _fm(I[f"w_ffn_{b}_2"][l])
        A["plg" + s] = _fm(I["w_ple_gate_2"][l])
        A["plp" + s] = _fm(I["w_ple_proj_2"][l])
    w2 = []
    for l in range(2):
        k = I["a_cmp_w2_k_2"][l].reshape(2, 128, 64)
        v = I["a_cmp_w2_v_2"][l].reshape(2, 128, 64)
        w2.append(np.concatenate([k, k, v], 2).transpose(1, 0, 2))
    A["w2"] = np.ascontiguousarray(np.stack(w2))
    pos = np.stack([I["a_cmp_pos_k_2"], I["a_cmp_pos_v_2"]], 1).transpose(0, 3, 1, 2)
    A["cpos"] = np.ascontiguousarray(np.concatenate([pos, pos], 1))
    A["ple"] = np.stack([_rows(I["p_2"][l, 0]) for l in range(2)])

    nc = bacc.Bacc("TRN2", target_bir_lowering=False, num_devices=1)
    D = {n: nc.dram_tensor("in_" + n, a.shape, mybir.dt.from_np(a.dtype), kind="ExternalInput").ap()
         for n, a in A.items()}
    out = nc.dram_tensor("out_0", (KC, 128, T), F32, kind="ExternalOutput").ap()
    build(nc, D, out)
    r = run_bass_kernel_spmd(nc, [{"in_" + n: a for n, a in A.items()}], core_ids=[0])
    y = r.results[0]["out_0"]
    return np.ascontiguousarray(y.reshape(DM, T).T).reshape(1, T, DM)
```

```python
from contextlib import ExitStack

import numpy as np

import concourse.bass as bass
from concourse import mybir

F32 = mybir.dt.float32
F32R = mybir.dt.float32r
I32 = mybir.dt.int32
ALU = mybir.AluOpType
ACT = mybir.ActivationFunctionType
AX = mybir.AxisListType.X

T = 512
DM = 1024
KC = 8
FF = 2816
FC = 22
EPS = 1e-6
NEG = -1e30
BIG = 3e38
BASE = 16512
K = 1024

GAINS = ["ffn1_pre", "ffn1_post", "mix_pre", "mix_post", "ffn2_pre", "ffn2_post",
         "mix2_0", "ffn_0", "ple_0", "mix2_1", "ffn_1", "ple_1", "final"]
CONST = {}
_at = 0
for _n, _w in (("ident", 128), ("perm", 128), ("permc", 96), ("colmask", 64), ("cmpneg", 128),
               ("cmp01", 128), ("sel", 256), ("invf", 2), ("sgn", 2), ("causal", 512), ("band", 256)):
    CONST[_n] = (_at, _w)
    _at += _w
NCONST = _at


class Noted:

    def matmul(self, *a, **k):
        return lambda e: e.matmul(*a, **k)

    def transpose(self, *a, **k):
        return lambda e: e.transpose(*a, **k)

    def activation(self, *a, **k):
        return lambda e: e.activation(*a, **k)

    def copy(self, *a, **k):
        return lambda e: e.copy(*a, **k)

    def tensor_copy(self, *a, **k):
        return lambda e: e.tensor_copy(*a, **k)

    def tensor_tensor(self, *a, **k):
        return lambda e: e.tensor_tensor(*a, **k)

    def tensor_scalar(self, *a, **k):
        return lambda e: e.tensor_scalar(*a, **k)

    def scalar_tensor_tensor(self, *a, **k):
        return lambda e: e.scalar_tensor_tensor(*a, **k)

    def tensor_tensor_reduce(self, *a, **k):
        return lambda e: e.tensor_tensor_reduce(*a, **k)

    def tensor_reduce(self, *a, **k):
        return lambda e: e.tensor_reduce(*a, **k)

    def reciprocal(self, *a, **k):
        return lambda e: e.reciprocal(*a, **k)

    def memset(self, *a, **k):
        return lambda e: e.memset(*a, **k)

    def dma_start(self, *a, **k):
        return lambda e: e.dma_start(*a, **k)


NOTED = Noted()


class Queue:

    def __init__(self, name):
        self.name = name
        self.items = []
        self.at = 0
        self.met = {}

    def need(self, toks):
        for tok in toks:
            if tok is None:
                continue
            if isinstance(tok, list):
                self.need(tok)
                continue
            s, v = tok
            if self.met.get(s, 0) < v:
                self.met[s] = v
                self.items.append(("wait", s, v))

    def do(self, fn, *toks, mark=True):
        self.need(toks)
        self.items.append(("do", fn(NOTED), (self.name, 1) if mark else None))
        if mark:
            self.at += 1
            return (self.name, self.at)
        return None

    def dma(self, fn, sem, total, *toks):
        self.need(toks)
        self.items.append(("do", fn(NOTED), (sem, 16)))
        return (sem, total)

    def play(self, eng, sems):
        for it in self.items:
            if it[0] == "wait":
                eng.wait_ge(sems[it[1]], it[2])
            else:
                ins = it[1](eng)
                if it[2] is not None:
                    ins.then_inc(sems[it[2][0]], it[2][1])


class Ring:

    def __init__(self, bufs):
        self.bufs = bufs
        self.last = [None] * len(bufs)
        self.n = 0
        self.out = set()

    def take(self):
        i = self.n % len(self.bufs)
        self.n += 1
        assert i not in self.out
        self.out.add(i)
        return i, self.bufs[i], self.last[i]

    def give(self, i, *toks):
        self.last[i] = list(toks)
        self.out.remove(i)


def program(nc, seq, D, out):
    pe, act, dve, pool, sp = (Queue(n) for n in ("pe", "act", "dve", "pool", "sp"))
    dsum = {}

    def dma(q, dst, src, *toks, sem="misc"):
        dsum[sem] = dsum.get(sem, 0) + 16
        return q.dma(lambda e: e.dma_start(dst, src), sem, dsum[sem], *toks)

    nmisc = [0]

    def load(dst, src, *toks):
        nmisc[0] += 1
        sem = f"m{nmisc[0] % 12}"
        return dma(pool, dst, src, (sem, dsum[sem]) if sem in dsum else None, *toks, sem=sem)

    def now():
        return [(q.name, q.at) for q in (pe, act, dve, pool) if q.at]

    names = [0]

    def at(shape, off, dt=F32):
        names[0] += 1
        return nc.alloc_sbuf_tensor_at(f"t{names[0]}_{'s' if seq is None else 'r'}", shape, dt,
                                       offset=BASE + off)

    RA = 92 * K
    MI = RA + 88 * K
    xT = at([128, KC, T], 0)
    hT = at([128, 2, KC, T], 16 * K, F32R)
    fT = at([128, KC, T], 16 * K)
    raw = [at([128, 1024], (48 + 4 * i) * K) for i in range(3)]
    spl = [at([128, 2, 1024], (60 + 8 * i) * K, F32R) for i in range(4)]
    con = at([128, NCONST], MI)
    o = MI + (NCONST * 4 + 31) // 32 * 32
    gn = at([128, len(GAINS), KC], o)
    gcn = at([128, 8], o + 416)
    gh = at([128, 2, KC], o + 448)
    ones = at([128, 128], o + 512)
    acc = at([128, T], o + 1024)
    rstd = at([128, T], o + 3 * K)
    st = at([128, 256], o + 5 * K)
    tmp = Ring([at([128, T], o + (6 + 2 * i) * K) for i in range(6)])
    assert o + 20 * K + BASE <= 229368
    Sr = Ring([at([128, T], RA + (78 + 2 * i) * K) for i in range(3)] + [at([128, T], o + 18 * K)])
    PTr = Ring([at([128, T], RA + (84 + 2 * i) * K) for i in range(2)])
    banks = [nc.alloc_psum_tensor(f"bk{i}_{'s' if seq is None else 'r'}", [128, T], F32)
             for i in range(8)] if seq is not None else [None] * 8
    if seq is None:
        banks = [xT[:, i, :] for i in range(8)]
    PB = Ring(banks[0:4])
    OB = Ring(banks[4:8])

    def cn(name):
        a, w = CONST[name]
        return con[:, a:a + w]

    units = []
    loaded, parted = [], []
    freed = {}
    AHEAD = 2

    def load_unit():
        if seq is None:
            return
        i = len(loaded)
        name, m, c0, n = seq[i]
        w = parted[i - 3] if i >= 3 else None
        loaded.append(dma(sp, raw[i % 3][:, 0:n], D[name][m, :, c0:c0 + n], w, sem=f"w{i % 3}"))

    g_tok = dma(sp, gn[:], D["gains"], sem="g")
    x_toks = []
    for c in range(KC):
        x_toks.append(dma(sp, xT[:, c, :], D["xT"][:, c, :], sem=f"x{c}"))
        if c in (0, 4):
            load_unit()
    dma(sp, con[:], D["const"], sem="c")
    dma(sp, gcn[:], D["cgains"], sem="c")
    c_tok = g_tok2 = ("c", 32)
    one_tok = dve.do(lambda e: e.memset(ones[:], 1.0))
    half = st[:, 240:248]
    half_tok = dve.do(lambda e: e.memset(half, -0.5))
    gh_tok = [dve.do(lambda e, i=i, j=j: e.tensor_scalar(gh[:, i, :], gn[:, j, :], 0.5, None, ALU.mult),
                     g_tok) for i, j in ((0, 1), (1, 5))]

    def stream(u, ahead):
        if seq is None:
            return
        while len(loaded) <= min(u + ahead + 2, len(seq) - 1):
            i = len(loaded)
            if i >= 3 and len(parted) <= i - 3:
                part(i - 3)
            load_unit()
        while len(parted) <= min(u + ahead, len(seq) - 1):
            part(len(parted))

    def part(i):
        n = seq[i][3]
        hi = spl[i % 4][:, 0, 0:n]
        lo = spl[i % 4][:, 1, 0:n]
        r = raw[i % 3][:, 0:n]
        f = freed[i - 4] if i >= 4 else None
        a = act.do(lambda e: e.copy(hi, r), loaded[i], f)
        b = dve.do(lambda e: e.tensor_tensor(lo, r, hi.bitcast(F32), ALU.subtract), a, loaded[i], f)
        parted.append([a, b])

    def unit(name, m, c0, n, ahead=AHEAD):
        u = len(units)
        units.append((name, m, c0, n))
        stream(u, ahead)
        return u, spl[u % 4][:, 0, 0:n], spl[u % 4][:, 1, 0:n], (parted[u] if seq is not None else None)

    def mm3(o_, wh, wl, xh, xl, start, stop, *toks):
        pe.do(lambda e: e.matmul(o_, wh, xh, start=start, stop=False), *toks, mark=False)
        pe.do(lambda e: e.matmul(o_, wh, xl, start=False, stop=False), mark=False)
        return lambda mark: pe.do(lambda e: e.matmul(o_, wl, xh, start=False, stop=stop), mark=mark)

    def dense(parts, xs, M=128):
        b, bank, bt = PB.take()
        for i, (name, m, c0, chunks) in enumerate(parts):
            u, wh, wl, wt = unit(name, m, c0, len(chunks) * M)
            for j, c in enumerate(chunks):
                xh, xl, xt = xs(c)
                last = j == len(chunks) - 1
                tok = mm3(bank[0:M, :], wh[:, j * M:(j + 1) * M], wl[:, j * M:(j + 1) * M], xh, xl,
                          i == 0 and j == 0, last and i == len(parts) - 1, wt, xt, bt)(last)
            freed[u] = tok
        stage()
        return b, bank, tok

    def dense4(names, xs):
        res = [OB.take() for _ in names]
        us = [unit(name, m, 0, K, ahead=3 - k) for k, (name, m) in enumerate(names)]
        order = [(c, k) for c in range(KC - 2) for k in range(4)] + [(c, k) for k in range(4) for c in (KC - 2, KC - 1)]
        for c, k in order:
            xh, xl, xt = xs(c)
            u, wh, wl, wt = us[k]
            b, bank, bt = res[k]
            tok = mm3(bank[:], wh[:, c * 128:(c + 1) * 128], wl[:, c * 128:(c + 1) * 128], xh, xl,
                      c == 0, c == KC - 1, wt, xt, bt)(c == KC - 1)
            if c == KC - 1:
                freed[u] = tok
                res[k] = (b, bank, tok)
                if k < 2:
                    stream(us[3][0], k + 1)
        return res

    steps = []
    late = []
    factor_due = [False]

    turns = []

    def turned():
        fs = list(turns)
        turns.clear()
        for fn in fs:
            fn()

    def stage():
        turned()
        if steps:
            steps.pop(0)()
            if not factor_due[0]:
                for fn in reversed(late):
                    fn()
                late.clear()

    def split(hi, lo, src, *toks):
        a = act.do(lambda e: e.copy(hi, src), *toks)
        b = dve.do(lambda e: e.tensor_tensor(lo, src, hi.bitcast(F32), ALU.subtract), a, *toks)
        return [a, b]

    acc_free = [None]
    rstd_free = [None]

    def square_in(src, first, *toks):
        if first:
            t = act.do(lambda e: e.activation(acc[:], src, ACT.Square), acc_free[0], *toks)
            return t, t
        i, q, f = tmp.take()
        a = act.do(lambda e: e.activation(q[:], src, ACT.Square), f, *toks)
        d = pool.do(lambda e: e.tensor_tensor(acc[:], acc[:], q[:], ALU.add), a, acc_tok[0])
        tmp.give(i, d)
        return d, a

    acc_tok = [None]

    vt_ = st[:, 232:240]
    v_free = [None]
    v_tok = [None]

    def rms(width, tok, dst, *free, n=4):
        got = []

        def first():
            b, bank, bt = PB.take()
            for c in range(n):
                a_ = acc[:, c * 128:(c + 1) * 128] if c < 4 else acc[:, c - 4:c - 4 + 509:4]
                t = pe.do(lambda e: e.matmul(bank[:, c:c + 1], a_, ones[:, 0:1],
                                             start=True, stop=True), bt, tok, one_tok, mark=c == n - 1)
            acc_free[0] = t
            a = dve.do(lambda e: e.tensor_scalar(vt_[:, 0:n], bank[:, 0:n], 1.0 / width, EPS, ALU.mult, ALU.add),
                       t, v_free[0])
            PB.give(b, a)
            v_tok[0] = pool.do(lambda e: e.tensor_tensor(vt_[:, 0:n], vt_[:, 0:n], half[:, 0:n], ALU.pow),
                               a, half_tok)

        def second():
            b, bank, bt = PB.take()
            i, dg, f = tmp.take()
            d = dve.do(lambda e: e.tensor_tensor(
                dg[:].rearrange("p (c t) -> p c t", c=4), cn("ident").unsqueeze(1).broadcast_to([128, 4, 128]),
                vt_[:, 0:4].unsqueeze(2).broadcast_to([128, 4, 128]), ALU.mult), v_tok[0], f, c_tok)
            v_free[0] = d
            t = pe.do(lambda e: e.matmul(bank[:], ones[:], dg[:], start=True, stop=True), d, bt)
            tmp.give(i, t)
            d = act.do(lambda e: e.copy(dst, bank[:]), t, *free)
            PB.give(b, d)
            got.append(d)
        return first, second, got

    def sumsq(srcs, toks):
        reads = []
        for c, s in enumerate(srcs):
            acc_tok[0], r = square_in(s, c == 0, toks[c])
            reads.append(r)
        return reads

    def scaled(srcs, dst, gain, factor, rt, toks, *free):
        res = []
        for c, s in enumerate(srcs):
            i, h, f = tmp.take()
            g = gain(c)
            a = dve.do(lambda e, h=h, s=s, g=g: e.scalar_tensor_tensor(h[:], s, g, factor, ALU.mult, ALU.mult),
                       f, rt, toks[c], g_tok2)
            w = split(dst(0, c), dst(1, c), h[:], a, *free)
            tmp.give(i, *w)
            res.append(w)
        return res

    rf_tok = [None]
    nv = st[:, 248:256]
    nv_tok = [None]

    def times_rstd(dst, src, *toks):
        return dve.do(lambda e: e.tensor_tensor(dst, src, rstd[0:dst.shape[0], :], ALU.mult), rf_tok[0], *toks)

    def gained(gi, c, t, *free):
        g = gn[:, gi, c:c + 1]
        hi = hT[:, 0, c, :]
        a = act.do(lambda e: e.activation(hi, xT[:, c, :], ACT.Copy, scale=g), t, g_tok, *free)
        b = dve.do(lambda e: e.scalar_tensor_tensor(hT[:, 1, c, :], xT[:, c, :], g, hi.bitcast(F32), ALU.mult,
                                                    ALU.subtract), a, t, g_tok, *free)
        return [a, b]

    def dve_last():
        return (dve.name, dve.at)

    def factor(n=4):
        first, second, got = rms(DM, acc_tok[0], rstd[:], dve_last(), n=n)

        def last():
            second()
            factor_due[0] = False
            rf_tok[0] = got[0]
            nv_tok[0] = v_free[0] = dve.do(lambda e: e.tensor_copy(nv[:, 0:n], vt_[:, 0:n]), v_tok[0],
                                           (act.name, act.at))
        factor_due[0] = True
        steps.extend([first, last])

    def hs(toks):
        return lambda c: (hT[:, 0, c, :], hT[:, 1, c, :], toks[c])

    def sigmul(dst, gbank, other, gtok, *toks, gate_free):
        i, e1, f = tmp.take()
        a = times_rstd(e1[:], gbank[:], gtok, f)
        gate_free(a)
        a = act.do(lambda e: e.activation(e1[:], e1[:], ACT.Tanh, scale=0.5), a)
        d = dve.do(lambda e: e.scalar_tensor_tensor(dst, e1[:], 1.0, other, ALU.add, ALU.mult), a, *toks)
        tmp.give(i, d)
        return d

    def down(name, nk, xs, post, early=False):
        for m in range(KC):
            parts = [(name, m, c0 * 128, list(range(c0, min(c0 + 8, nk)))) for c0 in range(0, nk, 8)]
            b, bank, tok = dense(parts, xs)
            if m == KC - 1 and early:
                stream(len(units) - 1, 3)
            PB.give(b, *post(m, bank, tok))

    def add_post(free):
        ft = []

        def post(m, bank, tok):
            a = act.do(lambda e: e.copy(fT[:, m, :], bank[:]), tok, free)
            acc_tok[0], r = square_in(fT[:, m, :], m == 0, a)
            ft.append(a)
            return [a]
        return post, ft

    def postnorm(gain, ft, xt, gi=None, n=4):
        first, second, got = rms(DM, acc_tok[0], rstd[:], dve_last())
        first()
        stream(len(units) - 1, 4)
        second()
        new, ht = [], []
        for c in range(KC):
            i, h, f = tmp.take()
            a = dve.do(lambda e, c=c, h=h: e.scalar_tensor_tensor(h[:], fT[:, c, :], gain(c), rstd[:],
                                                                 ALU.mult, ALU.mult), f, got[0], ft[c], g_tok, gh_tok)
            b = dve.do(lambda e, c=c, h=h: e.tensor_tensor(xT[:, c, :], xT[:, c, :], h[:], ALU.add), a, xt[c])
            tmp.give(i, b)
            ht.append(gained(gi, c, b) if gi is not None else None)
            acc_tok[0], r = square_in(xT[:, c, :], c == 0, b)
            new.append([b, r])
        if gi is not None:
            factor(n)
        return new, ht

    def ffn(name, ht, hook=None, wide=False):
        free = now()
        hid = at([128, 2, FC, T], RA, F32R)
        toks = {}

        def gate_up(j, ring, bg, g, tg, bu, u_, tu, free):
            i, s, f = tmp.take()
            ie, e1, fe = tmp.take()
            d = times_rstd(s[:], g[:], tg, f)
            ring.give(bg, d)
            yield
            a = act.do(lambda e: e.activation(e1[:], s[:], ACT.Tanh, scale=0.5), d, fe)
            yield
            d = dve.do(lambda e: e.scalar_tensor_tensor(s[:], e1[:], 1.0, s[:], ALU.add, ALU.mult), a)
            yield
            d = dve.do(lambda e: e.scalar_tensor_tensor(e1[:], u_[:], 0.5, rstd[:], ALU.mult, ALU.mult), d, tu)
            ring.give(bu, d)
            yield
            d = dve.do(lambda e: e.tensor_tensor(s[:], s[:], e1[:], ALU.mult), d)
            tmp.give(ie, d)
            yield
            a = act.do(lambda e: e.copy(hid[:, 0, j, :], s[:]), d, free)
            yield
            b = dve.do(lambda e: e.tensor_tensor(hid[:, 1, j, :], s[:], hid[:, 0, j, :].bitcast(F32), ALU.subtract),
                       a, d, free)
            tmp.give(i, a, b)
            toks[j] = [a, b]

        j0 = 0
        if wide:
            r = dense4([(name + "_g", 0), (name + "_u", 0), (name + "_g", 1), (name + "_u", 1)], hs(ht))
            j0 = 2
        for j in range(j0, FC):
            two = dense([(name + "_g", j, 0, list(range(8)))], hs(ht)) + dense(
                [(name + "_u", j, 0, list(range(8)))], hs(ht))
            work = [gate_up(j, PB, *two, [free, rope_done] if hook is not None and j == 13 else free)]
            if j == 2 and j0:
                work += [gate_up(k, OB, *r[2 * k], *r[2 * k + 1], free) for k in range(2)]
            for _ in range(7):
                for w in work:
                    next(w, None)
            if hook is not None:
                next(hook, None)
        return lambda c: (hid[:, 0, c, :], hid[:, 1, c, :], toks[c])


    def attend(us):
        n = len(us)
        st_ = [dict() for _ in us]
        for s in range(n + 5):
            turned()
            if 0 <= s - 4 < n:
                X = st_[s - 4]
                w, S = X["w"], X["S"]
                b, bank, bt = PB.take()
                for j in range(w // 128):
                    t = pe.do(lambda e: e.transpose(
                        bank[:, j * 128:(j + 1) * 128], S[:, j * 128:(j + 1) * 128], cn("ident")),
                        bt, X["p"], c_tok, mark=j == w // 128 - 1)
                Sr.give(X["i"], t)
                i, PT, f = PTr.take()
                d = act.do(lambda e: e.copy(PT[:, 0:w], bank[:, 0:w]), t, f)
                PB.give(b, d)
                X.update(PT=PT, pi=i, p=d)
            if s < n:
                X = st_[s]
                for U in us[s]:
                    if U.get("pre"):
                        U["pre"]()
                b, bank, bt = PB.take()
                i, S, f = Sr.take()
                o_ = 0
                for U in us[s]:
                    U["at"] = o_
                    q, k, w = U["q"](), U["k"](), U["w"]
                    t = pe.do(lambda e: e.matmul(bank[:, o_:o_ + w], q, k, start=True, stop=True),
                              bt, U["qk"](), mark=U is us[s][-1])
                    o_ += w
                for U in us[s]:
                    if U.get("after"):
                        U["after"](t)
                assert o_ <= 512
                X.update(S=S, i=i, w=o_)
                ds, es = [], []
                for U in us[s]:
                    c, w = U["at"], U["w"]
                    ds.append(dve.do(lambda e: e.tensor_tensor_reduce(
                        S[:, c:c + w], bank[:, c:c + w], U["table"], -U["scale"], U.get("init", BIG),
                        ALU.add, ALU.min, U["nm"]), t, f, U.get("tt")))
                PB.give(b, ds[-1])
                for U, d in zip(us[s], ds):
                    c, w = U["at"], U["w"]
                    es.append(act.do(lambda e: e.activation(
                        S[:, c:c + w], S[:, c:c + w], ACT.Exp, bias=U["nm"], scale=-1.0, accum_out=U["sm"]), d))
                X["es"] = es
                if us[s][0].get("extra"):
                    X["x"] = us[s][0]["extra"](us[s], es, ds)
            if 0 <= s - 1 < n:
                X, B = st_[s - 1], us[s - 1]
                S, w, nh = X["S"], X["w"], len(B)
                sm_, rs_ = B[0]["sms"](nh), B[0]["rss"](nh)
                d = dve.do(lambda e: e.reciprocal(rs_, sm_), X["es"], X.get("x"), B[0].get("rst"))
                if B[0].get("gate"):
                    g_, gt = B[0]["gate"](nh)
                    d = dve.do(lambda e: e.tensor_tensor(rs_, rs_, g_, ALU.mult), d, gt)
                X["p"] = dve.do(lambda e: e.tensor_tensor(
                    S[:, 0:w].rearrange("p (h k) -> p h k", h=nh), S[:, 0:w].rearrange("p (h k) -> p h k", h=nh),
                    rs_.unsqueeze(2).broadcast_to([128, nh, w // nh]), ALU.mult), d)
            if 0 <= s - 5 < n:
                X = st_[s - 5]
                for U in us[s - 5]:
                    if U.get("open"):
                        U["open"]()
                    vs, o_ = U["v"](), U["o"]()
                    add = U.get("add", False)
                    for j, v in enumerate(vs):
                        c = U["at"] + j * 128
                        t = pe.do(lambda e: e.matmul(o_, v, X["PT"][:, c:c + 128], start=j == 0 and not add,
                                                     stop=j == len(vs) - 1, skip_group_check=add),
                                  X["p"], U["vt"](), U["ot"](), mark=j == len(vs) - 1)
                    U["t"] = t
                PTr.give(X["pi"], t)
                for U in us[s - 5]:
                    if U.get("done"):
                        U["done"](U["t"])

    def batches(us):
        res = []
        for U in us:
            L_ = res[-1][-1] if res else None
            if res and (U["row"], U["w"]) == (L_["row"], L_["w"]) and (len(res[-1]) + 1) * U["w"] <= 512:
                res[-1].append(U)
            else:
                res.append([U])
        return res

    def split_out(oT, bank, qt, *toks):
        return split(oT[:, 0, :, qt * 128:(qt + 1) * 128], oT[:, 1, :, qt * 128:(qt + 1) * 128],
                     bank[:].rearrange("p (c t) -> p c t", c=4), oT_free[0], *toks)

    def head_out(bank, h):
        return bank[64 * (h % 2):64 * (h % 2) + 64, (h // 2) * 128:(h // 2) * 128 + 128]

    def columns(base, h, step):
        return lambda n: st[:, base + h:base + h + step * (n - 1) + 1:step]

    oT_free = [None]
    S_NM, S_SM, S_RS = 0, 32, 64
    nm = lambda i: st[:, S_NM + i:S_NM + i + 1]
    sm = lambda i: st[:, S_SM + i:S_SM + i + 1]

    def project(name, m, xs, dst, *free, view=lambda a: a, M=128):
        return evacuate(PB, *dense([(name, m, 0, list(range(8)))], xs, M), dst, *free, view=view, M=M)

    def evacuate(ring, b, bank, tok, dst, *free, view=lambda a: a, M=128):
        res = []

        def fn():
            r_ = view(rstd[0:M, :])
            d = dve.do(lambda e: e.tensor_tensor(dst, view(bank[0:M, :]), r_, ALU.mult), tok, rf_tok[0], *free)
            ring.give(b, d)
            res.append(d)
        if factor_due[0]:
            late.append(fn)
        else:
            fn()
        return res

    def tokens_first(name, ncol, per, xs, dst, *free, toks_of=None, nk=8, by=None):
        if toks_of is None:
            toks_of = lambda a, t: a[:, t * 128:(t + 1) * 128]
        bs = [OB.take() for _ in range(4)]
        for k0 in range(0, nk, per):
            u, wh, wl, wt = unit(name, 0, k0 * ncol, per * ncol)
            for j in range(per):
                xh, xl, xt = xs(k0 + j)
                for t in range(4):
                    last = j == per - 1 and t == 3
                    o_ = bs[t][1][:, 0:ncol]
                    s, e_ = k0 + j == 0, k0 + j == nk - 1
                    a, b_ = wh[:, j * ncol:(j + 1) * ncol], wl[:, j * ncol:(j + 1) * ncol]
                    hh, hl = toks_of(xh, t), toks_of(xl, t)
                    pe.do(lambda e, o_=o_, hh=hh, a=a, s=s: e.matmul(o_, hh, a, start=s, stop=False),
                          wt, xt, bs[t][2], mark=False)
                    pe.do(lambda e, o_=o_, hh=hh, b_=b_: e.matmul(o_, hh, b_, start=False, stop=False), mark=False)
                    tok = pe.do(lambda e, o_=o_, hl=hl, a=a, e_=e_: e.matmul(o_, hl, a, start=False, stop=e_))
                    if e_:
                        if by is None:
                            d = act.do(lambda e, t=t, o_=o_: e.copy(dst(t), o_), tok, *free)
                        else:
                            d = act.do(lambda e, t=t, o_=o_: e.activation(dst(t), o_, ACT.Copy, scale=by[0][:, t:t + 1]),
                                       tok, by[1], *free)
                        OB.give(bs[t][0], d)
            freed[u] = tok
            stage()
        return d

    xt = x_toks
    ht = []
    for c in range(KC):
        ht.append(gained(0, c, xt[c]))
        if c == 0 and seq is not None:
            part(0)
        acc_tok[0], r = square_in(xT[:, c, :], c == 0, xt[c])
    factor()

    rope_done = []

    rope_tok = []

    def rope_tables():
        pi_ = at([128, T], RA + 64 * K, I32)
        pf = at([128, T], RA + 66 * K)
        ang = at([128, T], RA + 68 * K)
        y = at([128, T], RA + 70 * K)
        ki = at([128, T], RA + 72 * K, I32)
        kf = at([128, T], RA + 74 * K)
        r = [at([128, T], RA + (76 + 2 * i) * K) for i in range(4)]
        a = load(pi_[:], D["positions"].partition_broadcast(128), now())
        yield
        a = dve.do(lambda e: e.tensor_copy(pf[:], pi_[:]), a)
        x = None
        done = []
        for w in range(2):
            ang_t = dve.do(lambda e, w=w: e.tensor_scalar(ang[:], pf[:], cn("invf")[:, w:w + 1], None, ALU.mult),
                           a, c_tok, x)
            for j, (frac, ph) in enumerate(((0.25, float(np.pi / 2)), (0.0, 0.0))):
                d = r[2 * w + j]
                x = dve.do(lambda e, frac=frac: e.tensor_scalar(y[:], ang[:], float(1 / (2 * np.pi)), frac,
                                                               ALU.mult, ALU.add), ang_t, x)
                x = dve.do(lambda e: e.tensor_copy(ki[:], y[:]), x)
                x = dve.do(lambda e: e.tensor_copy(kf[:], ki[:]), x)
                yield
                c1, c2, c3 = 6.28125, 0.0019340515136718750, float(2 * np.pi - 6.28125 - 0.0019340515136718750)
                x = dve.do(lambda e: e.scalar_tensor_tensor(y[:], kf[:], -c1, ang[:], ALU.mult, ALU.add), x)
                x = dve.do(lambda e: e.scalar_tensor_tensor(y[:], kf[:], -c2, y[:], ALU.mult, ALU.add), x)
                x = dve.do(lambda e: e.scalar_tensor_tensor(y[:], kf[:], -c3, y[:], ALU.mult, ALU.add), x)
                x = dve.do(lambda e, ph=ph: e.tensor_scalar(y[:], y[:], ph, 3.1415925, ALU.add, ALU.min), x)
                x = dve.do(lambda e: e.tensor_scalar(d[:], y[:], -3.1415925, None, ALU.max), x)
                done.append(x)
                yield
        for i, d in enumerate(r):
            x = act.do(lambda e: e.activation(d[:], d[:], ACT.Sin), done[i])
            if i % 2:
                x = dve.do(lambda e: e.tensor_scalar(d[:], d[:], cn("sgn")[:, i // 2:i // 2 + 1], None, ALU.mult), x)
            elif i == 2:
                x = dve.do(lambda e: e.memset(d[0:64, :], 1.0), x)
            rope_tok.append(load(D["rope"][i], d[:], x))
            rope_done.append(rope_tok[-1])

    xs = ffn("f1", ht, hook=rope_tables())
    post, ft = add_post(now())
    down("f1_d", FC, xs, post, early=True)
    xt, ht = postnorm(lambda c: gh[:, 0, c:c + 1], ft, xt, 2, n=8)

    H = hs(ht)
    fr = now()
    oa = at([128, 2, 4, T], RA, F32R)
    qa = at([128, 4, T], RA + 16 * K)
    ka = at([128, 4, T], RA + 24 * K)
    va = at([128, 4, T], RA + 32 * K)
    rp = at([120, 127], RA + 72 * K)
    BT = [at([128, 14, 64], RA + 40 * K + i * 3584) for i in range(8)]
    z = dve.do(lambda e: e.memset(rp[:], 0.0), fr, rope_done)
    z = load(rp[:, 48:79], D["rpb"], z)
    z = load(D["rpbs"].ap().rearrange("(a c b) -> a c b", b=127, c=64),
             rp[:].unsqueeze(1).broadcast_to([120, 64, 127]), z)
    qt_, kt_ = [], []
    for m, r in enumerate(dense4([("qka", m) for m in range(4)], H)):
        qt_.append(evacuate(OB, *r, qa[:, m, :], fr))
    for m in range(4):
        kt_.append(project("qka", 4 + m, H, ka[:, m, :], fr))
    v_t = tokens_first("va", 512, 2, H, lambda t: va[:, t, :], fr, by=(nv, nv_tok[0]))
    ob4 = {}
    bt_ = {}

    def na_table(h):
        bt = BT[h]
        w = []
        for a in range(2):
            src = bass.AP(D["rpbs"], (h * 15 + (1 - a)) * 8128 + 63, [[126, 64], [8128, 14], [1, 64]])
            w.append(load(bt[64 * a:64 * a + 64, :, :], src, z, fr))
        return w

    def na_mask(h):
        bt = BT[h]
        bt_[h] = dve.do(lambda e: e.scalar_tensor_tensor(
            bt[:], bt[:], 8.0, cn("colmask").unsqueeze(1).broadcast_to([128, 14, 64]), ALU.mult, ALU.add),
            bt_w[h], c_tok)

    bt_w = [na_table(h) for h in range(8)]
    na_mask(0)
    na_us = []
    for h in range(8):
        for qt in range(4):
            p0 = 64 * (h % 2)

            def opn(h=h, qt=qt):
                if h == 0:
                    ob4[qt] = OB.take()

            def done(t, h=h, qt=qt):
                if h == 7:
                    w_ = split_out(oa, ob4[qt][1], qt, t)
                    OB.give(ob4[qt][0], *w_)
                    oa_t.extend(w_)

            na_us.append(dict(
                row=p0, w=512, q=lambda h=h, qt=qt, p0=p0: qa[p0:p0 + 64, h // 2, qt * 128:(qt + 1) * 128],
                k=lambda h=h, p0=p0: ka[p0:p0 + 64, h // 2, :], qk=lambda h=h: [qt_[h // 2], kt_[h // 2]],
                scale=0.125, nm=nm(qt * 8 + h), sm=sm(qt * 8 + h), open=opn, done=done,
                sms=columns(S_SM, qt * 8 + h, 1), rss=columns(S_RS, qt * 8 + h, 1),
                v=lambda h=h: [va[:, j, h * 64:(h + 1) * 64] for j in range(4)], vt=lambda: v_t,
                o=lambda h=h, qt=qt: head_out(ob4[qt][1], h), ot=lambda qt=qt: ob4[qt][2]))

            def setup(U=na_us[-1], h=h, qt=qt):
                if qt == 1 and h < 7:
                    na_mask(h + 1)
                U["table"] = BT[h][:, 6 - 2 * qt:14 - 2 * qt, :].rearrange("p j k -> p (j k)")
                U["tt"] = bt_[h]
            na_us[-1]["pre"] = setup
    oa_t = []
    oT_free[0] = fr
    attend(batches(na_us))

    fr = now()
    obf = at([128, 6, T], RA + 40 * K)
    tb = at([128, 4, 640], RA + 52 * K)
    stm = at([4, 6, T], RA + 62 * K)
    tb_t = load(tb[:], D["dil"], fr)

    def perm_tile(a, g, t):
        if g == 0:
            return a[:, t * 128:(t + 1) * 128]
        return a.rearrange("p (l r) -> p r l", r=4)[:, t, :]

    def perm_all(a, g):
        return a if g == 0 else a.rearrange("p (l r) -> p r l", r=4)

    def shaped(a, g):
        return a if g == 0 else a.rearrange("p (r l) -> p r l", r=4)

    stm_t = []
    obf_t = []
    for g in range(3):
        o0 = RA + 16 * K + (g % 2) * 12 * K
        qg = at([128, 2, T], o0)
        kg = at([128, 2, T], o0 + 4 * K)
        vg = at([128, 4, 256], o0 + 8 * K)
        frg = fr if g < 2 else now()
        qt_ = [project("qb", 2 * g + c, H, shaped(qg[:, c, :], g), frg, view=lambda a, g=g: perm_all(a, g))
               for c in range(2)]
        kt_ = [project("kb", 2 * g + c, H, shaped(kg[:, c, :], g), frg, view=lambda a, g=g: perm_all(a, g))
               for c in range(2)]
        v_t = tokens_first(f"vb{g}", 256, 4, H, lambda t: vg[:, t, :], frg, toks_of=lambda a, t, g=g: perm_tile(a, g, t),
                           by=(nv[:, 4 * (g > 0):4 * (g > 0) + 4], nv_tok[0]))
        us = []
        obk = {}
        order = [(t, hh) for t in range(4) for hh in (0, 2, 1, 3)]
        if g > 0:
            order = [(t, hh) for t2 in (0, 2) for par in (0, 1) for t in (t2, t2 + 1) for hh in (par, par + 2)]
        seen = {}

        def dil_cols(base, g, t, hh):
            return lambda n: st[:, base + 4 * t + hh:base + 4 * t + hh + 2 * (n - 1) + 1:2]

        for t, hh in order:
            if True:
                if g == 0:
                    a, b = max(0, t - 1), min(4, t + 2)
                    tab = tb[:, hh, (a - t + 1) * 128:(b - t + 1) * 128]
                else:
                    a, b = t, t + 1
                    tab = tb[:, hh, 256 + g * 128:384 + g * 128]
                p0 = 64 * (hh % 2)

                def opn(t=t, hh=hh):
                    if t not in obk:
                        obk[t] = OB.take()

                def done(tok, t=t, hh=hh, g=g, obk=obk, seen=seen):
                    seen[t] = seen.get(t, 0) + 1
                    if seen[t] < 4:
                        return
                    for c in range(2):
                        o_ = perm_tile(obf[:, 2 * g + c, :], g, t)
                        a_ = act.do(lambda e: e.copy(o_, obk[t][1][:, c * 128:(c + 1) * 128]), tok, fr)
                    OB.give(obk[t][0], a_)
                    obf_t.append(a_)
                    b, bk, bt = PB.take()
                    for k_, s0 in ((0, S_NM), (1, S_SM)):
                        tk = pe.do(lambda e, k_=k_, s0=s0: e.transpose(
                            bk[0:4, k_ * 128:(k_ + 1) * 128], st[:, s0 + 4 * t:s0 + 4 * t + 4], cn("ident")), bt,
                            now())
                    for k_ in range(2):
                        o_ = perm_tile(stm[:, 2 * g + k_, :], g, t)
                        s_ = bk[0:4, k_ * 128:(k_ + 1) * 128]
                        a_ = act.do(lambda e, o_=o_, s_=s_: e.copy(o_, s_), tk, fr)
                    PB.give(b, a_)
                    stm_t.append(a_)

                us.append(dict(
                    row=p0, w=(b - a) * 128, q=lambda t=t, hh=hh, p0=p0, qg=qg: qg[p0:p0 + 64, hh // 2, t * 128:(t + 1) * 128],
                    k=lambda a=a, b=b, hh=hh, p0=p0, kg=kg: kg[p0:p0 + 64, hh // 2, a * 128:b * 128],
                    qk=lambda hh=hh, qt_=qt_, kt_=kt_: [qt_[hh // 2], kt_[hh // 2]], scale=0.125, table=tab, tt=tb_t,
                    nm=nm(4 * t + hh), sm=sm(4 * t + hh), open=opn, done=done,
                    v=lambda a=a, b=b, hh=hh, vg=vg: [vg[:, j, hh * 64:(hh + 1) * 64] for j in range(a, b)],
                    vt=lambda v_t=v_t: v_t, o=lambda t=t, hh=hh, obk=obk: head_out(obk[t][1], hh),
                    sms=dil_cols(S_SM, g, t, hh), rss=dil_cols(S_RS, g, t, hh),
                    ot=lambda t=t, obk=obk: obk[t][2]))
        attend(batches(us))

    fr0 = now()
    w = at([128, T], RA + 76 * K)[0:4, :]
    al = []

    def shares(a=None):
        a = dve.do(lambda e: e.tensor_tensor(w, stm[:, 0, :], stm[:, 2, :], ALU.min), stm_t, fr0)
        a = dve.do(lambda e: e.tensor_tensor(w, w, stm[:, 4, :], ALU.min), a)
        c = []
        for g in range(3):
            b = dve.do(lambda e, g=g: e.tensor_tensor(stm[:, 2 * g, :], w, stm[:, 2 * g, :], ALU.subtract), a)
            c.append(act.do(lambda e, g=g: e.activation(stm[:, 2 * g, :], stm[:, 2 * g, :], ACT.Exp), b))

        def sums():
            for g in range(3):
                b = dve.do(lambda e, g=g: e.tensor_tensor(stm[:, 2 * g + 1, :], stm[:, 2 * g, :],
                                                          stm[:, 2 * g + 1, :], ALU.mult), c[g])
            a = dve.do(lambda e: e.tensor_tensor(w, stm[:, 1, :], stm[:, 3, :], ALU.add), b)
            a = dve.do(lambda e: e.tensor_tensor(w, w, stm[:, 5, :], ALU.add), a)
            a = dve.do(lambda e: e.reciprocal(w, w), a)
            for g in range(3):
                al.append(dve.do(lambda e, g=g: e.tensor_tensor(stm[:, 2 * g + 1, :], stm[:, 2 * g + 1, :], w,
                                                                ALU.mult), a))
        turns.append(sums)
    turns.append(shares)
    def merge(mg, fr, branches, H, before=None):
        toks = []
        for m in range(KC):
            acc_i = None
            for n, (gname, g0, parts, xs_) in enumerate(branches):
                bg, gb, tg = dense([(gname, g0 + m, 0, list(range(8)))], H)
                if before is not None and m == 0 and n == 1:
                    before()
                    fr = now()
                bo, bb, to = dense([(nm_, m, c0, ch) for nm_, c0, ch in parts], xs_)
                i, s, f = tmp.take()
                d = sigmul(s[:], gb, bb[:], tg, to, f, gate_free=lambda a, bg=bg: PB.give(bg, a))
                PB.give(bo, d)
                if acc_i is None:
                    acc_i, s0 = i, s
                else:
                    d = dve.do(lambda e, s=s, s0=s0: e.tensor_tensor(s0[:], s0[:], s[:], ALU.add), d)
                    tmp.give(i, d)
            hi = mg[:, 0, m, :]
            a = act.do(lambda e: e.activation(hi, s0[:], ACT.Copy, scale=0.5), d, fr)
            w_ = [a, dve.do(lambda e: e.scalar_tensor_tensor(mg[:, 1, m, :], s0[:], 0.5, hi.bitcast(F32), ALU.mult,
                                                             ALU.subtract), a, d, fr)]
            tmp.give(acc_i, *w_)
            toks.append(w_)
        return lambda c: (mg[:, 0, c, :], mg[:, 1, c, :], toks[c])

    fr = now()
    ob = at([128, 2, 6, T], RA + 16 * K, F32R)
    ob_t = []

    def weigh():
        two = Ring([at([128, T], RA + (74 + 2 * n) * K) for n in range(2)])
        two.last = [fr, [fr, al]]
        for c6 in range(6):
            b, bank, bt = OB.take()
            t = pe.do(lambda e, c6=c6, bank=bank: e.matmul(
                bank[:], cn("sel")[0:4, (c6 % 2) * 128:(c6 % 2 + 1) * 128], stm[:, 2 * (c6 // 2) + 1, :],
                start=True, stop=True), bt, al, c_tok)
            i, s, f = two.take()
            d = dve.do(lambda e, c6=c6, s=s, bank=bank: e.tensor_tensor(s[:], bank[:], obf[:, c6, :], ALU.mult),
                       t, f, obf_t)
            OB.give(b, d)
            wv = split(ob[:, 0, c6, :], ob[:, 1, c6, :], s[:], d, fr)
            two.give(i, *wv)
            ob_t.append(wv)

    mg = at([128, 2, KC, T], RA + 40 * K, F32R)
    xs = merge(mg, fr, [
        ("ga", 0, [("bra", 0, list(range(4)))], lambda c: (oa[:, 0, c, :], oa[:, 1, c, :], oa_t)),
        ("gb", 0, [("brb", 0, list(range(6)))], lambda c: (ob[:, 0, c, :], ob[:, 1, c, :], ob_t[c]))], H, before=weigh)
    post, ft = add_post(now())
    down("wo", KC, xs, post, early=True)
    xt, ht = postnorm(lambda c: gn[:, 3, c:c + 1], ft, xt, 4)
    xs = ffn("f2", ht, wide=True)
    post, ft = add_post(now())
    down("f2_d", FC, xs, post, early=True)
    xt, ht = postnorm(lambda c: gh[:, 1, c:c + 1], ft, xt, 6)

    def rope(src_bank, b, tok, dst, M, cs, sn, permn, tr, *free, normed=True):
        iy, y, fy = tmp.take()
        if normed:
            a = times_rstd(y[0:M, :], src_bank[0:M, :], tok, fy)
        else:
            a = act.do(lambda e: e.copy(y[0:M, :], src_bank[0:M, :]), tok, fy)
        PB.give(b, a)
        res = []

        def turn():
            b2, bk2, bt2 = PB.take()
            t = pe.do(lambda e: e.matmul(bk2[0:M, :], cn(permn)[0:M, :], y[0:M, :], start=True, stop=True),
                      bt2, a, c_tok)
            ir, r, f_r = tmp.take()
            d1 = dve.do(lambda e: e.tensor_tensor(r[0:M, :], bk2[0:M, :], sn[0:M, :], ALU.mult), t, f_r, tr)
            PB.give(b2, d1)
            d2 = pool.do(lambda e: e.tensor_tensor(y[0:M, :], y[0:M, :], cs[0:M, :], ALU.mult), a, t, tr)
            if callable(dst):
                d = dve.do(lambda e: e.tensor_tensor(r[0:M, :], y[0:M, :], r[0:M, :], ALU.add), d1, d2)
                w_ = dst(r, d)
                tmp.give(ir, *w_)
                tmp.give(iy, d)
                res.extend(w_)
            else:
                d = dve.do(lambda e: e.tensor_tensor(dst, y[0:M, :], r[0:M, :], ALU.add), d1, d2, *free)
                tmp.give(ir, d)
                tmp.give(iy, d)
                res.append(d)
        turns.append(turn)
        return res

    def causal_units(qf, kf, qk, vf, vt, obank, hq, h, qt, scale, col, **kw):
        w = (qt + 1) * 128
        return dict(w=w, q=qf, k=kf, qk=qk, scale=scale, table=cn("causal")[:, 384 - qt * 128:512], tt=c_tok,
                    nm=nm(col), sm=sm(col), v=vf, vt=vt, **kw)

    for L in range(2):
        H = hs(ht)
        fr = now()
        s_ = str(L)
        oc = at([128, 2, 4, T], RA, F32R)
        ob = at([128, 2, 4, T], RA + 16 * K, F32R)
        oa = at([128, 2, 4, T], RA + 32 * K, F32R)
        rt_ = at([128, 4, T], RA + 48 * K)
        r_t = [load(rt_[:, i, :], D["rope"][i], fr, rope_tok[i]) for i in range(4)]
        cl = at([128, 2, 4, T], RA + 16 * K, F32R)
        cv = at([128, 4, T], RA + 32 * K)
        qf = Ring([at([96, T], RA + (40 + 2 * i) * K) for i in range(4)])
        kf = Ring([at([96, T], RA + (56 + 2 * i) * K) for i in range(4)])
        cf = at([128, 4, T], RA)
        rs2 = at([128, 2, T], RA + 8 * K)
        va = at([128, 4, 408], RA + 71 * K)
        kb = at([128, 2, T], RA + 64 * K)
        clt = [None] * 4
        ct = []

        def latent(n):
            sumsq([cf[:, 2 * n + c, :] for c in range(2)], ct[2 * n:2 * n + 2])
            first, second, got = rms(256, acc_tok[0], rs2[:, n, :], fr)

            def last():
                second()
                clt[2 * n:2 * n + 2] = scaled(
                    [cf[:, 2 * n + c, :] for c in range(2)], lambda p, c: cl[:, p, 2 * n + c, :],
                    lambda c: gcn[:, 4 * L + 2 * n + c:4 * L + 2 * n + c + 1], rs2[:, n, :], got[0],
                    ct[2 * n:2 * n + 2], fr)
            steps.extend([first, last])

        def roped(name, m, dst, M=128, fr=fr):
            b, bank, tok = dense([(name, m, 0, list(range(8)))], H, M)
            res = []

            def fn():
                if M == 96:
                    res.append(rope(bank, b, tok, dst, 96, rt_[:, 2, :], rt_[:, 3, :], "permc", r_t[2:4], fr))
                else:
                    res.append(rope(bank, b, tok, dst, 128, rt_[:, 0, :], rt_[:, 1, :], "perm", r_t[0:2], fr))
            if factor_due[0]:
                late.append(fn)
            else:
                fn()
            return res

        if L == 0:
            for m, r in enumerate(dense4([("clat" + s_, m) for m in range(4)], H)):
                ct.append(evacuate(OB, *r, cf[:, m, :], fr))
        else:
            for m in range(4):
                ct.append(project("clat" + s_, m, H, cf[:, m, :], fr))

        def kpe(r, d):
            return [dve.do(lambda e, i=i: e.tensor_copy(kf.bufs[i][64:96, :], r[64:96, :]), d, fr)
                    for i in range(4)]
        kp_t = roped("kpe" + s_, 0, kpe, 96)
        kb_t = [roped("kb2" + s_, 0, kb[:, 0, :])]
        latent(1)
        kb_t.append(roped("kb2" + s_, 1, kb[:, 1, :]))
        latent(0)
        v2_t = tokens_first("v2" + s_, 408, 2, H, lambda t: va[:, t, :], fr, by=(nv, nv_tok[0]))
        CX = lambda n: (lambda c: (cl[:, 0, 2 * n + c, :], cl[:, 1, 2 * n + c, :], clt[2 * n + c]))
        v_t = tokens_first("cv" + s_, 512, 2, CX(1), lambda t: cv[:, t, :], fr, nk=2)
        hd = {}
        ob4 = {}
        us = []

        def head_in(h):
            if h % 2 == 0:
                hd["u"] = unit("cup" + s_, h // 2, 0, 640)
            u, wh, wl, wt = hd["u"]
            c0 = 320 * (h % 2)
            res = []
            for n, M in ((0, 96), (1, 64)):
                b, bank, bt = PB.take()
                for c in range(2):
                    xh, xl, xt_ = CX(n)(c)
                    a_ = c0 + 192 * n + c * M
                    tok = mm3(bank[0:M, :], wh[:, a_:a_ + M], wl[:, a_:a_ + M], xh, xl, c == 0, c == 1,
                              wt, xt_, bt)(c == 1)
                res.append((b, bank, tok))
            freed[u] = tok
            iq, q_, fq = qf.take()
            ik, k_, fk = kf.take()
            b, bank, tok = res[1]
            kt = act.do(lambda e: e.copy(k_[0:64, :], bank[0:64, :]), tok, fk, fr)
            PB.give(b, kt)
            b, bank, tok = res[0]
            qt2 = rope(bank, b, tok, q_[:], 96, rt_[:, 2, :], rt_[:, 3, :], "permc", r_t[2:4], fq, fr,
                       normed=False)
            hd[h] = (iq, q_, ik, k_, [kt, qt2, kp_t])

        oc_t = []
        oT_free[0] = fr
        for h, qt in [(2 * hp + j, qt) for hp in range(4) for qt in range(4) for j in range(2)]:
            if True:
                def pre(h=h, qt=qt):
                    if h < 2 and qt == 0:
                        head_in(h)
                        if h == 1:
                            turned()
                    if qt == 2 and h < 6:
                        head_in(h + 2)

                def after(t, h=h, qt=qt):
                    if qt == 3:
                        qf.give(hd[h][0], t)
                        kf.give(hd[h][2], t)

                def opn(h=h, qt=qt):
                    if h == 0:
                        ob4[qt] = OB.take()

                def done(t, h=h, qt=qt):
                    if h == 7:
                        w_ = split_out(oc, ob4[qt][1], qt, t)
                        OB.give(ob4[qt][0], *w_)
                        oc_t.extend(w_)
                us.append(causal_units(
                    lambda h=h, qt=qt: hd[h][1][:, qt * 128:(qt + 1) * 128],
                    lambda h=h, qt=qt: hd[h][3][:, 0:(qt + 1) * 128], lambda h=h: hd[h][4],
                    lambda h=h, qt=qt: [cv[:, j, h * 64:(h + 1) * 64] for j in range(qt + 1)],
                    lambda: v_t, None, None, h, qt, float(96 ** -0.5), qt * 8 + h, row=0, pre=pre,
                    after=after, sms=columns(S_SM, qt * 8 + h, 1), rss=columns(S_RS, qt * 8 + h, 1), open=opn, done=done,
                    o=lambda h=h, qt=qt: head_out(ob4[qt][1], h), ot=lambda qt=qt: ob4[qt][2]))
        attend(batches(us))

        fr = now()
        qb = at([128, 4, T], RA + 56 * K)
        snk = st[:, 136:144]
        nsk = st[:, 144:152]
        esk = st[:, 96:128]
        s_t = load(snk, D["sinks"][L], fr)
        s_t = dve.do(lambda e: e.tensor_scalar(nsk, snk, -1.0, None, ALU.mult), s_t)
        v_t = v2_t
        kt_ = kb_t
        qt_ = [roped("qb2" + s_, m, qb[:, m, :], fr=fr) for m in range(4)]
        kw_ = at([128, 2, T], RA + 52 * K)
        kw_t = [roped("ks" + s_, 2, kw_[:, 0, :], fr=fr)]
        us = []
        obk = {}
        ob_t = []
        oT_free[0] = fr
        for qt in range(4):
            for h in (0, 2, 4, 6, 1, 3, 5, 7):
                a = max(0, qt - 1)
                p0 = 64 * (h % 2)

                def opn(qt=qt, h=h):
                    if h == 0:
                        obk[qt] = OB.take()

                def done(tok, qt=qt, h=h):
                    if h != 7:
                        return
                    w_ = split_out(ob, obk[qt][1], qt, now())
                    OB.give(obk[qt][0], *w_)
                    ob_t.extend(w_)

                def extra(batch, es, ds, qt=qt, h=h):
                    n = len(batch)
                    c = qt * 8 + h
                    col = lambda a: a[:, c:c + 2 * n - 1:2]
                    x = dve.do(lambda e: e.tensor_tensor(col(esk), snk[:, h:h + 2 * n - 1:2], col(st), ALU.add), ds)
                    x = act.do(lambda e: e.activation(col(esk), col(esk), ACT.Exp), x)
                    sm_ = columns(S_SM, c, 2)(n)
                    return dve.do(lambda e: e.tensor_tensor(sm_, sm_, col(esk), ALU.add), x, es)

                us.append(dict(
                    row=p0, w=(qt + 1 - a) * 128, q=lambda qt=qt, h=h, p0=p0: qb[p0:p0 + 64, h // 2, qt * 128:(qt + 1) * 128],
                    k=lambda qt=qt, a=a, h=h, p0=p0: kb[p0:p0 + 64, h // 4, a * 128:(qt + 1) * 128],
                    qk=lambda h=h: [qt_[h // 2], kt_[h // 4]], scale=0.125,
                    table=cn("band")[:, (a - qt + 1) * 128:256], tt=[c_tok, s_t], init=nsk[:, h:h + 1],
                    nm=nm(qt * 8 + h), sm=sm(qt * 8 + h), open=opn, done=done,
                    v=lambda qt=qt, a=a, h=h: [va[:, j, 256 + (h // 4) * 64:320 + (h // 4) * 64]
                                               for j in range(a, qt + 1)],
                    vt=lambda: v_t, o=lambda qt=qt, h=h: head_out(obk[qt][1], h), extra=extra,
                    sms=columns(S_SM, qt * 8 + h, 2), rss=columns(S_RS, qt * 8 + h, 2),
                    ot=lambda qt=qt: obk[qt][2]))
        attend(batches(us))

        fr = now()
        k2 = [at([128, 2, 2, 560], RA + int(o_ * K), F32R) for o_ in (32, 59.25)]
        w2 = at([128, 2, 192], RA + 41 * K)
        pos = at([128, 2, 32], RA + 43 * K)
        kcm = at([128, 64], RA + 68 * K)
        hids = [at([128, 2, 2, 34], RA + 68 * K + 256), at([128, 2, 2, 34], RA + 44 * K)]
        bd = at([128, 2, 256], RA + 69 * K)
        w2_t = load(w2[:], D["w2"][L], fr)
        p_t = load(pos[:], D["cpos"][L], fr)
        bd_t = dve.do(lambda e: e.memset(bd[:], 0.0), fr)
        kt2 = [[], []]
        qq = at([128, 4, T], RA + 56 * K)
        ks = at([128, 2, T], RA + 64 * K)
        z = [dve.do(lambda e, K2=K2: e.memset(K2[:, :, :, 543:560].bitcast(F32), 0.0), fr) for K2 in k2]

        def keys(kv, g):
            K2 = k2[kv]

            def put(r, d):
                w_ = []
                for p0, sh in ((0, 0), (64, 1)):
                    w_ += split(K2[p0:p0 + 64, 0, g, 0:512 - sh], K2[p0:p0 + 64, 1, g, 0:512 - sh],
                                r[p0:p0 + 64, sh:512], d, fr)
                return w_
            if kv == 0:
                kt2[kv].append(roped("kc" + s_, g, put, fr=fr))
            else:
                b, bank, tok = dense([("kc" + s_, 2 + g, 0, list(range(8)))], H)
                i, r_, f = tmp.take()
                d = times_rstd(r_[:], bank[:], tok, f)
                PB.give(b, d)
                w_ = put(r_, d)
                tmp.give(i, *w_)
                kt2[kv] += w_
            for p0, sh in ((0, 0), (64, 1)):
                kt2[kv] += split(K2[p0:p0 + 64, 0, g, 512 - sh:544 - sh], K2[p0:p0 + 64, 1, g, 512 - sh:544 - sh],
                                 pos[p0:p0 + 64, kv, :], p_t, z)

        def squeeze(kv, j4, bb):
            u, wh, wl, wt = unit("cw1" + s_, kv, j4 * 1024, 1024)
            for jj in range(4):
                j = j4 * 4 + jj
                for ch in range(2):
                    o_ = bb[ch][1][:, 0:68].rearrange("p (g n) -> p g n", g=2)
                    xh, xl = (k2[kv][:, p, :, 2 * j:2 * j + 529:16] for p in range(2))
                    a_ = jj * 256 + ch * 128
                    tok = mm3(o_, wh[:, a_:a_ + 128], wl[:, a_:a_ + 128], xh, xl, j == 0, j == 15,
                              wt, kt2[kv], bb[ch][2])(True)
            freed[u] = tok
            return tok

        qt_ = []
        keys(0, 0)
        keys(0, 1)
        keys(1, 0)
        keys(1, 1)
        others = [[lambda: kw_t.append(roped("ks" + s_, 3, kw_[:, 1, :], fr=fr))],
                  [lambda: qt_.append(roped("qa2" + s_, 0, qq[:, 0, :], fr=fr))]]
        hid_t = []
        for kv in range(2):
            bb = [OB.take() for _ in range(2)]
            for j4 in range(4):
                tok = squeeze(kv, j4, bb)
                if j4 < len(others[kv]):
                    others[kv][j4]()
            i, xx, f = tmp.take()
            i2, yy, f2 = tmp.take()
            hb = st[:, 160 + 2 * kv:162 + 2 * kv]
            for ch in range(2):
                bank = bb[ch][1]
                x_ = xx[:, ch * 68:ch * 68 + 68]
                d = dve.do(lambda e: e.tensor_copy(hb[:, ch:ch + 1], bank[:, 32:33]), tok, dve_last())
                d = dve.do(lambda e: e.tensor_scalar(x_, bank[:, 0:68], hb[:, ch:ch + 1], None, ALU.add), d, f)
                OB.give(bb[ch][0], d)
            X_, Y_ = xx[:, 0:136], yy[:, 0:136]
            d = dve.do(lambda e: e.tensor_tensor(Y_, X_, X_, ALU.mult), d, f2)
            d = dve.do(lambda e: e.tensor_scalar(Y_, Y_, 0.044715, 1.0, ALU.mult, ALU.add), d)
            d = dve.do(lambda e: e.tensor_tensor(Y_, Y_, X_, ALU.mult), d)
            d = act.do(lambda e: e.activation(Y_, Y_, ACT.Tanh, scale=0.7978845608028654), d)
            d = dve.do(lambda e: e.tensor_scalar(Y_, Y_, 0.5, 0.5, ALU.mult, ALU.add), d)
            H_ = hids[kv][:].rearrange("p c g n -> p (c g n)")
            d = dve.do(lambda e: e.tensor_tensor(H_, Y_, X_, ALU.mult), d, fr)
            tmp.give(i, d)
            tmp.give(i2, d)
            hid_t.append(d)

        fr2 = now()
        fr = fr2
        qt_.append(roped("qa2" + s_, 1, qq[:, 1, :], fr=fr))
        b, bank, bt = PB.take()
        for ch in range(2):
            tok = pe.do(lambda e: e.matmul(
                bank[:, 0:64].rearrange("p (g n) -> p g n", g=2), w2[:, ch, 0:128],
                hids[0][:, ch, :, 0:32], start=ch == 0, stop=ch == 1), bt, hid_t[0], w2_t)
        kc_t = act.do(lambda e: e.copy(kcm[:], bank[:, 0:64]), tok, fr2)
        PB.give(b, kc_t)
        i3, hr, f3 = tmp.take()
        for ch in range(2):
            for g in range(2):
                c = (2 * ch + g) * 128
                d = dve.do(lambda e: e.tensor_copy(
                    hr[:, c:c + 128].rearrange("p (r n) -> p r n", r=4),
                    hids[1][:, ch, g, 0:32].unsqueeze(1).broadcast_to([128, 4, 32])), hid_t[1], f3)
        qt_ += [roped("qa2" + s_, m, qq[:, m, :], fr=fr) for m in (2, 3)]
        for g in range(2):
            b, bank, bt = PB.take()
            for ch in range(2):
                lh = hr[:, (2 * ch + g) * 128:(2 * ch + g + 1) * 128]
                tok = pe.do(lambda e: e.matmul(
                    bank[:, 0:64], lh, w2[:, ch, 128:192], start=ch == 0, stop=ch == 1), bt, d, w2_t)
            for r in range(4):
                vc_t = act.do(lambda e: e.copy(
                    bd[32 * r:32 * r + 32, g, 64 * r:64 * r + 64], bank[32 * r:32 * r + 32, 0:64]), tok, bd_t)
            PB.give(b, vc_t)
        tmp.give(i3, tok)
        ks_t = [roped("ks" + s_, m, ks[:, m, :], fr=fr) for m in range(2)]
        sg = at([128, 4, 24], RA + 45 * K)
        sgt = act.do(lambda e: e.activation(sg[:], va[:, :, 384:408], ACT.Tanh, scale=0.5), fr, v_t)
        sgs = at([128, 4, 24], RA + 77 * K + 512)
        sgt = dve.do(lambda e: e.tensor_scalar(sgs[:], sg[:], 0.5, 0.5, ALU.mult, ALU.add), sgt, fr)
        oT_free[0] = [sgt, fr]
        oa_t = []
        us = []
        obk = {}
        cmp_ = {}
        for qt in range(4):
            for kind in range(2):
                for h in (0, 2, 4, 6, 1, 3, 5, 7):
                    p0 = 64 * (h % 2)
                    kk, kkt = (ks, ks_t) if kind == 0 else (kw_, kw_t)
                    col = kind * 8 + h + 16 * (qt % 2)

                    def cmp_scores(qt=qt):
                        b, bank, bt = PB.take()
                        tok = None
                        for h in (0, 2, 4, 6, 1, 3, 5, 7):
                            p0 = 64 * (h % 2)
                            tok = pe.do(lambda e, h=h, p0=p0: e.matmul(
                                bank[:, h * 32:h * 32 + 32], qq[p0:p0 + 64, h // 2, qt * 128:(qt + 1) * 128],
                                kcm[p0:p0 + 64, (h // 4) * 32:(h // 4) * 32 + 32], start=True, stop=True),
                                bt, qt_[h // 2], kc_t, tok if h == 1 else None)
                        i, S, f = tmp.take()
                        S3 = S[:, 0:256].rearrange("p (h n) -> p h n", h=8)
                        mk = cn("cmpneg")[:, qt * 32:qt * 32 + 32].unsqueeze(1).broadcast_to([128, 8, 32])
                        m01 = cn("cmp01")[:, qt * 32:qt * 32 + 32].unsqueeze(1).broadcast_to([128, 8, 32])
                        d = dve.do(lambda e: e.scalar_tensor_tensor(
                            S3, bank[:, 0:256].rearrange("p (h n) -> p h n", h=8), 0.125, mk, ALU.mult, ALU.add),
                            tok, f, c_tok)
                        PB.give(b, d)
                        mx, sx = st[:, 168:176], st[:, 176:184]
                        d = dve.do(lambda e: e.tensor_reduce(mx, S3, AX, ALU.max), d)
                        d = dve.do(lambda e: e.tensor_tensor(S3, S3, mx.unsqueeze(2).broadcast_to([128, 8, 32]),
                                                             ALU.subtract), d)
                        d = act.do(lambda e: e.activation(S[:, 0:256], S[:, 0:256], ACT.Exp), d)
                        x = dve.do(lambda e: e.tensor_reduce(sx, S3, AX, ALU.add), d)
                        x = dve.do(lambda e: e.reciprocal(sx, sx), x)
                        x = dve.do(lambda e: e.tensor_tensor(sx, sx, sgs[:, qt, 0:24:3], ALU.mult), x, sgt)
                        d = dve.do(lambda e: e.tensor_tensor(S3, S3, m01, ALU.mult), x)
                        d = dve.do(lambda e: e.tensor_tensor(S3, S3, sx.unsqueeze(2).broadcast_to([128, 8, 32]),
                                                             ALU.mult), d)
                        cmp_[qt] = (i, S, d)

                    def cmp_turn(qt=qt):
                        i, S, d = cmp_[qt]
                        b, bank2, bt = PB.take()
                        for g in range(2):
                            tok = pe.do(lambda e, g=g: e.transpose(bank2[:, g * 128:(g + 1) * 128],
                                                                   S[:, g * 128:(g + 1) * 128], cn("ident")), bt, d)
                        tmp.give(i, tok)
                        ip, PT, f = tmp.take()
                        d = dve.do(lambda e: e.tensor_copy(PT[:, 0:256], bank2[:, 0:256]), tok, f)
                        PB.give(b, d)
                        cmp_[qt] = (ip, PT, d)

                    def cmp_values(qt=qt):
                        ip, PT, d = cmp_[qt]
                        ob_ = OB.take()
                        for g in range(2):
                            for c in range(2):
                                ch = 2 * g + c
                                tok = pe.do(lambda e: e.matmul(
                                    ob_[1][:, ch * 128:(ch + 1) * 128], bd[:, g, c * 128:(c + 1) * 128],
                                    PT[:, g * 128:(g + 1) * 128], start=ch == 0, stop=ch == 3,
                                    skip_group_check=True), d, ob_[2], vc_t)
                        tmp.give(ip, tok)
                        obk[qt] = ob_

                    def opn(qt=qt, kind=kind, h=h, f_=cmp_values):
                        if h == 0 and kind == 0:
                            f_()

                    def pre(qt=qt, kind=kind, h=h, f_=cmp_scores, g_=cmp_turn):
                        if kind == 0 and h == 0:
                            f_()
                        if kind == 0 and h == (1 if qt < 2 else 6):
                            g_()

                    def done(tok, qt=qt, kind=kind, h=h):
                        if h != 7 or kind == 0:
                            return
                        w_ = split_out(oa, obk[qt][1], qt, tok)
                        OB.give(obk[qt][0], *w_)
                        oa_t.extend(w_)

                    def gate(n, qt=qt, kind=kind, h=h):
                        c = 3 * h + kind + 1
                        return sgs[:, qt, c:c + 6 * (n - 1) + 1:6], sgt

                    us.append(causal_units(
                        lambda h=h, qt=qt, p0=p0: qq[p0:p0 + 64, h // 2, qt * 128:(qt + 1) * 128],
                        lambda h=h, qt=qt, p0=p0, kk=kk: kk[p0:p0 + 64, h // 4, 0:(qt + 1) * 128],
                        lambda h=h, kkt=kkt: [qt_[h // 2], kkt[h // 4]],
                        lambda h=h, qt=qt, kind=kind: [va[:, j, kind * 128 + (h // 4) * 64:kind * 128 + (h // 4) * 64 + 64]
                                                       for j in range(qt + 1)],
                        lambda: v_t, None, None, h, qt, 0.125, col, open=opn, pre=pre, done=done, row=p0,
                        add=True, gate=gate, sms=columns(S_SM, col, 2), rss=columns(S_RS, col, 2),
                        o=lambda qt=qt, h=h: head_out(obk[qt][1], h), ot=lambda qt=qt: obk[qt][2]))
        attend(batches(us))

        fr = now()
        mg = at([128, 2, KC, T], RA + 48 * K, F32R)
        r4 = list(range(4))
        xs = merge(mg, fr, [
            ("gate" + s_, 0, [("br2a" + s_, 0, r4)], lambda c: (oa[:, 0, c, :], oa[:, 1, c, :], oa_t)),
            ("gate" + s_, 8, [("br2b" + s_, 0, r4)], lambda c: (ob[:, 0, c, :], ob[:, 1, c, :], ob_t)),
            ("gate" + s_, 16, [("br2c" + s_, 0, r4)], lambda c: (oc[:, 0, c, :], oc[:, 1, c, :], oc_t))], H)

        def residual(gi):
            new = []
            ht.clear()

            def post(m, bank, tok):
                d = dve.do(lambda e: e.tensor_tensor(xT[:, m, :], xT[:, m, :], bank[:], ALU.add), tok, xt[m])
                w_ = gained(gi, m, d)
                acc_tok[0], r = square_in(xT[:, m, :], m == 0, d)
                ht.append(w_)
                new.append([d, r, w_])
                return [d]
            return post, new
        post, new = residual(7 + 3 * L)
        down("wo2" + s_, KC, xs, post)
        xt = new
        factor()
        xs = ffn("f3" + s_, ht)
        post, new = residual(8 + 3 * L)
        down("f3" + s_ + "_d", FC, xs, post)
        xt = new
        factor()
        H = hs(ht)
        fr = now()
        pf = at([128, 2, T], RA + 12 * K)
        ps = at([128, 2, 2, T], RA, F32R)
        a = load(pf[:], D["ple"][L], fr)
        p_t = [split(ps[:, 0, c, :], ps[:, 1, c, :], pf[:, c, :], a, fr) for c in range(2)]
        new = []
        for m in range(KC):
            bg, gb, tg = dense([("plg" + s_, m, 0, list(range(8)))], H)
            bo, bb_, to = dense([("plp" + s_, m, 0, [0, 1])], lambda c: (ps[:, 0, c, :], ps[:, 1, c, :], p_t[c]))
            i, s, f = tmp.take()
            d = sigmul(s[:], gb, bb_[:], tg, to, f, gate_free=lambda a, bg=bg: PB.give(bg, a))
            PB.give(bo, d)
            d = dve.do(lambda e: e.scalar_tensor_tensor(xT[:, m, :], s[:], 0.5, xT[:, m, :], ALU.mult, ALU.add),
                       d, xt[m])
            tmp.give(i, d)
            acc_tok[0], r = square_in(xT[:, m, :], m == 0, d)
            new.append([d, r])
        xt = new
        if L == 0:
            ht = [gained(9, c, xt[c], tg) for c in range(KC)]
            xt = [[a, b] for a, b in zip(xt, ht)]
            factor()

    first, second, got = rms(DM, acc_tok[0], rstd[:], dve_last())
    first()
    second()
    rt = got[0]
    outs = []
    for c in range(KC):
        i, h, f = tmp.take()
        a = dve.do(lambda e, c=c, h=h: e.scalar_tensor_tensor(h[:], xT[:, c, :], gn[:, 12, c:c + 1], rstd[:],
                                                              ALU.mult, ALU.mult), f, rt, xt[c])
        w = dma(sp, out[c], h[:], a, sem=f"o{c}")
        tmp.give(i, w)
        outs.append(w)
    sp.need(outs)
    sp.need(rope_done)
    sp.need([("m" + str(i), dsum[f"m{i}"]) for i in range(12)])
    return units, (pe, act, dve, pool, sp), sorted(dsum)


def build(nc, D, out):
    D = dict(D)
    D["rope"] = nc.dram_tensor("rope_scratch", [4, 128, T], F32).ap()
    D["rpbs"] = nc.dram_tensor("rpb_scratch", [120 * 8128], F32)
    seq = program(nc, None, D, out)[0]
    with ExitStack() as ctx:
        _, queues, names = program(nc, seq, D, out)
        pe, act, dve, pool, sp = queues
        sems = {n: ctx.enter_context(nc.semaphore("s_" + n)) for n in ["pe", "act", "dve", "pool"] + names}
        block = ctx.enter_context(nc.Block())

        @block.sync
        def _(eng):
            sp.play(eng, sems)

        @block.gpsimd
        def _(eng):
            pool.play(eng, sems)

        @block.scalar
        def _(eng):
            act.play(eng, sems)

        @block.vector
        def _(eng):
            dve.play(eng, sems)

        @block.tensor
        def _(eng):
            pe.play(eng, sems)


def _fm(w, cols=None):
    w = w if cols is None else w[:, cols]
    k, m = w.shape
    return np.ascontiguousarray(w.reshape(k // 128, 128, m // 128, 128).transpose(2, 1, 0, 3)).reshape(m // 128, 128, k)


def _tf(w):
    k, n = w.shape
    return np.ascontiguousarray(w.reshape(k // 128, 128, n).transpose(1, 0, 2)).reshape(1, 128, -1)


def _dup(w):
    return _fm(np.concatenate([w[:, 0:64], w[:, 0:64], w[:, 64:128], w[:, 64:128]], axis=1))


def _rows(x):
    t, n = x.shape
    return np.ascontiguousarray(x.T.reshape(n // 128, 128, t).transpose(1, 0, 2))


def _constants():
    c = np.zeros((128, NCONST), np.float32)

    def put(name, a):
        o_, w = CONST[name]
        c[0:a.shape[0], o_:o_ + a.shape[1]] = a
    p = np.arange(128)
    put("ident", np.eye(128, dtype=np.float32))
    swap = np.where(p % 64 < 32, p + 32, p - 32)
    put("perm", (p[:, None] == swap[None, :]).astype(np.float32))
    q = np.arange(96)
    sw = np.where(q < 80, q + 16, q - 16)
    put("permc", ((q[:, None] == sw[None, :]) & (q[None, :] >= 64)).astype(np.float32))
    col = np.arange(64)
    c0 = np.clip(p % 64 - 8, 0, 48)
    ok = (col[None, :] >= c0[:, None]) & (col[None, :] < c0[:, None] + 16)
    put("colmask", np.where(ok, 0.0, NEG).astype(np.float32))
    n = np.arange(32)
    end = np.where(n < 31, n * 16 + 31, 10 ** 6)
    tq = np.arange(4)[None, :, None] * 128 + p[:, None, None]
    okc = (end[None, None, :] <= tq).reshape(128, 128)
    put("cmpneg", np.where(okc, 0.0, NEG).astype(np.float32))
    put("cmp01", okc.astype(np.float32))
    sel = np.zeros((4, 2, 128), np.float32)
    for ch in range(2):
        for i in range(128):
            sel[2 * ch + i // 64, ch, i] = 1.0
    put("sel", sel.reshape(4, 256))
    f = np.float32
    i64 = np.power(f(10000.0), -np.arange(0, 64, 2, dtype=f) / f(64)).astype(f)
    i32 = np.power(f(10000.0), -np.arange(0, 32, 2, dtype=f) / f(32)).astype(f)
    put("invf", np.stack([i64[p % 32], np.where((p >= 64) & (p < 96), i32[p % 16], f(0))], 1).astype(f))
    put("sgn", np.stack([np.where(p % 64 < 32, -1.0, 1.0), np.where(p % 32 < 16, -1.0, 1.0)], 1).astype(f))
    ca = np.zeros((128, 512), f)
    ca[:, 384:] = np.where(p[None, :] <= p[:, None], 0.0, NEG)
    put("causal", ca)
    kj = np.arange(256) - 128
    okb = (kj[None, :] <= p[:, None]) & (kj[None, :] > p[:, None] - 128)
    put("band", np.where(okb, 0.0, NEG).astype(f))
    slopes = np.exp2(f(-8.0) * (np.arange(12, dtype=f) + f(1)) / f(12)).astype(f)
    dil = np.zeros((128, 4, 640), f)
    for hh in range(4):
        r = np.abs(np.arange(384)[None, :] - 128 - p[:, None])
        dil[:, hh, 0:384] = np.where(r <= 64, -slopes[hh] * r.astype(f) * f(8), NEG)
        r = np.abs(p[None, :] - p[:, None])
        dil[:, hh, 384:512] = np.where(r <= 64, -slopes[4 + hh] * (4 * r).astype(f) * f(8), NEG)
        dil[:, hh, 512:640] = np.where(r % 4 == 0, -slopes[8 + hh] * (4 * r).astype(f) * f(8), NEG)
    return c, dil


def kernel(**inputs):
    import concourse.bacc as bacc
    from concourse.bass_utils import run_bass_kernel_spmd

    I = {k: np.asarray(v) for k, v in inputs.items()}
    A = {}
    A["xT"] = _rows(I["x"][0])
    A["const"], A["dil"] = _constants()
    gains = [I["ffn1_pre_g"][0], I["ffn1_post_g"][0], I["mix_pre_g"][0], I["mix_post_g"][0], I["ffn2_pre_g"][0],
             I["ffn2_post_g"][0]]
    for l in range(2):
        gains += [I["mix_norm_2"][l], I["ffn_norm_2"][l], I["ple_norm_2"][l]]
    gains.append(I["final_norm_2"])
    A["gains"] = np.ascontiguousarray(np.stack(gains).reshape(len(GAINS), KC, 128).transpose(2, 0, 1))
    cg = np.concatenate([np.concatenate([I["c_q_norm_2"][l], I["c_kv_norm_2"][l]]) for l in range(2)])
    A["cgains"] = np.ascontiguousarray(cg.reshape(8, 128).T)
    A["positions"] = np.ascontiguousarray(I["positions_2"])
    A["rpb"] = np.ascontiguousarray(I["na_rpb"][0].reshape(120, 31))
    A["sinks"] = np.ascontiguousarray(np.broadcast_to(I["b_sinks_2"][:, None, :], (2, 128, 8)))
    for n, p in (("f1", "ffn1"), ("f2", "ffn2")):
        A[n + "_g"], A[n + "_u"], A[n + "_d"] = (_fm(I[f"{p}_w_{k}"][0]) for k in ("gate", "up", "down"))
    w = I["w_in"][0]
    A["qka"] = _fm(w[:, 0:1024])
    A["va"] = _tf(w[:, 1024:1536])
    A["qb"] = _fm(w[:, 1536:2304])
    A["kb"] = _fm(w[:, 2304:3072])
    for g in range(3):
        A[f"vb{g}"] = _tf(w[:, 3072 + 256 * g:3328 + 256 * g])
    A["ga"] = _fm(w[:, 3840:4864])
    A["gb"] = _fm(w[:, 4864:5888])
    A["bra"], A["brb"], A["wo"] = _fm(I["w_branch_a"][0]), _fm(I["w_branch_b"][0]), _fm(I["w_out"][0])
    for l in range(2):
        s = str(l)
        w = I["w_in_2"][l]
        A["clat" + s] = _fm(w[:, 2072:2584])
        kpe = np.concatenate([np.zeros((DM, 64), np.float32), w[:, 2584:2616]], 1)
        A["kpe" + s] = _tf(kpe)
        up = I["c_w_q_up_2"][l].reshape(2, 128, 8, 96)
        kv = I["c_w_kv_up_2"][l].reshape(2, 128, 8, 128)
        hq = up.transpose(2, 1, 0, 3).reshape(8, 128, 192)
        hk = kv[..., 0:64].transpose(2, 1, 0, 3).reshape(8, 128, 128)
        hh = np.concatenate([hq, hk], 2).reshape(4, 2, 128, 320).transpose(0, 2, 1, 3)
        A["cup" + s] = np.ascontiguousarray(hh).reshape(4, 128, 640)
        A["cv" + s] = np.ascontiguousarray(kv[..., 64:128].transpose(1, 0, 2, 3)).reshape(1, 128, 1024)
        A["v2" + s] = _tf(np.concatenate([w[:, 896:1024], w[:, 1152:1280], w[:, 1944:2072], w[:, 1280:1304]], 1))
        A["qb2" + s] = _fm(w[:, 1304:1816])
        A["kb2" + s] = _dup(w[:, 1816:1944])
        A["kc" + s] = np.concatenate([_dup(w[:, 512:640]), _dup(w[:, 640:768])])
        A["qa2" + s] = _fm(w[:, 0:512])
        A["ks" + s] = np.concatenate([_dup(w[:, 768:896]), _dup(w[:, 1024:1152])])
        A["cw1" + s] = np.concatenate([_tf(I["a_cmp_w1_k_2"][l]), _tf(I["a_cmp_w1_v_2"][l])])
        A["gate" + s] = _fm(I["w_branch_gate_2"][l])
        for b in "abc":
            A["br2" + b + s] = _fm(I[f"w_branch_{b}_2"][l])
        A["wo2" + s] = _fm(I["w_out_2"][l])
        for a, b in (("_g", "gate"), ("_u", "up"), ("_d", "down")):
            A["f3" + s + a] = _fm(I[f"w_ffn_{b}_2"][l])
        A["plg" + s] = _fm(I["w_ple_gate_2"][l])
        A["plp" + s] = _fm(I["w_ple_proj_2"][l])
    w2 = []
    for l in range(2):
        k = I["a_cmp_w2_k_2"][l].reshape(2, 128, 64)
        v = I["a_cmp_w2_v_2"][l].reshape(2, 128, 64)
        w2.append(np.concatenate([k, k, v], 2).transpose(1, 0, 2))
    A["w2"] = np.ascontiguousarray(np.stack(w2))
    pos = np.stack([I["a_cmp_pos_k_2"], I["a_cmp_pos_v_2"]], 1).transpose(0, 3, 1, 2)
    A["cpos"] = np.ascontiguousarray(np.concatenate([pos, pos], 1))
    A["ple"] = np.stack([_rows(I["p_2"][l, 0]) for l in range(2)])

    nc = bacc.Bacc("TRN2", target_bir_lowering=False, num_devices=1)
    D = {n: nc.dram_tensor("in_" + n, a.shape, mybir.dt.from_np(a.dtype), kind="ExternalInput").ap()
         for n, a in A.items()}
    out = nc.dram_tensor("out_0", (KC, 128, T), F32, kind="ExternalOutput").ap()
    build(nc, D, out)
    r = run_bass_kernel_spmd(nc, [{"in_" + n: a for n, a in A.items()}], core_ids=[0])
    y = r.results[0]["out_0"]
    return np.ascontiguousarray(y.reshape(DM, T).T).reshape(1, T, DM)
```
